# Optimizing a Trainium2 kernel written in Bass

```python
import math
import jax, jax.numpy as jnp
from jax import lax
import numpy as np

D_MODEL = 1024
BATCH = 1
SEQ = 256
DEPTH = 2

N_A_LAYERS = DEPTH // 2
N_B_LAYERS = DEPTH - N_A_LAYERS
ALPHA = (2.0 * DEPTH) ** 0.25
BETA = (8.0 * DEPTH) ** -0.25
LN_EPS = 1e-5
ROPE_THETA = 10000.0
NEG = -1e30

RET_HEADS = 4
RET_DK = D_MODEL // RET_HEADS
RET_DV = 2 * RET_DK
RET_CHUNK = 128

NSA_HEADS = 16
NSA_GROUPS = 4
NSA_REP = NSA_HEADS // NSA_GROUPS
NSA_DH = D_MODEL // NSA_HEADS
KV_W = NSA_GROUPS * NSA_DH
CMP_LEN = 32
CMP_STRIDE = 16
CMP_HIDDEN = 256
SLC_BLOCK = 64
SLC_TOPK = 16
WINDOW = 512
Q_BLOCK = 128
FORCE_BONUS = 1e3

N_EXPERTS = 16
N_EXPERT_GROUPS = 4
EXPERTS_PER_GROUP = N_EXPERTS // N_EXPERT_GROUPS
TOP_K = 2
D_EXPERT = 512


def layer_norm(x, g, b):
    xf = x.astype(jnp.float32)
    mu = xf.mean(-1, keepdims=True)
    var = jnp.square(xf - mu).mean(-1, keepdims=True)
    y = (xf - mu) * lax.rsqrt(var + LN_EPS) * g.astype(jnp.float32) + b.astype(jnp.float32)
    return y.astype(x.dtype)

def rope(x, pos):
    d = x.shape[-1]
    inv = ROPE_THETA ** (-jnp.arange(0, d, 2, dtype=jnp.float32) / d)
    ang = pos.astype(jnp.float32)[:, None] * inv[None, :]
    cos = jnp.cos(ang)[None, :, None, :]
    sin = jnp.sin(ang)[None, :, None, :]
    xf = x.astype(jnp.float32)
    x1, x2 = xf[..., : d // 2], xf[..., d // 2:]
    return jnp.concatenate([x1 * cos - x2 * sin, x2 * cos + x1 * sin], -1).astype(x.dtype)

def masked_softmax(s, mask):
    p = jax.nn.softmax(jnp.where(mask, s, NEG), axis=-1)
    return jnp.where(mask, p, 0.0)

def retention(h, w_in, w_out):
    B, S, _ = h.shape
    dt = h.dtype
    H, dk, dv, C = RET_HEADS, RET_DK, RET_DV, RET_CHUNK
    proj = h @ w_in
    q, k, v, g = jnp.split(proj, [H * dk, 2 * H * dk, 2 * H * dk + H * dv], axis=-1)
    pos = jnp.arange(S)
    q = rope(q.reshape(B, S, H, dk), pos)
    k = rope(k.reshape(B, S, H, dk), pos) * (dk ** -0.5)
    v = v.reshape(B, S, H, dv)
    nC = S // C

    def chunks(t):
        return t.reshape(B, nC, C, H, -1).transpose(0, 3, 1, 2, 4)

    qc, kc, vc = chunks(q), chunks(k), chunks(v)
    log_gamma = jnp.log1p(-(2.0 ** (-5.0 - jnp.arange(H, dtype=jnp.float32))))
    idx = jnp.arange(C, dtype=jnp.float32)
    diff = idx[:, None] - idx[None, :]
    decay_mask = jnp.where(diff >= 0, jnp.exp(log_gamma[:, None, None] * jnp.maximum(diff, 0.0)), 0.0).astype(dt)
    inner = jnp.einsum('bhncd,bhnmd->bhncm', qc, kc) * decay_mask[None, :, None]
    o_inner = jnp.einsum('bhncm,bhnme->bhnce', inner, vc)
    q_decay = jnp.exp(log_gamma[:, None] * (idx[None, :] + 1.0)).astype(dt)
    k_decay = jnp.exp(log_gamma[:, None] * (C - 1.0 - idx[None, :])).astype(dt)
    chunk_decay = jnp.exp(log_gamma * C).astype(dt)

    def step(state, xs):
        q_i, k_i, v_i = xs
        o = jnp.einsum('bhcd,bhde->bhce', q_i * q_decay[None, :, :, None], state)
        state = state * chunk_decay[None, :, None, None] + jnp.einsum(
            'bhcd,bhce->bhde', k_i * k_decay[None, :, :, None], v_i)
        return state, o

    state0 = jnp.zeros((B, H, dk, dv), dt)
    _, o_cross = lax.scan(step, state0, (qc.transpose(2, 0, 1, 3, 4),
                                         kc.transpose(2, 0, 1, 3, 4),
                                         vc.transpose(2, 0, 1, 3, 4)))
    o = o_inner + o_cross.transpose(1, 2, 0, 3, 4)
    o = o.transpose(0, 2, 3, 1, 4).reshape(B, S, H, dv)
    of = o.astype(jnp.float32)
    mu = of.mean(-1, keepdims=True)
    var = jnp.square(of - mu).mean(-1, keepdims=True)
    o = ((of - mu) * lax.rsqrt(var + LN_EPS)).reshape(B, S, H * dv).astype(dt)
    return (jax.nn.silu(g) * o) @ w_out

def nsa_shared_kv(h, w_kv, cmp_pe_k, cmp_pe_v, cmp_k_w1, cmp_k_w2, cmp_v_w1, cmp_v_w2):
    B, S, _ = h.shape
    G, dh = NSA_GROUPS, NSA_DH
    pos = jnp.arange(S)
    parts = jnp.split(h @ w_kv, 6, axis=-1)
    kc, vc, ks, vs, kw, vw = [p.reshape(B, S, G, dh) for p in parts]
    kc, ks, kw = rope(kc, pos), rope(ks, pos), rope(kw, pos)
    n_cmp = (S - CMP_LEN) // CMP_STRIDE + 1
    cidx = jnp.arange(n_cmp)[:, None] * CMP_STRIDE + jnp.arange(CMP_LEN)[None, :]

    def compress(t, pe, w1, w2):
        blk = t[:, cidx] + pe[None, None, :, None, :]
        blk = blk.transpose(0, 3, 1, 2, 4).reshape(B, G, n_cmp, CMP_LEN * dh)
        return jax.nn.gelu(blk @ w1) @ w2

    k_cmp = compress(kc, cmp_pe_k, cmp_k_w1, cmp_k_w2)
    v_cmp = compress(vc, cmp_pe_v, cmp_v_w1, cmp_v_w2)
    nS = S // SLC_BLOCK

    def to_blocks(t):
        return t.transpose(0, 2, 1, 3).reshape(B, G, nS, SLC_BLOCK, dh)

    def pad_win(t):
        return jnp.pad(t.transpose(0, 2, 1, 3), ((0, 0), (0, 0), (WINDOW, 0), (0, 0)))

    return (k_cmp, v_cmp, to_blocks(ks), to_blocks(vs), pad_win(kw), pad_win(vw))

def nsa_attention(h, w_in, w_out, shared):
    k_cmp, v_cmp, k_slc, v_slc, k_win, v_win = shared
    B, S, _ = h.shape
    dt = h.dtype
    H, G, R, dh = NSA_HEADS, NSA_GROUPS, NSA_REP, NSA_DH
    proj = h @ w_in
    q = rope(proj[..., : H * dh].reshape(B, S, H, dh), jnp.arange(S)) * (dh ** -0.5)
    gates = jax.nn.sigmoid(proj[..., H * dh:].astype(jnp.float32)).reshape(B, S, H, 3)
    nQ = S // Q_BLOCK
    q_blocks = q.reshape(B, nQ, Q_BLOCK, G, R, dh).transpose(1, 0, 3, 4, 2, 5)
    g_blocks = gates.reshape(B, nQ, Q_BLOCK, G, R, 3).transpose(1, 0, 3, 4, 2, 5)
    n_cmp = k_cmp.shape[2]
    nS = k_slc.shape[2]
    top_k = min(SLC_TOPK, nS)
    ci = jnp.arange(n_cmp)
    sj = jnp.arange(nS)
    cmp_end = ci * CMP_STRIDE + CMP_LEN - 1
    overlap = ((ci[:, None] * CMP_STRIDE < (sj[None, :] + 1) * SLC_BLOCK)
               & (ci[:, None] * CMP_STRIDE + CMP_LEN > sj[None, :] * SLC_BLOCK)).astype(jnp.float32)
    gather_blocks = jax.vmap(jax.vmap(lambda kb, ix: kb[ix]))

    def block(xs):
        i, qb, gb = xs
        t = i * Q_BLOCK + jnp.arange(Q_BLOCK)
        s = jnp.einsum('bgrqd,bgnd->bgrqn', qb, k_cmp).astype(jnp.float32)
        p_cmp = masked_softmax(s, cmp_end[None, :] <= t[:, None])
        o_cmp = jnp.einsum('bgrqn,bgnd->bgrqd', p_cmp.astype(dt), v_cmp)
        imp = jnp.einsum('bgrqn,ns->bgqs', p_cmp, overlap)
        valid = sj[None, :] * SLC_BLOCK <= t[:, None]
        cur = t // SLC_BLOCK
        forced = (sj[None, :] == 0) | (sj[None, :] == cur[:, None]) | (sj[None, :] == cur[:, None] - 1)
        score = jnp.where(valid, imp + jnp.where(forced, FORCE_BONUS, 0.0), NEG)
        _, sel = lax.top_k(score, top_k)
        ks = gather_blocks(k_slc, sel).reshape(B, G, Q_BLOCK, top_k * SLC_BLOCK, dh)
        vs = gather_blocks(v_slc, sel).reshape(B, G, Q_BLOCK, top_k * SLC_BLOCK, dh)
        key_pos = (sel[..., None] * SLC_BLOCK + jnp.arange(SLC_BLOCK)).reshape(B, G, Q_BLOCK, top_k * SLC_BLOCK)
        s = jnp.einsum('bgrqd,bgqkd->bgrqk', qb, ks).astype(jnp.float32)
        p = masked_softmax(s, (key_pos <= t[:, None])[:, :, None])
        o_slc = jnp.einsum('bgrqk,bgqkd->bgrqd', p.astype(dt), vs)
        kw = lax.dynamic_slice_in_dim(k_win, i * Q_BLOCK, Q_BLOCK + WINDOW, axis=2)
        vw = lax.dynamic_slice_in_dim(v_win, i * Q_BLOCK, Q_BLOCK + WINDOW, axis=2)
        wpos = i * Q_BLOCK - WINDOW + jnp.arange(Q_BLOCK + WINDOW)
        dist = t[:, None] - wpos[None, :]
        wmask = (dist >= 0) & (dist < WINDOW) & (wpos[None, :] >= 0)
        s = jnp.einsum('bgrqd,bgkd->bgrqk', qb, kw).astype(jnp.float32)
        p = masked_softmax(s, wmask)
        o_win = jnp.einsum('bgrqk,bgkd->bgrqd', p.astype(dt), vw)
        o = gb[..., 0:1] * o_cmp + gb[..., 1:2] * o_slc + gb[..., 2:3] * o_win
        return o.astype(dt)

    o = lax.map(block, (jnp.arange(nQ), q_blocks, g_blocks))
    o = o.transpose(1, 0, 4, 2, 3, 5).reshape(B, S, H * dh)
    return o @ w_out

def moe(h, router_w, router_b, w_gate, w_up, w_down):
    B, S, D = h.shape
    x = h.reshape(-1, D)
    T = x.shape[0]
    aff = jax.nn.sigmoid((x @ router_w).astype(jnp.float32))
    sel_score = aff + router_b.astype(jnp.float32)
    grp_score = lax.top_k(sel_score.reshape(T, N_EXPERT_GROUPS, EXPERTS_PER_GROUP), TOP_K)[0].sum(-1)
    best = jnp.argmax(grp_score, axis=-1)
    in_group = (jnp.arange(N_EXPERTS) // EXPERTS_PER_GROUP)[None, :] == best[:, None]
    _, top_idx = lax.top_k(jnp.where(in_group, sel_score, NEG), TOP_K)
    chosen = jax.nn.one_hot(top_idx, N_EXPERTS, dtype=jnp.float32).sum(1)
    w = aff * chosen
    w = (w / w.sum(-1, keepdims=True)).astype(x.dtype)
    y = jnp.zeros_like(x)
    for e in range(N_EXPERTS):
        he = (jax.nn.silu(x @ w_gate[e]) * (x @ w_up[e])) @ w_down[e]
        y = y + w[:, e:e + 1] * he
    return y.reshape(B, S, D)

def first_inputs(seed: int = 0) -> dict:
    key = jax.random.key(seed)
    ks = jax.random.split(key, 32)
    f32 = jnp.float32
    D = D_MODEL

    def nrm(k, shape, scale):
        return jax.random.normal(k, shape, f32) * scale

    x = nrm(ks[0], (BATCH, SEQ, D), 1.0)
    ret_w_in = jnp.concatenate([
        nrm(ks[1], (N_A_LAYERS, D, 2 * RET_HEADS * RET_DK), D ** -0.5),
        nrm(ks[2], (N_A_LAYERS, D, RET_HEADS * RET_DV), D ** -0.5 * BETA),
        nrm(ks[3], (N_A_LAYERS, D, RET_HEADS * RET_DV), D ** -0.5)], axis=-1)
    ret_w_out = nrm(ks[4], (N_A_LAYERS, RET_HEADS * RET_DV, D), (RET_HEADS * RET_DV) ** -0.5 * BETA)
    kv_k = nrm(ks[5], (3, D, KV_W), D ** -0.5)
    kv_v = nrm(ks[6], (3, D, KV_W), D ** -0.5 * BETA)
    nsa_w_kv = jnp.stack([kv_k, kv_v], 1).transpose(2, 0, 1, 3).reshape(D, 6 * KV_W)
    cmp_pe_k = nrm(ks[7], (CMP_LEN, NSA_DH), 0.1)
    cmp_pe_v = nrm(ks[8], (CMP_LEN, NSA_DH), 0.1)
    cmp_k_w1 = nrm(ks[9], (CMP_LEN * NSA_DH, CMP_HIDDEN), (CMP_LEN * NSA_DH) ** -0.5)
    cmp_k_w2 = nrm(ks[10], (CMP_HIDDEN, NSA_DH), CMP_HIDDEN ** -0.5)
    cmp_v_w1 = nrm(ks[11], (CMP_LEN * NSA_DH, CMP_HIDDEN), (CMP_LEN * NSA_DH) ** -0.5)
    cmp_v_w2 = nrm(ks[12], (CMP_HIDDEN, NSA_DH), CMP_HIDDEN ** -0.5)
    nsa_w_in = nrm(ks[13], (N_B_LAYERS, D, NSA_HEADS * NSA_DH + 3 * NSA_HEADS), D ** -0.5)
    nsa_w_out = nrm(ks[14], (N_B_LAYERS, NSA_HEADS * NSA_DH, D), (NSA_HEADS * NSA_DH) ** -0.5 * BETA)
    router_w = nrm(ks[15], (D, N_EXPERTS), D ** -0.5)
    router_b = nrm(ks[16], (N_EXPERTS,), 0.01)
    moe_w_gate = nrm(ks[17], (DEPTH, N_EXPERTS, D, D_EXPERT), D ** -0.5)
    moe_w_up = nrm(ks[18], (DEPTH, N_EXPERTS, D, D_EXPERT), D ** -0.5 * BETA)
    moe_w_down = nrm(ks[19], (DEPTH, N_EXPERTS, D_EXPERT, D), D_EXPERT ** -0.5 * BETA)
    ln_mix_g = 1.0 + nrm(ks[20], (DEPTH, D), 0.02)
    ln_mix_b = nrm(ks[21], (DEPTH, D), 0.02)
    ln_ffn_g = 1.0 + nrm(ks[22], (DEPTH, D), 0.02)
    ln_ffn_b = nrm(ks[23], (DEPTH, D), 0.02)
    return {'x': x, 'ret_w_in': ret_w_in, 'ret_w_out': ret_w_out, 'nsa_w_kv': nsa_w_kv,
            'cmp_pe_k': cmp_pe_k, 'cmp_pe_v': cmp_pe_v, 'cmp_k_w1': cmp_k_w1, 'cmp_k_w2': cmp_k_w2,
            'cmp_v_w1': cmp_v_w1, 'cmp_v_w2': cmp_v_w2, 'nsa_w_in': nsa_w_in, 'nsa_w_out': nsa_w_out,
            'router_w': router_w, 'router_b': router_b, 'moe_w_gate': moe_w_gate, 'moe_w_up': moe_w_up,
            'moe_w_down': moe_w_down, 'ln_mix_g': ln_mix_g, 'ln_mix_b': ln_mix_b,
            'ln_ffn_g': ln_ffn_g, 'ln_ffn_b': ln_ffn_b}

def first_block(x, ret_w_in, ret_w_out, nsa_w_kv, cmp_pe_k, cmp_pe_v, cmp_k_w1, cmp_k_w2, cmp_v_w1, cmp_v_w2,
              nsa_w_in, nsa_w_out, router_w, router_b, moe_w_gate, moe_w_up, moe_w_down,
              ln_mix_g, ln_mix_b, ln_ffn_g, ln_ffn_b):
    h = x
    shared = None
    for l in range(DEPTH):
        if l < N_A_LAYERS:
            mix = retention(h, ret_w_in[l], ret_w_out[l])
        else:
            if l == N_A_LAYERS:
                shared = nsa_shared_kv(h, nsa_w_kv, cmp_pe_k, cmp_pe_v, cmp_k_w1, cmp_k_w2, cmp_v_w1, cmp_v_w2)
            j = l - N_A_LAYERS
            mix = nsa_attention(h, nsa_w_in[j], nsa_w_out[j], shared)
        h = layer_norm(ALPHA * h + mix, ln_mix_g[l], ln_mix_b[l])
        h = layer_norm(ALPHA * h + moe(h, router_w, router_b, moe_w_gate[l], moe_w_up[l], moe_w_down[l]),
                       ln_ffn_g[l], ln_ffn_b[l])
    return h


DEPTH_2 = 1

SSD_EXPAND = 2
D_INNER = SSD_EXPAND * D_MODEL
SSD_HEAD_DIM = 64
SSD_HEADS = D_INNER // SSD_HEAD_DIM
SSD_GROUPS = 4
SSD_HEADS_PER_GROUP = SSD_HEADS // SSD_GROUPS
D_STATE = 128
D_CONV = 5
SSD_CHUNK = 128
CONV_DIM = D_INNER + 2 * SSD_GROUPS * D_STATE
NORM_EPS = 1e-5

ATTN_HEAD_DIM = 64
DIL_PATTERNS = ((128, 1), (512, 4), (2048, 16))
N_PATTERNS = len(DIL_PATTERNS)
HEADS_PER_PATTERN = 4
ATTN_HEADS = N_PATTERNS * HEADS_PER_PATTERN
ATTN_WIDTH = ATTN_HEADS * ATTN_HEAD_DIM
ATTN_OUT_WIDTH = HEADS_PER_PATTERN * ATTN_HEAD_DIM

D_FF = 4 * D_MODEL
N_BRANCHES = 2
IN_SPLITS = (D_INNER, CONV_DIM, SSD_HEADS, SSD_HEADS, ATTN_WIDTH, ATTN_WIDTH, ATTN_WIDTH, N_BRANCHES * D_MODEL)
IN_COLS = sum(IN_SPLITS)


def layer_norm_2(x, g, b):
    xf = x.astype(jnp.float32)
    mu = jnp.mean(xf, axis=-1, keepdims=True)
    var = jnp.mean(jnp.square(xf - mu), axis=-1, keepdims=True)
    return ((xf - mu) * lax.rsqrt(var + NORM_EPS) * g.astype(jnp.float32) + b.astype(jnp.float32)).astype(x.dtype)

def centred_depthwise_conv(u, w, b):
    pad = D_CONV // 2
    out = lax.conv_general_dilated(u, w[:, None, :].astype(u.dtype), window_strides=(1,), padding=((pad, pad),),
                                   dimension_numbers=('NWC', 'WIO', 'NWC'), feature_group_count=u.shape[-1])
    return out + b.astype(u.dtype)

def segsum_exp(a_cs):
    q = a_cs.shape[-1]
    diff = a_cs[..., :, None] - a_cs[..., None, :]
    mask = jnp.tril(jnp.ones((q, q), dtype=bool))
    return jnp.where(mask, jnp.exp(jnp.where(mask, diff, 0.0)), 0.0)

def ssd_chunked(xh, dt, a_coef, bm, cm):
    bsz, s = xh.shape[:2]
    nc = s // SSD_CHUNK
    g, r, p = SSD_GROUPS, SSD_HEADS_PER_GROUP, SSD_HEAD_DIM
    xc = (xh * dt[..., None]).reshape(bsz, nc, SSD_CHUNK, g, r, p)
    a = (dt * a_coef).reshape(bsz, nc, SSD_CHUNK, g, r).transpose(0, 3, 4, 1, 2)
    bc = bm.reshape(bsz, nc, SSD_CHUNK, g, D_STATE)
    cc = cm.reshape(bsz, nc, SSD_CHUNK, g, D_STATE)
    a_cs = jnp.cumsum(a, axis=-1)
    lmat = segsum_exp(a_cs)
    cb = jnp.einsum('bclgn,bcsgn->bgcls', cc, bc)
    y_diag = jnp.einsum('bgcls,bgrcls,bcsgrp->bclgrp', cb, lmat, xc)
    decay_states = jnp.exp(a_cs[..., -1:] - a_cs)
    states = jnp.einsum('bclgn,bgrcl,bclgrp->bcgrpn', bc, decay_states, xc)
    chunk_decay = jnp.exp(a_cs[..., -1])

    def step(h, inp):
        dec, st = inp
        return dec[..., None, None] * h + st, h

    h0 = jnp.zeros_like(states[:, 0])
    _, prev = lax.scan(step, h0, (jnp.moveaxis(chunk_decay, -1, 0), jnp.moveaxis(states, 1, 0)))
    prev = jnp.moveaxis(prev, 0, 1)
    y_off = jnp.einsum('bclgn,bcgrpn,bgrcl->bclgrp', cc, prev, jnp.exp(a_cs))
    return (y_diag + y_off).reshape(bsz, s, g * r, p)

def ssd_branch(z, xbc, dt_f_raw, dt_b_raw, conv_w, conv_b, dt_bias_f, dt_bias_b, a_log_f, a_log_b, d_skip, ssd_norm_w):
    bsz, s = z.shape[:2]
    xbc = jax.nn.silu(centred_depthwise_conv(xbc, conv_w, conv_b)).astype(jnp.float32)
    xs, bm, cm = jnp.split(xbc, [D_INNER, D_INNER + SSD_GROUPS * D_STATE], axis=-1)
    xh = xs.reshape(bsz, s, SSD_HEADS, SSD_HEAD_DIM)
    bm = bm.reshape(bsz, s, SSD_GROUPS, D_STATE)
    cm = cm.reshape(bsz, s, SSD_GROUPS, D_STATE)
    dt_f = jax.nn.softplus(dt_f_raw.astype(jnp.float32) + dt_bias_f.astype(jnp.float32))
    dt_b = jax.nn.softplus(dt_b_raw.astype(jnp.float32) + dt_bias_b.astype(jnp.float32))
    a_f = -jnp.exp(a_log_f.astype(jnp.float32))
    a_b = -jnp.exp(a_log_b.astype(jnp.float32))
    y_f = ssd_chunked(xh, dt_f, a_f, bm, cm)
    flip = lambda t: jnp.flip(t, axis=1)
    y_b = flip(ssd_chunked(flip(xh), flip(dt_b), a_b, flip(bm), flip(cm)))
    y = y_f + y_b + d_skip.astype(jnp.float32)[:, None] * xh
    y = y.reshape(bsz, s, D_INNER) * jax.nn.silu(z.astype(jnp.float32))
    yg = y.reshape(bsz, s, SSD_GROUPS, D_INNER // SSD_GROUPS)
    yg = yg * lax.rsqrt(jnp.mean(jnp.square(yg), axis=-1, keepdims=True) + NORM_EPS)
    return (yg.reshape(bsz, s, D_INNER) * ssd_norm_w.astype(jnp.float32)).astype(z.dtype)

def dilated_window_attention(q, k, v, slopes, dilation, half):
    bsz, s, h, e = q.shape
    seq_l = s // dilation
    blk = half
    nb = -(-seq_l // blk)
    lp = nb * blk

    def to_strided(a):
        return a.astype(jnp.float32).reshape(bsz, seq_l, dilation, h, e).transpose(0, 2, 3, 1, 4)

    qs = jnp.pad(to_strided(q), ((0, 0), (0, 0), (0, 0), (0, lp - seq_l), (0, 0))).reshape(bsz, dilation, h, nb, blk, e)

    def windows(a):
        a = jnp.pad(to_strided(a), ((0, 0), (0, 0), (0, 0), (blk, blk + lp - seq_l), (0, 0)))
        a = a.reshape(bsz, dilation, h, nb + 2, blk, e)
        return jnp.concatenate([a[:, :, :, :-2], a[:, :, :, 1:-1], a[:, :, :, 2:]], axis=4)

    ks, vs = windows(k), windows(v)
    qpos = jnp.arange(nb)[:, None] * blk + jnp.arange(blk)[None, :]
    kpos = jnp.arange(nb)[:, None] * blk - blk + jnp.arange(3 * blk)[None, :]
    rel = kpos[:, None, :] - qpos[:, :, None]
    valid = (jnp.abs(rel) <= half) & (kpos[:, None, :] >= 0) & (kpos[:, None, :] < seq_l)
    dist = (jnp.abs(rel) * dilation).astype(jnp.float32)
    scores = jnp.einsum('bdhine,bdhime->bdhinm', qs, ks) * (1.0 / math.sqrt(e))
    scores = scores - slopes.astype(jnp.float32)[:, None, None, None] * dist
    scores = jnp.where(valid, scores, -jnp.inf)
    m = jnp.max(scores, axis=-1, keepdims=True)
    p = jnp.exp(scores - m)
    den = jnp.sum(p, axis=-1, keepdims=True)
    o = jnp.einsum('bdhinm,bdhime->bdhine', p, vs) / den
    lse = (m + jnp.log(den))[..., 0]

    def from_strided(a):
        a = a.reshape(bsz, dilation, h, lp, *a.shape[5:])[:, :, :, :seq_l]
        a = jnp.moveaxis(a, 3, 1)
        return a.reshape(bsz, s, h, *a.shape[4:])

    return from_strided(o), from_strided(lse)

def attention_branch(q, k, v):
    bsz, s = q.shape[:2]
    q = q.reshape(bsz, s, ATTN_HEADS, ATTN_HEAD_DIM)
    k = k.reshape(bsz, s, ATTN_HEADS, ATTN_HEAD_DIM)
    v = v.reshape(bsz, s, ATTN_HEADS, ATTN_HEAD_DIM)
    slopes = jnp.asarray(2.0 ** (-8.0 * np.arange(1, ATTN_HEADS + 1) / ATTN_HEADS), dtype=jnp.float32)
    outs, lses = [], []
    for gi, (window, dilation) in enumerate(DIL_PATTERNS):
        hs = slice(gi * HEADS_PER_PATTERN, (gi + 1) * HEADS_PER_PATTERN)
        o, l = dilated_window_attention(q[:, :, hs], k[:, :, hs], v[:, :, hs], slopes[hs], dilation, window // (2 * dilation))
        outs.append(o)
        lses.append(l)
    o = jnp.stack(outs, axis=0)
    lse = jnp.stack(lses, axis=0)
    w = jax.nn.softmax(lse, axis=0)
    y = jnp.sum(w[..., None] * o, axis=0)
    return y.reshape(bsz, s, ATTN_OUT_WIDTH).astype(q.dtype)

def second_inputs(seed: int = 0) -> dict:
    key = jax.random.key(seed)
    ks = jax.random.split(key, 24)
    beta = (8.0 * DEPTH_2) ** -0.25
    nrm = lambda k, shape: jax.random.normal(k, shape, dtype=jnp.float32)

    def dt_bias(k):
        dt = jnp.exp(jax.random.uniform(k, (SSD_HEADS,), minval=math.log(1e-3), maxval=math.log(1e-1)))
        return dt + jnp.log(-jnp.expm1(-dt))

    return {
        "x": nrm(ks[0], (BATCH, SEQ, D_MODEL)),
        "w_in": nrm(ks[1], (D_MODEL, IN_COLS)) * D_MODEL ** -0.5,
        "b_gate": 0.02 * nrm(ks[2], (N_BRANCHES * D_MODEL,)),
        "conv_w": nrm(ks[3], (D_CONV, CONV_DIM)) * D_CONV ** -0.5,
        "conv_b": 0.02 * nrm(ks[4], (CONV_DIM,)),
        "dt_bias_f": dt_bias(ks[5]),
        "dt_bias_b": dt_bias(ks[6]),
        "a_log_f": jnp.log(jax.random.uniform(ks[7], (SSD_HEADS,), minval=1.0, maxval=16.0)),
        "a_log_b": jnp.log(jax.random.uniform(ks[8], (SSD_HEADS,), minval=1.0, maxval=16.0)),
        "d_skip": 1.0 + 0.1 * nrm(ks[9], (SSD_HEADS,)),
        "ssd_norm_w": 1.0 + 0.1 * nrm(ks[10], (D_INNER,)),
        "w_proj_ssd": nrm(ks[11], (D_INNER, D_MODEL)) * D_INNER ** -0.5 * beta,
        "w_proj_attn": nrm(ks[12], (ATTN_OUT_WIDTH, D_MODEL)) * ATTN_OUT_WIDTH ** -0.5 * beta,
        "w_out": nrm(ks[13], (D_MODEL, D_MODEL)) * D_MODEL ** -0.5 * beta,
        "ln1_g": 1.0 + 0.1 * nrm(ks[14], (D_MODEL,)),
        "ln1_b": 0.02 * nrm(ks[15], (D_MODEL,)),
        "w_up": nrm(ks[16], (D_MODEL, D_FF)) * D_MODEL ** -0.5 * beta,
        "w_down": nrm(ks[17], (D_FF, D_MODEL)) * D_FF ** -0.5 * beta,
        "ln2_g": 1.0 + 0.1 * nrm(ks[18], (D_MODEL,)),
        "ln2_b": 0.02 * nrm(ks[19], (D_MODEL,)),
    }

def second_block(x, w_in, b_gate, conv_w, conv_b, dt_bias_f, dt_bias_b, a_log_f, a_log_b, d_skip, ssd_norm_w,
              w_proj_ssd, w_proj_attn, w_out, ln1_g, ln1_b, w_up, w_down, ln2_g, ln2_b):
    alpha = (2.0 * DEPTH_2) ** 0.25
    h = x
    for _ in range(DEPTH_2):
        bsz, s = h.shape[:2]
        u = h @ w_in
        z, xbc, dt_f_raw, dt_b_raw, q, k, v, gate_logits = jnp.split(u, list(np.cumsum(IN_SPLITS)[:-1]), axis=-1)
        y_ssd = ssd_branch(z, xbc, dt_f_raw, dt_b_raw, conv_w, conv_b, dt_bias_f, dt_bias_b,
                           a_log_f, a_log_b, d_skip, ssd_norm_w) @ w_proj_ssd
        y_att = attention_branch(q, k, v) @ w_proj_attn
        gates = jax.nn.sigmoid(gate_logits + b_gate).reshape(bsz, s, N_BRANCHES, D_MODEL)
        mix = (gates[:, :, 0] * y_ssd + gates[:, :, 1] * y_att) @ w_out
        h = layer_norm_2(alpha * h + mix, ln1_g, ln1_b)
        f = jnp.square(jax.nn.relu(h @ w_up)) @ w_down
        h = layer_norm_2(alpha * h + f, ln2_g, ln2_b)
    return h


def setup_inputs(seed=0):
    out = dict(first_inputs(seed))
    for name, value in second_inputs(seed + 1).items():
        if name != "x":
            out[name + "_2"] = value
    return out


def reference(
    x, ret_w_in, ret_w_out, nsa_w_kv, cmp_pe_k, cmp_pe_v, cmp_k_w1, cmp_k_w2, cmp_v_w1,
    cmp_v_w2, nsa_w_in, nsa_w_out, router_w, router_b, moe_w_gate, moe_w_up, moe_w_down,
    ln_mix_g, ln_mix_b, ln_ffn_g, ln_ffn_b, w_in_2, b_gate_2, conv_w_2, conv_b_2, dt_bias_f_2,
    dt_bias_b_2, a_log_f_2, a_log_b_2, d_skip_2, ssd_norm_w_2, w_proj_ssd_2, w_proj_attn_2,
    w_out_2, ln1_g_2, ln1_b_2, w_up_2, w_down_2, ln2_g_2, ln2_b_2,
):
    x = first_block(
        x, ret_w_in, ret_w_out, nsa_w_kv, cmp_pe_k, cmp_pe_v, cmp_k_w1, cmp_k_w2, cmp_v_w1,
        cmp_v_w2, nsa_w_in, nsa_w_out, router_w, router_b, moe_w_gate, moe_w_up, moe_w_down,
        ln_mix_g, ln_mix_b, ln_ffn_g, ln_ffn_b,
    )
    return second_block(
        x, w_in_2, b_gate_2, conv_w_2, conv_b_2, dt_bias_f_2, dt_bias_b_2, a_log_f_2, a_log_b_2,
        d_skip_2, ssd_norm_w_2, w_proj_ssd_2, w_proj_attn_2, w_out_2, ln1_g_2, ln1_b_2, w_up_2,
        w_down_2, ln2_g_2, ln2_b_2,
    )


_drawn_inputs = setup_inputs


def setup_inputs(seed=0):
    import zlib

    import numpy as np

    out = dict(_drawn_inputs(seed))
    spreads = {}
    factors = {'cmp_pe_k': 8.0,
     'cmp_pe_v': 3.715,
     'cmp_k_w1': 5.007,
     'cmp_k_w2': 4.64,
     'b_gate_2': 8.0,
     'conv_b_2': 8.0,
     'd_skip_2': 5.958,
     'ssd_norm_w_2': 3.454,
     'ln1_b_2': 2.851}
    for name, (base, spread) in spreads.items():
        noise = np.random.default_rng([zlib.crc32(name.encode()), seed]).standard_normal(out[name].shape)
        drawn = base * np.exp(spread * noise) if base else spread * noise
        out[name] = __import__('jax').numpy.asarray(drawn.astype(out[name].dtype))
    for name, factor in factors.items():
        out[name] = (out[name] * factor).astype(out[name].dtype)
    return out
```

```python
from contextlib import ExitStack

import numpy as np
import concourse.bass as bass
from concourse import mybir

F32 = mybir.dt.float32
ALU = mybir.AluOpType
ACT = mybir.ActivationFunctionType
AXX = mybir.AxisListType.X

P = 128
T = 256
NT = T // P
D = 1024
KC = D // P
SLAB = 4096
NSLOT = 3
WORK = 31700
ALPHA0 = float((2.0 * 2) ** 0.25)
ALPHA1 = float(2.0 ** 0.25)
EPS = 1e-5
NEG = -1e30

RET_H = 4
RET_DV = 512
N_EXP = 16
EXP_PER_GROUP = 4
NSA_H, NSA_G, DH = 16, 4, 64
CMP_N, CMP_LEN, CMP_STRIDE = 15, 32, 16
SSD_H, SSD_G, SSD_N = 32, 4, 128
D_INNER = 2048
CONV_CH = 24
TAPS = 5
ATT_H, ATT_PAT, ATT_HPP = 12, 3, 4
D_FF = 4096

STAGES = [
    ("ret_in", 12, 12, 12, 12), ("ret_yT", 0, 0, 8, 8), ("ret_out", 4, 2, 0, 0), ("ln0", 0, 0, 4, 4),
    ("router0", 0, 0, 1, 1), ("moe0", 48, 32, 64, 0), ("ln1", 0, 0, 4, 4),
    ("nsa_in", 5, 5, 1, 1), ("nsa_T", 0, 0, 12, 12), ("cmp", 2, 0, 4, 2), ("nsa_att", 0, 16, 48, 48),
    ("nsa_oT", 0, 0, 4, 4), ("nsa_out", 2, 2, 0, 0), ("ln2", 0, 0, 4, 4),
    ("router1", 0, 0, 1, 1), ("moe1", 48, 32, 64, 0), ("ln3", 0, 0, 4, 4),
    ("att_in", 5, 5, 0, 0), ("dt", 0, 0, 1, 1), ("att", 6, 6, 36, 36), ("gates", 4, 4, 0, 0), ("att_T", 0, 0, 1, 1),
    ("cums", 0, 0, 1, 1), ("xT", 0, 0, 8, 8), ("ssd", 4, 8, 44, 44), ("proj_attn", 0, 0, 4, 4),
    ("ssd_yT", 0, 0, 8, 8), ("proj_ssd", 4, 0, 4, 0), ("out2", 2, 2, 0, 0), ("ln4", 0, 0, 4, 4),
    ("up", 8, 8, 0, 0), ("down", 8, 2, 0, 0),
]
SL, PJ, AX, AR = {}, {}, {}, {}
_at = [0, 0, 0, 0]
for _name, *_counts in STAGES:
    for _table, _n in zip((SL, PJ, AX, AR), _at):
        _table[_name] = _n
    _at = [x + n for x, n in zip(_at, _counts)]
N_SLABS = _at[0]
SLABS_OF = {name: n for name, n, *_ in STAGES}

def columns(**widths):
    at, out = 0, {}
    for name, w in widths.items():
        out[name] = (at, w)
        at += w
    return out, at

C_ALL, N_ALL = columns(ident=128, router_w=KC * N_EXP, router_b=N_EXP, tie=16)
C_RET, N_RET = columns(cosq=256, sinq=256, cosk=256, sink=256, decay=RET_H * T)
C_NSA, N_NSA = columns(cosk=64, sink=64, cosq=64, sinq=64, causal=768, cmp_add=32, cmp_one=32,
                       pe_k=16, pe_v=16, w_gates=KC * 48, w2k=256, w2v=128)
C_SSD, N_SSD = columns(le=128, gt=128, ge=128, lt=128, w_dt=KC * 64, dt_bias=64, a_log=64, d_skip=SSD_H,
                       conv_w=CONV_CH * TAPS, conv_b=CONV_CH, b_gate=16, norm_w=D_INNER)
N_ATT = ATT_H * NT * T
N_PATTN = 2 * D


def build(nc, x_tok, x_feat, slabs, c_all, c_ret, c_nsa, c_ssd, c_att, w_pattn, ln_gb, out, n_slabs=N_SLABS, n_ln=6):
    ctx = ExitStack()
    with ctx:
        def sb(name, shape):
            return ctx.enter_context(nc.sbuf_tensor(name, shape, F32))

        def sem(name):
            return ctx.enter_context(nc.semaphore(name))

        ring = sb("ring", [P, NSLOT, SLAB])
        h = sb("h", [P, NT, D])
        hT = sb("hT", [P, KC, T])
        y = sb("y", [P, NT, D])
        gb = sb("gb", [P, 2, D])
        call = sb("call", [P, N_ALL])
        small = sb("small", [P, 512])
        work = sb("work", [P, WORK])

        def const(t, cols, name):
            a, w = cols[name]
            return t[:, a:a + w]

        ident = const(call, C_ALL, "ident")
        router_w = const(call, C_ALL, "router_w").rearrange("p (k e) -> p k e", k=KC)
        router_b = const(call, C_ALL, "router_b")
        tie = const(call, C_ALL, "tie").rearrange("p (i j) -> p i j", i=4)

        class Work:
            def __init__(self, at=0):
                self.at = at

            def __call__(self, n):
                self.at += n
                assert self.at <= WORK, self.at
                return work[:, self.at - n:self.at]

        ps = ctx.enter_context(nc.psum_tensor("ps", [P, 8, 512], F32))

        def bank(b, n=1):
            return ps[:, b:b + n, :].rearrange("p b n -> p (b n)")

        st6 = small[:, 0:24].rearrange("p (i a s) -> p i a s", i=NT, a=2)
        mv = small[:, 48:52].rearrange("p (i s) -> p i s", i=NT)
        rstd = small[:, 64:66]
        aff = small[:, 72:104].rearrange("p (i e) -> p i e", i=NT)
        selsc = small[:, 104:136]
        gw = small[:, 136:168].rearrange("p (i e) -> p i e", i=NT)
        rank = small[:, 168:200]
        grp = small[:, 200:208]
        grank = small[:, 208:216]
        wsum = small[:, 216:218]
        rank4 = rank.rearrange("p (g i) -> p g i", i=4)
        cmpA = small[:, 224:256]
        cmpB = small[:, 256:288]
        cmpA3, cmpB3 = (t.rearrange("p (g i) -> p g i", i=4) for t in (cmpA, cmpB))
        cmpA2, cmpB2 = (t[:, 0:8].rearrange("p (t g) -> p t g", t=NT) for t in (cmpA, cmpB))

        w_ = Work()
        cret = w_(N_RET)
        r_cos = [const(cret, C_RET, n) for n in ("cosq", "cosk")]
        r_sin = [const(cret, C_RET, n) for n in ("sinq", "sink")]
        decay = const(cret, C_RET, "decay").rearrange("p (h c) -> p h c", h=RET_H)
        r_qkT = w_(4096).rearrange("p (h f t) -> p h f t", h=2 * RET_H, f=2)
        r_v = w_(4096).rearrange("p (i n) -> p i n", i=NT)
        r_g = w_(4096).rearrange("p (i n) -> p i n", i=NT)
        r_o = w_(4096).rearrange("p (i n) -> p i n", i=NT)
        r_yT = w_(4096).rearrange("p (c t) -> p c t", c=16)
        r_P = w_(2 * 384).rearrange("p (b n) -> p b n", b=2)
        r_t = w_(4 * 512).rearrange("p (a h t) -> p a h t", a=4, h=2)
        r_st6 = w_(48).rearrange("p (h i s) -> p h i s", h=RET_H, i=NT)
        r_mv = w_(16).rearrange("p (h i s) -> p h i s", h=RET_H, i=NT)
        r_rstd = w_(8).rearrange("p (h i) -> p h i", h=RET_H)
        w_ = Work()
        m_sg = w_(1024)
        m_he = w_(1024)
        m_heT = m_he.rearrange("p (c t) -> p c t", c=4)
        cnsa = w_(N_NSA)
        n_cos, n_sin, n_cosq, n_sinq = (const(cnsa, C_NSA, n).rearrange("p (i d) -> p i d", i=NT)
                                        for n in ("cosk", "sink", "cosq", "sinq"))
        causal = const(cnsa, C_NSA, "causal")
        cmp_add, cmp_one = (const(cnsa, C_NSA, n).rearrange("p (i n) -> p i n", i=NT)[:, :, 0:CMP_N]
                            for n in ("cmp_add", "cmp_one"))
        cmp_pe = [const(cnsa, C_NSA, n) for n in ("pe_k", "pe_v")]
        w_gates = const(cnsa, C_NSA, "w_gates")
        w2k = const(cnsa, C_NSA, "w2k").rearrange("p (f n) -> p f n", f=2)
        w2v = const(cnsa, C_NSA, "w2v").rearrange("p (f n) -> p f n", f=2)
        n_t = w_(4 * 512).rearrange("p (a n) -> p a n", a=4)
        KCMP, VCMP, KSLC, KWIN = range(4)
        n_dup_flat = w_(4 * 1024)
        n_dup = n_dup_flat.rearrange("p (y i g u d) -> p y i g u d", y=4, i=NT, g=NSA_G, u=2)
        n_oT = n_dup_flat[:, 0:2048].rearrange("p (c t) -> p c t", c=KC)
        n_v = w_(1024).rearrange("p (y i n) -> p y i n", y=2, i=NT)
        n_q = w_(2048).rearrange("p (i n) -> p i n", i=NT)
        n_qT = w_(2048).rearrange("p (c t) -> p c t", c=KC)
        n_kT = w_(2048).rearrange("p (y g t) -> p y g t", y=2, g=NSA_G)
        n_cT = w_(2048).rearrange("p (y g t) -> p y g t", y=2, g=NSA_G)
        n_blk = w_(2 * 960).rearrange("p (y c g n) -> p y c g n", y=2, c=16, g=NSA_G)
        n_hid = w_(240).rearrange("p (y f n) -> p y f n", y=2, f=2)
        n_kcmp = w_(60)
        n_vcmp = w_(256)
        n_gw = w_(96).rearrange("p (h k) -> p h k", h=NSA_H)
        n_S = w_(2 * 800).rearrange("p (b n) -> p b n", b=2)
        n_P = w_(2 * 1024).rearrange("p (b n) -> p b n", b=2)
        n_PT = w_(1024).rearrange("p (a t) -> p a t", a=8)
        n_o = w_(2048).rearrange("p (i n) -> p i n", i=NT)
        n_max = w_(12).rearrange("p (b k) -> p b k", b=2)
        n_nmax = w_(12).rearrange("p (b k) -> p b k", b=2)
        n_sum = w_(12).rearrange("p (b k) -> p b k", b=2)
        n_w = w_(12).rearrange("p (b k) -> p b k", b=2)
        n_ow = w_(384).rearrange("p (k d) -> p k d", k=6)
        n_o2 = w_(128).rearrange("p (i d) -> p i d", i=NT)
        w_ = Work()
        cssd = w_(N_SSD)
        tri_le, tri_gt, tri_ge, tri_lt, w_dt, dt_bias, a_log, d_skip, conv_w, conv_b, b_gate, norm_w = (
            const(cssd, C_SSD, n) for n in C_SSD)
        pattn = y[:].rearrange("p i n -> p (i n)").rearrange("p (k n) -> p k n", k=2)
        xbcT = w_(6144).rearrange("p (c t) -> p c t", c=CONV_CH)
        s_yT = xbcT[:, 0:16, :]
        a_y = w_(512).rearrange("p (i n) -> p i n", i=NT)
        a_yT = w_(512).rearrange("p (c t) -> p c t", c=2)
        s_v = w_(128).rearrange("p (i n) -> p i n", i=NT)
        s_dt = w_(128).rearrange("p (i n) -> p i n", i=NT)
        s_a = w_(128).rearrange("p (i n) -> p i n", i=NT)
        s_u = w_(128).rearrange("p (i n) -> p i n", i=NT)
        s_l = w_(128).rearrange("p (i n) -> p i n", i=NT)
        s_m = w_(128).rearrange("p (i n) -> p i n", i=NT)
        s_A = w_(64)
        s_E = w_(128).rearrange("p (k h) -> p k h", k=4)
        shared_columns = w_.at
        catt = w_(N_ATT)
        a_bias = catt.rearrange("p (h n) -> p h n", h=ATT_H)
        a_qkT = w_(3072).rearrange("p (c t) -> p c t", c=12)
        a_v = w_(1536).rearrange("p (i n) -> p i n", i=NT)
        a_S = w_(1024).rearrange("p (b n) -> p b n", b=2)
        a_P = w_(1024).rearrange("p (b n) -> p b n", b=2)
        a_PT = w_(1024).rearrange("p (b n) -> p b n", b=2)
        a_o = w_(1536).rearrange("p (h i d) -> p h i d", h=ATT_H, i=NT)
        a_max, a_nmax, a_den, a_lse, a_w = (w_(24).rearrange("p (h i) -> p h i", h=ATT_H) for _ in range(5))
        a_top = w_(8)
        a_sum = w_(8)
        c_raw = w_(2 * 4 * 260).rearrange("p (b c t) -> p b c t", b=2, c=4)
        c_acc = w_(2 * 2 * 256).rearrange("p (b c t) -> p b c t", b=2, c=2)
        w_ = Work(shared_columns)
        gateT = w_(4096).rearrange("p (c t) -> p c t", c=16)
        s_x = w_(4096).rearrange("p (i n) -> p i n", i=NT)
        s_xdt = w_(2048).rearrange("p (r i n) -> p r i n", r=2, i=NT)
        s_xd = w_(1024).rearrange("p (r n) -> p r n", r=2)
        s_cb = w_(512).rearrange("p (k t) -> p k t", k=4)
        s_cbx = w_(256).rearrange("p (k t) -> p k t", k=2)
        s_A4 = w_(1024).rearrange("p (b k t) -> p b k t", b=2, k=4)
        s_L = w_(1024).rearrange("p (b n) -> p b n", b=2)
        s_M = w_(1024).rearrange("p (b k t) -> p b k t", b=2, k=4)
        s_z = w_(1024).rearrange("p (i n) -> p i n", i=NT)
        s_t = w_(1024).rearrange("p (i n) -> p i n", i=NT)
        s_junk = w_(512)
        s_ss = w_(8).rearrange("p (i g) -> p i g", i=NT)
        s_rstd = w_(8).rearrange("p (i g) -> p i g", i=NT)
        mixT = s_xdt.rearrange("p r i n -> p (r i n)").rearrange("p (c t) -> p c t", c=KC)
        mix_t = s_z.rearrange("p i n -> p (i n)")[:, 0:512]
        w_ = Work()
        fT = w_(8192).rearrange("p (c t) -> p c t", c=32)
        f_relu = w_(2048).rearrange("p (b n) -> p b n", b=2)

        slab_loaded = [sem(f"slab_loaded{i}") for i in range(NSLOT)]
        slab_done = sem("slab_done")
        pair_out = [sem("pair_out0"), sem("pair_out1")]
        aux_ready = sem("aux_ready")
        aux_out = [sem(f"aux_out{i}") for i in range(4)]
        x_loaded = sem("x_loaded")
        call_loaded = sem("call_loaded")
        stage_loaded = sem("stage_loaded")
        gb_loaded = sem("gb_loaded")
        stored = sem("stored")
        rope_ready = sem("rope_ready")
        ret_p_ready = sem("ret_p_ready")
        ret_var_ready = sem("ret_var_ready")
        ret_std_ready = sem("ret_std_ready")
        ret_y_ready = sem("ret_y_ready")
        nsa_rot = sem("nsa_rot")
        blk_ready = sem("blk_ready")
        score_ready = sem("score_ready")
        nmax_ready = sem("nmax_ready")
        att_loaded, pattn_loaded = sem("att_loaded"), sem("pattn_loaded")
        dt_v_ready, dt_u_ready, dt_w_ready, dt_l_ready, a_ready = (
            sem(n) for n in ("dt_v_ready", "dt_u_ready", "dt_w_ready", "dt_l_ready", "a_ready"))
        att_max_ready, att_exp_ready, att_o_ready = (sem(n) for n in ("att_max_ready", "att_exp_ready", "att_o_ready"))
        att_lse_ready, att_mix_ready, att_y_ready = (sem(n) for n in ("att_lse_ready", "att_mix_ready", "att_y_ready"))
        raw_zeroed, conv_ready, xbc_ready = sem("raw_zeroed"), sem("conv_ready"), sem("xbc_ready")
        a4_ready, xdt_ready, m_ready = sem("a4_ready"), sem("xdt_ready"), sem("m_ready")
        decay_ready, diag_done, group_done = sem("decay_ready"), sem("diag_done"), sem("group_done")
        cb_ready, ssd_y_ready, square_ready = sem("cb_ready"), sem("ssd_y_ready"), sem("square_ready")
        ssd_var_ready, ssd_std_ready, ssd_n_ready = sem("ssd_var_ready"), sem("ssd_std_ready"), sem("ssd_n_ready")
        mix_ready, f_ready = sem("mix_ready"), sem("f_ready")
        exp_ready = sem("exp_ready")
        prob_ready = sem("prob_ready")
        o_ready = sem("o_ready")
        p_zeroed = sem("p_zeroed")
        var_ready = sem("var_ready")
        std_ready = sem("std_ready")
        h_ready = sem("h_ready")
        y_zeroed = sem("y_zeroed")
        dve_stats = sem("dve_stats")
        dve_chain = sem("dve_chain")
        act_chain = sem("act_chain")
        pool_chain = sem("pool_chain")

        block = ctx.enter_context(nc.Block())

        def chain(eng, signal):
            count = [0]

            def link(ins):
                count[0] += 1
                ins.then_inc(signal, 1)
                eng.wait_ge(signal, count[0])
            return link

        def wait_pair_out(eng, j):
            eng.wait_ge(pair_out[j % 2], j // 2 + 1)

        def wait_aux_out(eng, b):
            eng.wait_ge(aux_out[b % 4], b // 4 + 1)

        def pair(j):
            return bank(2 * (j % 2), 2)

        def aux(b):
            return bank(4 + b % 4)

        @block.sync
        def _(sp):
            for n in range(NSLOT):
                sp.dma_start(ring[:, n, :], slabs[n]).then_inc(slab_loaded[n], 16)
            with sp.Fori(1, n_slabs // NSLOT) as r:
                for slot in range(NSLOT):
                    sp.wait_ge(slab_done, r * NSLOT + (slot - NSLOT + 1))
                    sp.dma_start(ring[:, slot, :], slabs[r * NSLOT + slot]).then_inc(slab_loaded[slot], 16)
            for n in range(n_slabs // NSLOT * NSLOT, n_slabs):
                sp.wait_ge(slab_done, n - NSLOT + 1)
                sp.dma_start(ring[:, n % NSLOT, :], slabs[n]).then_inc(slab_loaded[n % NSLOT], 16)
            for i in range(NT):
                sp.wait_ge(h_ready, 2 * n_ln - 1 + i)
                sp.dma_start(out[i], h[:, i, :]).then_inc(stored, 16)
            sp.wait_ge(stored, 16 * NT)

        @block.gpsimd
        def _(pool):
            pool.dma_start(hT[:], x_feat).then_inc(x_loaded, 16)
            pool.dma_start(h[:], x_tok).then_inc(x_loaded, 16)
            pool.dma_start(cret, c_ret).then_inc(stage_loaded, 16)
            pool.dma_start(call[:], c_all).then_inc(call_loaded, 16)

            def load_gb(n):
                if n:
                    pool.wait_ge(h_ready, 2 * n)
                pool.dma_start(gb[:].rearrange("p a n -> p (a n)"),
                               ln_gb[n:n + 1, :].broadcast_to([P, 2 * D])).then_inc(gb_loaded, 16)

            load_gb(0)
            load_gb(1)
            nc.gpsimd.memset(y[:], 0.0).then_inc(y_zeroed, 1)
            pool.dma_start(cnsa, c_nsa).then_inc(stage_loaded, 16)
            nc.gpsimd.memset(n_P, 0.0).then_inc(p_zeroed, 1)
            load_gb(2)
            load_gb(3)
            nc.gpsimd.memset(y[:], 0.0).then_inc(y_zeroed, 1)
            pool.wait_ge(h_ready, 8)
            pool.dma_start(cssd, c_ssd).then_inc(stage_loaded, 16)
            pool.dma_start(catt, c_att).then_inc(att_loaded, 16)
            pool.dma_start(y[:].rearrange("p i n -> p (i n)"), w_pattn).then_inc(pattn_loaded, 16)
            nc.gpsimd.memset(c_raw, 0.0).then_inc(raw_zeroed, 1)
            load_gb(4)

            pool.wait_ge(a_ready, 1)
            pool.wait_ge(xbc_ready, 12)

            def decays(hh):
                if hh >= 2:
                    pool.wait_ge(aux_ready, AR["ssd"] + 11 * ((hh - 2) // 8) + 2 + (hh - 2) % 8)
                for r, tri in enumerate((tri_gt, tri_lt)):
                    last = nc.gpsimd.tensor_tensor(s_A4[:, hh % 2, 2 * r:2 * r + 2, :],
                                                   tri.unsqueeze(1).broadcast_to([P, NT, P]),
                                                   s_a[:, :, 32 * r + hh:32 * r + hh + 1].broadcast_to([P, NT, P]),
                                                   ALU.mult)
                last.then_inc(a4_ready, 1)

            wait_x = [False]
            for hh in range(SSD_H):
                g, k = hh // 8, hh % 8
                if hh == 0:
                    wait_aux_out(pool, AX["xT"] + 7)
                    wait_aux_out(pool, AX["xT"] + 6)
                    wait_aux_out(pool, AX["xT"] + 5)
                    wait_aux_out(pool, AX["xT"] + 4)
                    pool.wait_ge(decay_ready, 1)
                decays(hh)
                if k == 0:
                    if g:
                        pool.wait_ge(group_done, g)
                    xg = s_x[:, :, g * 512:(g + 1) * 512].rearrange("p i (h d) -> p i h d", h=8)
                    for r in range(2):
                        d = s_dt[:, :, 32 * r + 8 * g:32 * r + 8 * g + 8].unsqueeze(3).broadcast_to([P, NT, 8, DH])
                        last = nc.gpsimd.tensor_tensor(s_xdt[:, r].rearrange("p i (h d) -> p i h d", h=8), xg, d, ALU.mult)
                    last.then_inc(pool_chain, 1)
                    pool.wait_ge(pool_chain, g + 1)
                    for r in range(2):
                        last = nc.gpsimd.tensor_tensor(
                            s_xd[:, r].rearrange("p (h d) -> p h d", h=8),
                            s_xdt[:, r, r].rearrange("p (h d) -> p h d", h=8),
                            s_E[:, 2 + r, 8 * g:8 * g + 8].unsqueeze(2).broadcast_to([P, 8, DH]), ALU.mult)
                    last.then_inc(xdt_ready, 1)
            load_gb(5)

        @block.tensor
        def _(pe):
            def slab(n):
                pe.wait_ge(slab_loaded[n % NSLOT], 16 * (n // NSLOT + 1))
                return ring[:, n % NSLOT, :]

            def take_pair(j):
                if j >= 2:
                    wait_pair_out(pe, j - 2)
                return pair(j)

            def take_aux(b):
                if b >= 4:
                    wait_aux_out(pe, b - 4)
                return aux(b)

            def mode_a(dst, w, src, cols=512):
                w3 = w[:, 0:KC * cols].rearrange("p (k n) -> p k n", k=KC)
                for i in range(NT):
                    for k in range(KC):
                        last = nc.tensor.matmul(dst[:, i, 0:cols], src[:, k, i * P:(i + 1) * P], w3[:, k, :],
                                                start=(k == 0), stop=(k == KC - 1))
                return last

            def mode_b(dst, w, src):
                w3 = w.rearrange("p (k n) -> p k n", k=KC)
                for c in range(4):
                    for k in range(KC):
                        last = nc.tensor.matmul(dst[:, c, :], w3[:, k, c * P:(c + 1) * P], src[:, k, :],
                                                start=(k == 0), stop=(k == KC - 1))
                return last

            def slab_a(n, j, src, cols=512):
                dst = take_pair(j).rearrange("p (i n) -> p i n", i=NT)
                mode_a(dst, slab(n), src, cols).then_inc(slab_done, 1)

            def slab_b(n, j, src):
                dst = take_pair(j).rearrange("p (c t) -> p c t", c=4)
                mode_b(dst, slab(n), src).then_inc(slab_done, 1)

            def transpose4(b, src):
                dst = take_aux(b)
                for q in range(4):
                    last = nc.tensor.transpose(dst[:, q * P:(q + 1) * P], src(q), ident)
                last.then_inc(aux_ready, 1)

            def tokens_to_features(stage, src, groups, ready, first):
                for i in range(NT):
                    pe.wait_ge(ready, first + i)
                    for c in range(groups):
                        transpose4(AX[stage] + groups * i + c,
                                   lambda q: src[:, i, (4 * c + q) * P:(4 * c + q + 1) * P])

            def wait_transposed(stage, batches):
                for b in range(max(0, batches - 4), batches):
                    wait_aux_out(pe, AX[stage] + b)

            pe.wait_ge(x_loaded, 32)
            for j in range(4):
                slab_b(j, j, hT)
            for j in range(4, 8):
                slab_a(j, j, hT)
            pe.wait_ge(rope_ready, 4)
            for hd in range(RET_H):
                b = AX["ret_in"] + 3 * hd
                s = take_aux(b)
                for m in range(NT):
                    cols = slice(0, T) if m == 0 else slice(T, T + P)
                    for f in range(2):
                        last = nc.tensor.matmul(s[:, cols], r_qkT[:, RET_H + hd, f, m * P:(m + 1) * P],
                                                r_qkT[:, hd, f, m * P:T], start=(f == 0), stop=(f == 1))
                last.then_inc(aux_ready, 1)
                slab_a(8 + hd, 8 + hd, hT)
                pe.wait_ge(ret_p_ready, hd + 1)
                wait_pair_out(pe, 4 + hd)
                cols = slice(hd * RET_DV, (hd + 1) * RET_DV)
                o = take_aux(b + 1)
                nc.tensor.matmul(o, r_P[:, hd % 2, 0:P], r_v[:, 0, cols],
                                 start=True, stop=True).then_inc(aux_ready, 1)
                o = take_aux(b + 2)
                nc.tensor.matmul(o, r_P[:, hd % 2, P:T], r_v[:, 0, cols], start=True, stop=False)
                nc.tensor.matmul(o, r_P[:, hd % 2, T:T + P], r_v[:, 1, cols],
                                 start=False, stop=True).then_inc(aux_ready, 1)
            pe.wait_ge(call_loaded, 16)
            for hd in range(RET_H):
                for i in range(NT):
                    pe.wait_ge(ret_y_ready, 2 * hd + i + 1)
                    transpose4(AX["ret_yT"] + 2 * hd + i,
                               lambda q: r_o[:, i, (4 * hd + q) * P:(4 * hd + q + 1) * P])
            wait_transposed("ret_yT", 8)

            def accumulate(stage, n, src):
                dst = [take_pair(PJ[stage] + i) for i in range(NT)]
                for s in range(n):
                    w = slab(SL[stage] + s).rearrange("p (k n) -> p k n", k=4)
                    for i in range(NT):
                        for c in range(2):
                            for k in range(4):
                                last = nc.tensor.matmul(dst[i][:, c * 512:(c + 1) * 512],
                                                        src[:, 4 * s + k, i * P:(i + 1) * P],
                                                        w[:, k, c * 512:(c + 1) * 512],
                                                        start=(s == 0 and k == 0), stop=(s == n - 1 and k == 3))
                    last.then_inc(slab_done, 1)

            accumulate("ret_out", 4, r_yT)

            def norm_to_features(n):
                tokens_to_features(f"ln{n}", h, 2, h_ready, 2 * n + 1)
                wait_transposed(f"ln{n}", 4)

            norm_to_features(0)

            def experts(layer):
                n0, j0, b0 = SL[f"moe{layer}"], PJ[f"moe{layer}"], AX[f"moe{layer}"]
                logits = take_aux(AX[f"router{layer}"])
                for i in range(NT):
                    for k in range(KC):
                        last = nc.tensor.matmul(logits[:, i * N_EXP:(i + 1) * N_EXP], hT[:, k, i * P:(i + 1) * P],
                                                router_w[:, k, :], start=(k == 0), stop=(k == KC - 1))
                last.then_inc(aux_ready, 1)
                slab_b(n0, j0, hT)

                def slot(n, e):
                    at = n0 + n
                    pe.wait_ge(slab_loaded[at % NSLOT], e * 16 + 16 * (at // NSLOT + 1))
                    return ring[:, at % NSLOT, :]

                def hidden(n, e, j):
                    pe.wait_ge(pair_out[j % 2], e + j // 2)
                    mode_b(pair(j).rearrange("p (c t) -> p c t", c=4), slot(n, e), hT).then_inc(slab_done, 1)

                def down(n, e):
                    w = slot(n, e).rearrange("p (k n) -> p k n", k=4)
                    pe.wait_ge(pair_out[(j0 + 1) % 2], e + ((j0 + 1) // 2 + 1))
                    for q in range(4):
                        i, c = q // 2, q % 2
                        b = b0 + q
                        pe.wait_ge(aux_out[b % 4], e + b // 4)
                        for k in range(4):
                            last = nc.tensor.matmul(aux(b), m_heT[:, k, i * P:(i + 1) * P],
                                                    w[:, k, c * 512:(c + 1) * 512], start=(k == 0), stop=(k == 3))
                    last.then_inc(slab_done, 1)

                with pe.Fori(0, N_EXP - 1) as e:
                    hidden(1, e, j0 + 1)
                    hidden(2, e, j0 + 2)
                    down(3, e)
                hidden(1, N_EXP - 1, j0 + 1)
                down(2, N_EXP - 1)

            experts(0)
            norm_to_features(1)

            for s in range(5):
                slab_a(SL["nsa_in"] + s, PJ["nsa_in"] + s, hT)
            pe.wait_ge(stage_loaded, 32)
            mode_a(take_aux(AX["nsa_in"])[:, 0:96].rearrange("p (i n) -> p i n", i=NT),
                   w_gates, hT, 48).then_inc(aux_ready, 1)
            for ty in (KCMP, VCMP, KSLC, KWIN):
                pe.wait_ge(nsa_rot, (1, 1, 2, 3)[ty])
                for i in range(NT):
                    transpose4(AX["nsa_T"] + 2 * ty + i,
                               lambda g: n_dup[:, ty, i, g, :, :].rearrange("p u d -> p (u d)"))
            pe.wait_ge(nsa_rot, 5)
            for i in range(NT):
                for c in range(2):
                    transpose4(AX["nsa_T"] + 8 + 2 * i + c,
                               lambda q: n_q[:, i, (4 * c + q) * P:(4 * c + q + 1) * P])
            for kv in range(2):
                dst = take_aux(AX["cmp"] + kv)
                w = slab(SL["cmp"] + kv).rearrange("p (c n) -> p c n", c=16)
                pe.wait_ge(blk_ready, kv + 1)
                for f in range(2):
                    for c in range(16):
                        last = nc.tensor.matmul(dst[:, f * 60:(f + 1) * 60], w[:, c, f * P:(f + 1) * P],
                                                n_blk[:, kv, c, :, :].rearrange("p g n -> p (g n)"),
                                                start=(c == 0), stop=(c == 15))
                last.then_inc(slab_done, 1)
            dst = take_aux(AX["cmp"] + 2)
            wait_aux_out(pe, AX["cmp"])
            for f in range(2):
                last = nc.tensor.matmul(dst[:, 0:60], w2k[:, f, :], n_hid[:, 0, f, :], start=(f == 0), stop=(f == 1))
            last.then_inc(aux_ready, 1)
            dst = take_aux(AX["cmp"] + 3)
            wait_aux_out(pe, AX["cmp"] + 1)
            for g in range(NSA_G):
                for f in range(2):
                    last = nc.tensor.matmul(dst[0:CMP_N, g * DH:(g + 1) * DH],
                                            n_hid[:, 1, f, g * CMP_N:(g + 1) * CMP_N], w2v[:, f, :],
                                            start=(f == 0), stop=(f == 1))
            last.then_inc(aux_ready, 1)
            wait_aux_out(pe, AX["cmp"] + 2)
            wait_aux_out(pe, AX["cmp"] + 3)
            wait_transposed("nsa_T", 12)

            def nsa_scores(hd):
                s = take_pair(PJ["nsa_att"] + hd)
                g, half = hd // (NSA_H // NSA_G), slice(hd % 2 * DH, hd % 2 * DH + DH)
                q = [n_qT[half, hd // 2, i * P:(i + 1) * P] for i in range(NT)]
                for y_ in range(2):
                    nc.tensor.matmul(s[:, y_ * T:(y_ + 1) * T], q[1], n_kT[half, y_, g, :], start=True, stop=True)
                    nc.tensor.matmul(s[:, 512 + y_ * P:512 + (y_ + 1) * P], q[0], n_kT[half, y_, g, 0:P],
                                     start=True, stop=True)
                for i in (1, 0):
                    last = nc.tensor.matmul(s[:, 768 + (1 - i) * 16:768 + (1 - i) * 16 + CMP_N], q[i],
                                            n_kcmp[half, g * CMP_N:(g + 1) * CMP_N], start=True, stop=True)
                last.then_inc(score_ready, 1)

            nsa_scores(0)
            for hd in range(NSA_H):
                if hd + 1 < NSA_H:
                    nsa_scores(hd + 1)
                b, g = AX["nsa_att"] + 3 * hd, hd // (NSA_H // NSA_G)
                pe.wait_ge(prob_ready, hd + 1)
                transpose4(b, lambda q: n_P[:, hd % 2, q * P:(q + 1) * P])
                transpose4(b + 1, lambda q: n_P[:, hd % 2, (4 + q) * P:(5 + q) * P])
                o = take_aux(b + 2)
                wait_aux_out(pe, b)
                wait_aux_out(pe, b + 1)
                cols = slice(g * DH, (g + 1) * DH)
                for y_ in range(2):
                    for i in range(NT):
                        nc.tensor.matmul(o[:, y_ * DH:(y_ + 1) * DH], n_PT[:, 2 * y_ + i, :], n_v[:, y_, i, cols],
                                         start=(i == 0), stop=(i == 1))
                for y_ in range(2):
                    nc.tensor.matmul(o[:, (2 + y_) * DH:(3 + y_) * DH], n_PT[:, 4 + y_, :], n_v[:, y_, 0, cols],
                                     start=True, stop=True)
                for i in range(NT):
                    last = nc.tensor.matmul(o[:, (4 + i) * DH:(5 + i) * DH], n_PT[0:CMP_N, 6 + i, :],
                                            n_vcmp[0:CMP_N, cols], start=True, stop=True)
                last.then_inc(aux_ready, 1)
            pe.wait_ge(o_ready, NSA_H)
            for i in range(NT):
                for c in range(2):
                    transpose4(AX["nsa_oT"] + 2 * i + c,
                               lambda q: n_o[:, 1 - i, (4 * c + q) * P:(4 * c + q + 1) * P])
            wait_transposed("nsa_oT", 4)
            for s in range(2):
                slab_a(SL["nsa_out"] + s, PJ["nsa_out"] + s, n_oT)
            norm_to_features(2)
            experts(1)
            norm_to_features(3)

            for s in range(3):
                slab_b(SL["att_in"] + s, PJ["att_in"] + s, hT)
            slab_a(SL["att_in"] + 3, PJ["att_in"] + 3, hT)
            slab_a(SL["att_in"] + 4, PJ["att_in"] + 4, hT, 256)
            pe.wait_ge(stage_loaded, 48)
            mode_a(take_aux(AX["dt"])[:, 0:128].rearrange("p (i n) -> p i n", i=NT), w_dt, hT, 64).then_inc(aux_ready, 1)

            def att_scores(hd):
                s = take_aux(AX["att"] + 3 * hd)
                half = slice(hd % 2 * DH, hd % 2 * DH + DH)
                for i in range(NT):
                    last = nc.tensor.matmul(s[:, i * T:(i + 1) * T], a_qkT[half, hd // 2, i * P:(i + 1) * P],
                                            a_qkT[half, 6 + hd // 2, :], start=True, stop=True)
                last.then_inc(aux_ready, 1)

            def xbc_half(n):
                j = PJ["att"] + n // 2
                dst = (take_pair(j) if n % 2 == 0 else pair(j)).rearrange("p (c t) -> p c t", c=4)
                w3 = slab(SL["att"] + n // 2).rearrange("p (k n) -> p k n", k=KC)
                for c in (2 * (n % 2), 2 * (n % 2) + 1):
                    for k in range(KC):
                        last = nc.tensor.matmul(dst[:, c, :], w3[:, k, c * P:(c + 1) * P], hT[:, k, :],
                                                start=(k == 0), stop=(k == KC - 1))
                if n % 2:
                    last.then_inc(slab_done, 1)

            for s in range(5):
                if s >= 3:
                    wait_pair_out(pe, PJ["att_in"] + s)
            for hd in range(ATT_H):
                att_scores(hd)
                xbc_half(hd)
                b = AX["att"] + 3 * hd
                pe.wait_ge(att_exp_ready, hd + 1)
                transpose4(b + 1, lambda q: a_P[:, hd % 2, q * P:(q + 1) * P])
                o = take_aux(b + 2)
                wait_aux_out(pe, b + 1)
                for i in range(NT):
                    for k in range(NT):
                        last = nc.tensor.matmul(o[:, i * DH:(i + 1) * DH],
                                                a_PT[:, hd % 2, (2 * i + k) * P:(2 * i + k + 1) * P],
                                                a_v[:, k, hd * DH:(hd + 1) * DH], start=(k == 0), stop=(k == 1))
                last.then_inc(aux_ready, 1)

            for s in range(4):
                slab_b(SL["gates"] + s, PJ["gates"] + s, hT)
            pe.wait_ge(att_y_ready, 1)
            transpose4(AX["att_T"], lambda q: a_y[:, q // 2, q % 2 * P:(q % 2 + 1) * P])
            c = take_aux(AX["cums"])
            pe.wait_ge(a_ready, 1)
            for k, (tri, i, r) in enumerate(((tri_ge, 0, 1), (tri_le, 1, 0), (tri_gt, 0, 0), (tri_lt, 1, 1))):
                last = nc.tensor.matmul(c[:, k * 32:(k + 1) * 32], tri, s_a[:, i, r * 32:(r + 1) * 32],
                                        start=True, stop=True)
            last.then_inc(aux_ready, 1)
            pe.wait_ge(xbc_ready, 12)
            for i in range(NT):
                for g in range(SSD_G):
                    transpose4(AX["xT"] + 4 * i + g, lambda q: xbcT[:, 4 * g + q, i * P:(i + 1) * P])

            for g in range(SSD_G):
                b, j = AX["ssd"] + 11 * g, PJ["ssd"] + 2 * g
                cb = take_aux(b)
                for k in range(NT):
                    last = nc.tensor.matmul(cb[:, k * T:(k + 1) * T], xbcT[:, 16 + g, k * P:(k + 1) * P],
                                            xbcT[:, 20 + g, :], start=True, stop=True)
                last.then_inc(aux_ready, 1)
                diag = take_pair(j).rearrange("p (i n) -> p i n", i=NT)

                def decay_sums(h_):
                    dst = take_aux(b + 1 + h_)
                    hh = 8 * g + h_
                    pe.wait_ge(a4_ready, hh + 1)
                    for k in range(4):
                        last = nc.tensor.matmul(dst[:, k * P:(k + 1) * P], s_A4[:, hh % 2, k, :],
                                                (tri_le, tri_ge)[k // 2], start=True, stop=True)
                    last.then_inc(aux_ready, 1)

                def z_part(h_):
                    dst = (take_pair(j + 1) if h_ == 0 else pair(j + 1)).rearrange("p (i n) -> p i n", i=NT)
                    w3 = slab(SL["ssd"] + g).rearrange("p (k n) -> p k n", k=KC)
                    i = h_ // 4
                    for k in (2 * (h_ % 4), 2 * (h_ % 4) + 1):
                        last = nc.tensor.matmul(dst[:, i, :], hT[:, k, i * P:(i + 1) * P], w3[:, k, :],
                                                start=(k == 0), stop=(k == KC - 1))
                    if h_ == 7:
                        last.then_inc(slab_done, 1)

                decay_sums(0)
                for h_ in range(8):
                    hh = 8 * g + h_
                    if h_ < 7:
                        decay_sums(h_ + 1)
                    z_part(h_)
                    if h_ == 0:
                        pe.wait_ge(xdt_ready, g + 1)
                    pe.wait_ge(m_ready, hh + 1)
                    for i in range(NT):
                        for r in range(2):
                            last = nc.tensor.matmul(diag[:, i, h_ * DH:(h_ + 1) * DH], s_M[:, hh % 2, 2 * r + i, :],
                                                    s_xdt[:, r, i, h_ * DH:(h_ + 1) * DH],
                                                    start=(r == 0), stop=(r == 1))
                    last.then_inc(diag_done, 1)
                pe.wait_ge(cb_ready, g + 1)
                for i in range(NT):
                    last = nc.tensor.matmul(take_aux(b + 9 + i), s_cbx[:, 1 - i, :], s_xd[:, 1 - i, :],
                                            start=True, stop=True)
                    last.then_inc(aux_ready, 1)
                pe.wait_ge(aux_ready, AR["ssd"] + 11 * (g + 1))
                pe.nop().then_inc(group_done, 1)

            pe.wait_ge(pattn_loaded, 16)
            wait_aux_out(pe, AX["att_T"])
            for c2 in range(4):
                dst = take_aux(AX["proj_attn"] + c2)
                for c in range(2):
                    for k in range(2):
                        last = nc.tensor.matmul(dst[:, c * T:(c + 1) * T],
                                                pattn[:, k, (2 * c2 + c) * P:(2 * c2 + c + 1) * P], a_yT[:, k, :],
                                                start=(k == 0), stop=(k == 1))
                last.then_inc(aux_ready, 1)
            for g in range(SSD_G):
                for i in range(NT):
                    pe.wait_ge(ssd_n_ready, 2 * g + i + 1)
                    transpose4(AX["ssd_yT"] + 2 * g + i,
                               lambda q: s_x[:, i, (4 * g + q) * P:(4 * g + q + 1) * P])
            wait_transposed("ssd_yT", 8)
            for s in range(4):
                dst = take_aux(AX["proj_ssd"] + s)
                w = slab(SL["proj_ssd"] + s).rearrange("p (k n) -> p k n", k=16)
                for c in range(2):
                    for k in range(16):
                        last = nc.tensor.matmul(dst[:, c * T:(c + 1) * T], w[:, k, c * P:(c + 1) * P], s_yT[:, k, :],
                                                start=(k == 0), stop=(k == 15))
                last.then_inc(slab_done, 1)
            pe.wait_ge(mix_ready, 4)
            for s in range(2):
                slab_a(SL["out2"] + s, PJ["out2"] + s, mixT)
            norm_to_features(4)
            for s in range(8):
                slab_b(SL["up"] + s, PJ["up"] + s, hT)
            wait_pair_out(pe, PJ["up"] + 6)
            wait_pair_out(pe, PJ["up"] + 7)
            accumulate("down", 8, fT)

        @block.scalar
        def _(act):
            link = chain(act, act_chain)

            def copy_transposed(stage, batches, which, dst, groups=2):
                for b in which:
                    i, c = b // groups, b % groups
                    act.wait_ge(aux_ready, AR[stage] + b + 1)
                    nc.scalar.activation(dst[:, 4 * c:4 * c + 4, i * P:(i + 1) * P],
                                         aux(AX[stage] + b).rearrange("p (q t) -> p q t", q=4),
                                         ACT.Copy).then_inc(aux_out[(AX[stage] + b) % 4], 1)

            for j in range(4, 8):
                act.wait_ge(slab_done, j + 1)
                nc.scalar.activation(r_v[:, :, (j - 4) * 512:(j - 3) * 512],
                                     pair(j).rearrange("p (i n) -> p i n", i=NT),
                                     ACT.Copy).then_inc(pair_out[j % 2], 1)
            for hd in range(RET_H):
                j = 8 + hd
                act.wait_ge(slab_done, j + 1)
                nc.scalar.activation(r_g[:, :, hd * 512:(hd + 1) * 512],
                                     pair(j).rearrange("p (i n) -> p i n", i=NT),
                                     ACT.Silu).then_inc(pair_out[j % 2], 1)
                for i in range(NT):
                    b = 3 * hd + 1 + i
                    act.wait_ge(aux_ready, b + 1)
                    nc.scalar.activation(r_o[:, i, hd * 512:(hd + 1) * 512], aux(b),
                                         ACT.Copy).then_inc(aux_out[b % 4], 1)
            act.wait_ge(ret_var_ready, 1)
            nc.scalar.activation(r_rstd, r_mv[:, :, :, 1], ACT.Sqrt).then_inc(ret_std_ready, 1)
            for hd in range(RET_H):
                b = 2 * hd + 1
                act.wait_ge(aux_ready, AR["ret_yT"] + b + 1)
                nc.scalar.activation(r_yT[:, 4 * hd:4 * hd + 4, P:T],
                                     aux(AX["ret_yT"] + b).rearrange("p (q t) -> p q t", q=4),
                                     ACT.Copy).then_inc(aux_out[(AX["ret_yT"] + b) % 4], 1)

            def norm(n):
                act.wait_ge(var_ready, n + 1)
                nc.scalar.activation(rstd, mv[:, :, 1], ACT.Sqrt).then_inc(std_ready, 1)
                copy_transposed(f"ln{n}", 4, (1, 3), hT)

            norm(0)

            def experts(layer):
                n0, j0 = SL[f"moe{layer}"], PJ[f"moe{layer}"]
                act.wait_ge(aux_ready, AR[f"router{layer}"] + 1)
                logits = aux(AX[f"router{layer}"])
                nc.scalar.activation(aff, logits[:, 0:NT * N_EXP].rearrange("p (i e) -> p i e", i=NT),
                                     ACT.Sigmoid).then_inc(aux_out[AX[f"router{layer}"] % 4], 1)

                def silu(done, e):
                    act.wait_ge(slab_done, done)
                    nc.scalar.activation(m_sg, pair(j0), ACT.Silu).then_inc(pair_out[j0 % 2], 1)

                silu(n0 + 1, 0)
                with act.Fori(1, N_EXP) as e:
                    act.wait_ge(pair_out[(j0 + 1) % 2], e + (j0 + 1) // 2)
                    silu(e * 3 + n0, e)

            experts(0)
            norm(1)

            act.wait_ge(aux_ready, AR["nsa_in"] + 1)
            gates = aux(AX["nsa_in"])[:, 0:96].rearrange("p (i h n) -> p i h n", i=NT, h=NSA_H)
            for k, (i, n) in enumerate(((1, 1), (1, 2), (0, 1), (0, 2), (1, 0), (0, 0))):
                last = nc.scalar.activation(n_gw[:, :, k], gates[:, i, :, n], ACT.Sigmoid)
            last.then_inc(aux_out[AX["nsa_in"] % 4], 1)
            for ty in (KSLC, KWIN):
                for i in range(NT):
                    b = 2 * ty + i
                    act.wait_ge(aux_ready, AR["nsa_T"] + b + 1)
                    nc.scalar.activation(n_kT[:, ty - 2, :, i * P:(i + 1) * P],
                                         aux(AX["nsa_T"] + b).rearrange("p (g t) -> p g t", g=NSA_G),
                                         ACT.Copy).then_inc(aux_out[(AX["nsa_T"] + b) % 4], 1)
            for b in range(4):
                i, c = b // 2, b % 2
                act.wait_ge(aux_ready, AR["nsa_T"] + 8 + b + 1)
                nc.scalar.activation(n_qT[:, 4 * c:4 * c + 4, i * P:(i + 1) * P],
                                     aux(AX["nsa_T"] + 8 + b).rearrange("p (q t) -> p q t", q=4),
                                     ACT.Copy).then_inc(aux_out[(AX["nsa_T"] + 8 + b) % 4], 1)
            for kv in range(2):
                act.wait_ge(slab_done, SL["cmp"] + kv + 1)
                nc.scalar.activation(n_hid[:, kv, :, :].rearrange("p f n -> p (f n)"), aux(AX["cmp"] + kv)[:, 0:120],
                                     ACT.Gelu_apprx_tanh).then_inc(aux_out[(AX["cmp"] + kv) % 4], 1)
            act.wait_ge(aux_ready, AR["cmp"] + 1)
            nc.scalar.activation(n_kcmp, aux(AX["cmp"] + 2)[:, 0:60], ACT.Copy).then_inc(aux_out[(AX["cmp"] + 2) % 4], 1)
            act.wait_ge(aux_ready, AR["cmp"] + 2)
            nc.scalar.activation(n_vcmp[0:CMP_N, :], aux(AX["cmp"] + 3)[0:CMP_N, 0:256],
                                 ACT.Copy).then_inc(aux_out[(AX["cmp"] + 3) % 4], 1)
            act.wait_ge(p_zeroed, 1)

            def nsa_exps(hd):
                u = hd % 2
                act.wait_ge(nmax_ready, hd + 1)
                for k, (a, c, n) in enumerate(((0, 0, 256), (256, 256, 256), (512, 512, 128), (640, 640, 128),
                                               (768, 768, CMP_N), (784, 896, CMP_N))):
                    last = nc.scalar.activation(n_P[:, u, c:c + n], n_S[:, u, a:a + n], ACT.Exp,
                                                bias=n_nmax[:, u, k:k + 1], accum_out=n_sum[:, u, k:k + 1])
                last.then_inc(exp_ready, 1)

            nsa_exps(0)
            for hd in range(NSA_H):
                if hd + 1 < NSA_H:
                    nsa_exps(hd + 1)
                for v in range(2):
                    b = 3 * hd + v
                    act.wait_ge(aux_ready, AR["nsa_att"] + b + 1)
                    nc.scalar.activation(n_PT[:, 4 * v:4 * v + 4, :].rearrange("p a t -> p (a t)"),
                                         aux(AX["nsa_att"] + b), ACT.Copy).then_inc(aux_out[(AX["nsa_att"] + b) % 4], 1)
            copy_transposed("nsa_oT", 4, (1, 3), n_oT)
            norm(2)
            experts(1)
            norm(3)

            act.wait_ge(h_ready, 8)
            for s in range(5):
                j = PJ["att_in"] + s
                act.wait_ge(slab_done, SL["att_in"] + s + 1)
                if s < 3:
                    nc.scalar.activation(a_qkT[:, 4 * s:4 * s + 4, :], pair(j).rearrange("p (c t) -> p c t", c=4),
                                         ACT.Copy).then_inc(pair_out[j % 2], 1)
                else:
                    n = (512, 256)[s - 3]
                    nc.scalar.activation(a_v[:, :, (s - 3) * 512:(s - 3) * 512 + n],
                                         pair(j).rearrange("p (i n) -> p i n", i=NT)[:, :, 0:n],
                                         ACT.Copy).then_inc(pair_out[j % 2], 1)
            act.wait_ge(stage_loaded, 48)
            act.wait_ge(dt_v_ready, 1)
            nc.scalar.activation(s_A, a_log, ACT.Exp)
            nc.scalar.activation(s_u, s_m, ACT.Exp, scale=-1.0).then_inc(dt_u_ready, 1)
            act.wait_ge(dt_w_ready, 1)
            nc.scalar.activation(s_l, s_m, ACT.Ln).then_inc(dt_l_ready, 1)

            act.wait_ge(raw_zeroed, 1)

            def conv_out(n):
                act.wait_ge(conv_ready, n + 1)
                for c in range(2):
                    last = nc.scalar.activation(xbcT[:, 2 * n + c, :], c_acc[:, n % 2, c, :], ACT.Silu,
                                                bias=conv_b[:, 2 * n + c:2 * n + c + 1])
                last.then_inc(xbc_ready, 1)

            for hd in range(ATT_H):
                u = hd % 2
                act.wait_ge(att_max_ready, hd + 1)
                for i in range(NT):
                    last = nc.scalar.activation(a_P[:, u, i * T:(i + 1) * T], a_S[:, u, i * T:(i + 1) * T], ACT.Exp,
                                                bias=a_nmax[:, hd, i:i + 1], accum_out=a_den[:, hd, i:i + 1])
                last.then_inc(att_exp_ready, 1)
                b = 3 * hd + 1
                act.wait_ge(aux_ready, AR["att"] + b + 1)
                nc.scalar.activation(a_PT[:, u, :], aux(AX["att"] + b), ACT.Copy).then_inc(aux_out[(AX["att"] + b) % 4], 1)
                if hd % 2:
                    s = hd // 2
                    j = PJ["att"] + s
                    act.wait_ge(slab_done, SL["att"] + s + 1)
                    if s >= 2:
                        act.wait_ge(conv_ready, 2 * (s - 2) + 2)
                    nc.scalar.activation(c_raw[:, s % 2, :, 2:2 + T], pair(j).rearrange("p (c t) -> p c t", c=4),
                                         ACT.Copy).then_inc(pair_out[j % 2], 1)
                if hd >= 3:
                    conv_out(hd - 3)
            for n in range(9, 12):
                conv_out(n)
            act.wait_ge(att_o_ready, ATT_H)
            nc.scalar.activation(a_lse, a_den, ACT.Ln).then_inc(att_lse_ready, 1)
            act.wait_ge(att_mix_ready, 1)
            nc.scalar.activation(a_w, a_lse, ACT.Exp).then_inc(att_lse_ready, 1)
            for s in range(4):
                j = PJ["gates"] + s
                act.wait_ge(slab_done, SL["gates"] + s + 1)
                for c in range(4):
                    last = nc.scalar.activation(gateT[:, 4 * s + c, :], pair(j)[:, c * T:(c + 1) * T], ACT.Sigmoid,
                                                bias=b_gate[:, 4 * s + c:4 * s + c + 1])
                last.then_inc(pair_out[j % 2], 1)
            act.wait_ge(aux_ready, AR["cums"] + 1)
            nc.scalar.activation(s_E, aux(AX["cums"])[:, 0:128].rearrange("p (k h) -> p k h", k=4),
                                 ACT.Exp).then_inc(aux_out[AX["cums"] % 4], 1)
            wait_aux_out(act, AX["cums"])
            act.nop().then_inc(decay_ready, 1)
            for b in range(1, 8, 2):
                act.wait_ge(aux_ready, AR["xT"] + b + 1)
                nc.scalar.activation(s_x[:, b // 4, b % 4 * 512:(b % 4 + 1) * 512], aux(AX["xT"] + b),
                                     ACT.Copy).then_inc(aux_out[(AX["xT"] + b) % 4], 1)
            for g in range(SSD_G):
                for h_ in range(8):
                    hh, b = 8 * g + h_, 11 * g + 1 + h_
                    act.wait_ge(aux_ready, AR["ssd"] + b + 1)
                    if hh >= 2:
                        act.wait_ge(m_ready, hh - 1)
                    nc.scalar.activation(s_L[:, hh % 2, :], aux(AX["ssd"] + b), ACT.Exp).then_inc(
                        aux_out[(AX["ssd"] + b) % 4], 1)
                j = PJ["ssd"] + 2 * g + 1
                act.wait_ge(slab_done, SL["ssd"] + g + 1)
                if g:
                    act.wait_ge(ssd_y_ready, g)
                nc.scalar.activation(s_z, pair(j).rearrange("p (i n) -> p i n", i=NT), ACT.Silu).then_inc(
                    pair_out[j % 2], 1)
                act.wait_ge(ssd_y_ready, g + 1)
                for i in range(NT):
                    last = nc.scalar.activation(s_junk, s_x[:, i, g * 512:(g + 1) * 512], ACT.Square,
                                                accum_out=s_ss[:, i, g:g + 1])
                    last.then_inc(square_ready, 1)
                    act.wait_ge(square_ready, 2 * g + i + 1)
            act.wait_ge(ssd_var_ready, 1)
            nc.scalar.activation(s_rstd, s_rstd, ACT.Sqrt).then_inc(ssd_std_ready, 1)
            for g in range(SSD_G):
                b = 2 * g + 1
                act.wait_ge(aux_ready, AR["ssd_yT"] + b + 1)
                nc.scalar.activation(s_yT[:, 4 * g:4 * g + 4, P:T],
                                     aux(AX["ssd_yT"] + b).rearrange("p (q t) -> p q t", q=4),
                                     ACT.Copy).then_inc(aux_out[(AX["ssd_yT"] + b) % 4], 1)
            norm(4)
            for s in range(8):
                j = PJ["up"] + s
                act.wait_ge(slab_done, SL["up"] + s + 1)
                if s >= 2:
                    wait_pair_out(act, j - 2)
                nc.scalar.activation(f_relu[:, s % 2, :], pair(j), ACT.Relu).then_inc(f_ready, 1)
            act.wait_ge(var_ready, 6)
            nc.scalar.activation(rstd, mv[:, :, 1], ACT.Sqrt).then_inc(std_ready, 1)

        @block.vector
        def _(dve):
            link = chain(dve, dve_chain)
            V = nc.vector

            def copy_transposed(stage, batches, which, dst, groups=2):
                for b in which:
                    i, c = b // groups, b % groups
                    dve.wait_ge(aux_ready, AR[stage] + b + 1)
                    V.tensor_copy(dst[:, 4 * c:4 * c + 4, i * P:(i + 1) * P],
                                  aux(AX[stage] + b).rearrange("p (q t) -> p q t", q=4)
                                  ).then_inc(aux_out[(AX[stage] + b) % 4], 1)

            dve.wait_ge(stage_loaded, 16)
            for j in range(4):
                dve.wait_ge(slab_done, j + 1)
                if j:
                    dve.wait_ge(rope_ready, j)
                src = pair(j).rearrange("p (h f t) -> p h f t", h=2, f=2)
                cos = r_cos[j // 2].unsqueeze(1).broadcast_to([P, 2, T])
                sin = r_sin[j // 2].unsqueeze(1).broadcast_to([P, 2, T])
                V.tensor_tensor(r_t[:, 0], src[:, :, 0, :], cos, ALU.mult)
                V.tensor_tensor(r_t[:, 1], src[:, :, 1, :], sin, ALU.mult)
                V.tensor_tensor(r_t[:, 2], src[:, :, 1, :], cos, ALU.mult)
                V.tensor_tensor(r_t[:, 3], src[:, :, 0, :], sin, ALU.mult).then_inc(pair_out[j % 2], 1)
                wait_pair_out(dve, j)
                V.tensor_tensor(r_qkT[:, 2 * j:2 * j + 2, 0, :], r_t[:, 0], r_t[:, 1], ALU.subtract)
                V.tensor_tensor(r_qkT[:, 2 * j:2 * j + 2, 1, :], r_t[:, 2], r_t[:, 3],
                                ALU.add).then_inc(rope_ready, 1)
            for hd in range(RET_H):
                b = 3 * hd
                dve.wait_ge(aux_ready, b + 1)
                V.tensor_tensor(r_P[:, hd % 2, 0:T], aux(b)[:, 0:T], decay[:, hd, :], ALU.mult)
                V.tensor_tensor(r_P[:, hd % 2, T:T + P], aux(b)[:, T:T + P], decay[:, hd, 0:P],
                                ALU.mult).then_inc(aux_out[b % 4], 1)
                wait_aux_out(dve, b)
                V.engine_nop().then_inc(ret_p_ready, 1)
                for i in range(NT):
                    wait_aux_out(dve, b + 1 + i)
                    V.bn_stats(r_st6[:, hd, i, :], r_o[:, i, hd * 512:(hd + 1) * 512]).then_inc(dve_stats, 1)
            dve.wait_ge(dve_stats, 8)
            for hd in range(RET_H):
                for i in range(NT):
                    last = V.bn_aggr(r_mv[:, hd, i, :], r_st6[:, hd, i, :])
            link(last)
            V.tensor_scalar_add(r_mv[:, :, :, 1], r_mv[:, :, :, 1], EPS).then_inc(ret_var_ready, 1)
            dve.wait_ge(ret_std_ready, 1)
            link(V.reciprocal(r_rstd, r_rstd))
            wait_pair_out(dve, 11)
            for hd in range(RET_H):
                for i in range(NT):
                    o = r_o[:, i, hd * 512:(hd + 1) * 512]
                    link(V.tensor_scalar(o, o, r_mv[:, hd, i, 0:1], r_rstd[:, hd, i:i + 1], ALU.subtract, ALU.mult))
                    V.tensor_tensor(o, o, r_g[:, i, hd * 512:(hd + 1) * 512], ALU.mult).then_inc(ret_y_ready, 1)
                    if i == 1 or True:
                        pass
                b = 2 * hd
                dve.wait_ge(aux_ready, AR["ret_yT"] + b + 1)
                V.tensor_copy(r_yT[:, 4 * hd:4 * hd + 4, 0:P],
                              aux(AX["ret_yT"] + b).rearrange("p (q t) -> p q t", q=4)
                              ).then_inc(aux_out[(AX["ret_yT"] + b) % 4], 1)

            def norm(n, transposed=True):
                for i in range(NT):
                    for c in range(2):
                        last = V.bn_stats(st6[:, i, c, :], y[:, i, c * 512:(c + 1) * 512])
                link(last)
                for i in range(NT):
                    last = V.bn_aggr(mv[:, i, :], st6[:, i, :, :])
                link(last)
                V.tensor_scalar_add(mv[:, :, 1], mv[:, :, 1], EPS).then_inc(var_ready, 1)
                dve.wait_ge(std_ready, n + 1)
                link(V.reciprocal(rstd, rstd))
                dve.wait_ge(gb_loaded, 16 * (n + 1))
                for i in range(NT):
                    link(V.tensor_scalar(y[:, i, :], y[:, i, :], mv[:, i, 0:1], rstd[:, i:i + 1],
                                         ALU.subtract, ALU.mult))
                    link(V.tensor_tensor(y[:, i, :], y[:, i, :], gb[:, 0, :], ALU.mult))
                    V.tensor_tensor(h[:, i, :], y[:, i, :], gb[:, 1, :], ALU.add).then_inc(h_ready, 1)
                if transposed:
                    copy_transposed(f"ln{n}", 4, (0, 2), hT)

            def add_residual_by_tile(stage, alpha):
                dve.wait_ge(slab_done, SL[stage] + SLABS_OF[stage])
                for i in range(NT):
                    j = PJ[stage] + i
                    V.scalar_tensor_tensor(out=y[:, i, :], in0=h[:, i, :], scalar=alpha, in1=pair(j),
                                           op0=ALU.mult, op1=ALU.add).then_inc(pair_out[j % 2], 1)
                    wait_pair_out(dve, j)

            dve.wait_ge(x_loaded, 32)
            add_residual_by_tile("ret_out", ALPHA0)
            norm(0)

            def experts(layer):
                n0, j0, b0 = SL[f"moe{layer}"], PJ[f"moe{layer}"], AX[f"moe{layer}"]
                wait_aux_out(dve, AX[f"router{layer}"])
                G = N_EXP // EXP_PER_GROUP
                link(V.tensor_tensor(selsc.rearrange("p (i e) -> p i e", i=NT), aff,
                                     router_b.unsqueeze(1).broadcast_to([P, NT, N_EXP]), ALU.add))
                s4 = selsc.rearrange("p (g i) -> p g i", i=4)
                for i in range(4):
                    si = s4[:, :, i:i + 1].broadcast_to([P, NT * G, 4])
                    link(V.tensor_tensor(cmpA3, s4, si, ALU.is_gt))
                    link(V.tensor_tensor(cmpB3, s4, si, ALU.is_equal))
                    link(V.tensor_tensor(cmpB3, cmpB3, tie[:, i, :].unsqueeze(1).broadcast_to([P, NT * G, 4]), ALU.mult))
                    link(V.tensor_tensor(cmpA3, cmpA3, cmpB3, ALU.add))
                    link(V.tensor_reduce(rank4[:, :, i], cmpA3, AXX, ALU.add))
                link(V.tensor_single_scalar(rank, rank, 1.5, ALU.is_lt))
                link(V.tensor_tensor(cmpB[:, 0:32], selsc, rank, ALU.mult))
                link(V.tensor_reduce(grp, cmpB[:, 0:32].rearrange("p (g i) -> p g i", i=4), AXX, ALU.add))
                g4 = grp.rearrange("p (t g) -> p t g", t=NT)
                for g in range(G):
                    gi = g4[:, :, g:g + 1].broadcast_to([P, NT, G])
                    link(V.tensor_tensor(cmpA2, g4, gi, ALU.is_gt))
                    link(V.tensor_tensor(cmpB2, g4, gi, ALU.is_equal))
                    link(V.tensor_tensor(cmpB2, cmpB2, tie[:, g, :].unsqueeze(1).broadcast_to([P, NT, G]), ALU.mult))
                    link(V.tensor_tensor(cmpA2, cmpA2, cmpB2, ALU.add))
                    link(V.tensor_reduce(grank.rearrange("p (t g) -> p t g", t=NT)[:, :, g], cmpA2, AXX, ALU.add))
                link(V.tensor_single_scalar(grank, grank, 0.5, ALU.is_lt))
                link(V.tensor_tensor(rank4, rank4, grank.unsqueeze(2).broadcast_to([P, NT * G, 4]), ALU.mult))
                gflat = gw.rearrange("p i e -> p (i e)")
                link(V.tensor_tensor(gflat, aff.rearrange("p i e -> p (i e)"), rank, ALU.mult))
                link(V.tensor_reduce(wsum, gw, AXX, ALU.add))
                link(V.reciprocal(wsum, wsum))
                link(V.tensor_tensor(gw, gw, wsum.unsqueeze(2).broadcast_to([P, NT, N_EXP]), ALU.mult))

                def hidden(e):
                    dve.wait_ge(slab_done, e * 3 + (n0 + 2))
                    dve.wait_ge(pair_out[j0 % 2], e + (j0 // 2 + 1))
                    V.tensor_tensor(m_he, m_sg, pair(j0 + 1), ALU.mult).then_inc(pair_out[(j0 + 1) % 2], 1)

                def add(e, done):
                    dve.wait_ge(slab_done, done)
                    for q in range(4):
                        i, c, b = q // 2, q % 2, b0 + q
                        part = y[:, i, c * 512:(c + 1) * 512]
                        dve.wait_ge(aux_out[b % 4], e + b // 4)
                        V.scalar_tensor_tensor(out=part, in0=aux(b), scalar=gw[:, i, bass.ds(e, 1)], in1=part,
                                               op0=ALU.mult, op1=ALU.add).then_inc(aux_out[b % 4], 1)

                dve.wait_ge(y_zeroed, layer + 1)
                hidden(0)
                with dve.Fori(0, N_EXP - 1) as e:
                    add(e, e * 3 + (n0 + 4))
                    hidden(e + 1)
                add(N_EXP - 1, n0 + 48)
                for q in range(4):
                    b = b0 + 60 + q
                    wait_aux_out(dve, b)
                for i in range(NT):
                    last = V.scalar_tensor_tensor(out=y[:, i, :], in0=h[:, i, :], scalar=ALPHA0, in1=y[:, i, :],
                                                  op0=ALU.mult, op1=ALU.add)
                link(last)

            experts(0)
            norm(1)

            dve.wait_ge(stage_loaded, 32)

            def rotate(src, heads, cos, sin, outs, signal):
                w4 = lambda t: t.unsqueeze(2).broadcast_to([P, NT, heads, 32])
                t = [n_t[:, a, 0:NT * heads * 32].rearrange("p (i h d) -> p i h d", i=NT, h=heads) for a in range(4)]
                V.tensor_tensor(t[0], src[:, :, :, 0, :], w4(cos), ALU.mult)
                V.tensor_tensor(t[1], src[:, :, :, 1, :], w4(sin), ALU.mult)
                V.tensor_tensor(t[2], src[:, :, :, 1, :], w4(cos), ALU.mult)
                last = V.tensor_tensor(t[3], src[:, :, :, 0, :], w4(sin), ALU.mult)
                signal(last)
                for o in outs:
                    V.tensor_tensor(o[:, :, :, 0, :], t[0], t[1], ALU.subtract)
                    last = V.tensor_tensor(o[:, :, :, 1, :], t[2], t[3], ALU.add)
                return last

            for s in range(5):
                j = PJ["nsa_in"] + s
                dve.wait_ge(slab_done, SL["nsa_in"] + s + 1)
                if s:
                    dve.wait_ge(nsa_rot, s)
                src = pair(j).rearrange("p (i n) -> p i n", i=NT)
                if s < 3:
                    k = src[:, :, 0:256].rearrange("p i (g f d) -> p i g f d", g=NSA_G, f=2)
                    v = src[:, :, 256:512]
                    kd = n_dup[:, (KCMP, KSLC, KWIN)[s]].rearrange("p i g u (f d) -> p i g u f d", f=2)
                    if s == 0:
                        v = v.rearrange("p i (g d) -> p i g d", g=NSA_G)
                        for u in range(2):
                            V.tensor_copy(n_dup[:, VCMP, :, :, u, :], v)
                    else:
                        V.tensor_copy(n_v[:, s - 1, :, :], v)
                    last = rotate(k, NSA_G, n_cos, n_sin, [kd[:, :, :, u] for u in range(2)],
                                  lambda x: (x.then_inc(pair_out[j % 2], 1), wait_pair_out(dve, j)))
                else:
                    q = src.rearrange("p i (h f d) -> p i h f d", h=8, f=2)
                    o = n_q[:, :, (s - 3) * 512:(s - 2) * 512].rearrange("p i (h f d) -> p i h f d", h=8, f=2)
                    last = rotate(q, 8, n_cosq, n_sinq, [o],
                                  lambda x: (x.then_inc(pair_out[j % 2], 1), wait_pair_out(dve, j)))
                last.then_inc(nsa_rot, 1)
            for kv in range(2):
                for i in range(NT):
                    b = 2 * kv + i
                    dve.wait_ge(aux_ready, AR["nsa_T"] + b + 1)
                    src = aux(AX["nsa_T"] + b).rearrange("p (g t) -> p g t", g=NSA_G)
                    first = 1 - i
                    V.tensor_copy(n_cT[0:64, kv, :, i * P:(i + 1) * P], src[0:64])
                    V.tensor_copy(n_cT[64:P, kv, :, i * P + first - 1:(i + 1) * P - 1],
                                  src[64:P, :, first:P]).then_inc(aux_out[(AX["nsa_T"] + b) % 4], 1)
            for kv in range(2):
                for i in range(NT):
                    wait_aux_out(dve, AX["nsa_T"] + 2 * kv + i)
                for g in range(NSA_G):
                    row = n_cT[:, kv, g, :]
                    win = bass.AP(tensor=row.tensor, offset=row.offset, ap=[row.ap[0], [2, 16], [CMP_STRIDE, CMP_N]])
                    last = V.tensor_tensor(n_blk[:, kv, :, g, :], win,
                                           cmp_pe[kv].unsqueeze(2).broadcast_to([P, 16, CMP_N]), ALU.add)
                last.then_inc(blk_ready, 1)

            def nsa_masked(hd):
                u, j = hd % 2, PJ["nsa_att"] + hd
                dve.wait_ge(score_ready, hd + 1)
                V.tensor_tensor(n_S[:, u, 0:768], pair(j)[:, 0:768], causal, ALU.add)
                sc = n_S[:, u, 768:800].rearrange("p (i n) -> p i n", i=NT)[:, :, 0:CMP_N]
                V.tensor_tensor(sc, pair(j)[:, 768:800].rearrange("p (i n) -> p i n", i=NT)[:, :, 0:CMP_N],
                                cmp_add, ALU.add).then_inc(pair_out[j % 2], 1)
                wait_pair_out(dve, j)
                V.tensor_reduce(n_max[:, u, 0:2], n_S[:, u, 0:512].rearrange("p (k n) -> p k n", k=2), AXX, ALU.max)
                V.tensor_reduce(n_max[:, u, 2:4], n_S[:, u, 512:768].rearrange("p (k n) -> p k n", k=2), AXX, ALU.max)
                link(V.tensor_reduce(n_max[:, u, 4:6], sc, AXX, ALU.max))
                V.tensor_single_scalar(n_nmax[:, u, :], n_max[:, u, :], -1.0, ALU.mult).then_inc(nmax_ready, 1)

            nsa_masked(0)
            for hd in range(NSA_H):
                if hd + 1 < NSA_H:
                    nsa_masked(hd + 1)
                u, b = hd % 2, AX["nsa_att"] + 3 * hd
                dve.wait_ge(exp_ready, hd + 1)
                pc = n_P[:, u, 768:1024].rearrange("p (i n) -> p i n", i=NT)[:, :, 0:CMP_N]
                V.tensor_tensor(pc, pc, cmp_one, ALU.mult).then_inc(prob_ready, 1)
                link(V.reciprocal(n_w[:, u, :], n_sum[:, u, :]))
                link(V.tensor_tensor(n_w[:, u, :], n_w[:, u, :], n_gw[:, hd, :], ALU.mult))
                dve.wait_ge(aux_ready, AR["nsa_att"] + 3 * hd + 3)
                if hd:
                    dve.wait_ge(o_ready, hd)
                V.tensor_tensor(n_ow, aux(b + 2)[:, 0:384].rearrange("p (k d) -> p k d", k=6),
                                n_w[:, u, :].unsqueeze(2).broadcast_to([P, 6, DH]),
                                ALU.mult).then_inc(aux_out[(b + 2) % 4], 1)
                wait_aux_out(dve, b + 2)
                four = n_ow[:, 0:4, :].rearrange("p (i y) d -> p i y d", i=NT)
                link(V.tensor_tensor(n_o2, four[:, :, 0, :], four[:, :, 1, :], ALU.add))
                V.tensor_tensor(n_o[:, :, hd * DH:(hd + 1) * DH], n_o2, n_ow[:, 4:6, :],
                                ALU.add).then_inc(o_ready, 1)
            copy_transposed("nsa_oT", 4, (0, 2), n_oT)

            def add_residual_by_half(stage, alpha):
                for s in range(2):
                    j = PJ[stage] + s
                    dve.wait_ge(slab_done, SL[stage] + s + 1)
                    V.scalar_tensor_tensor(out=y[:, :, s * 512:(s + 1) * 512], in0=h[:, :, s * 512:(s + 1) * 512],
                                           scalar=alpha, in1=pair(j).rearrange("p (i n) -> p i n", i=NT),
                                           op0=ALU.mult, op1=ALU.add).then_inc(pair_out[j % 2], 1)
                    wait_pair_out(dve, j)

            add_residual_by_half("nsa_out", ALPHA0)
            norm(2)
            experts(1)
            norm(3)

            dve.wait_ge(stage_loaded, 48)
            dve.wait_ge(aux_ready, AR["dt"] + 1)
            V.tensor_tensor(s_v, aux(AX["dt"])[:, 0:128].rearrange("p (i n) -> p i n", i=NT),
                            dt_bias.unsqueeze(1).broadcast_to([P, NT, 64]), ALU.add).then_inc(aux_out[AX["dt"] % 4], 1)
            wait_aux_out(dve, AX["dt"])
            V.scalar_tensor_tensor(out=s_m, in0=s_v, scalar=-1.0, in1=s_v, op0=ALU.mult,
                                   op1=ALU.max).then_inc(dt_v_ready, 1)
            dve.wait_ge(dt_u_ready, 1)
            V.tensor_scalar_add(s_m, s_u, 1.0).then_inc(dt_w_ready, 1)
            dve.wait_ge(dt_l_ready, 1)
            link(V.tensor_scalar_add(s_a, s_m, -1.0))
            link(V.tensor_single_scalar(s_dt, s_a, 0.0, ALU.is_equal))
            link(V.tensor_tensor(s_l, s_l, s_dt, ALU.add))
            link(V.tensor_tensor(s_a, s_a, s_dt, ALU.add))
            link(V.reciprocal(s_a, s_a))
            link(V.tensor_tensor(s_l, s_l, s_a, ALU.mult))
            link(V.tensor_tensor(s_l, s_l, s_u, ALU.mult))
            link(V.scalar_tensor_tensor(out=s_dt, in0=s_v, scalar=0.0, in1=s_l, op0=ALU.max, op1=ALU.add))
            V.scalar_tensor_tensor(out=s_a, in0=s_dt, scalar=-1.0, in1=s_A.unsqueeze(1).broadcast_to([P, NT, 64]),
                                   op0=ALU.mult, op1=ALU.mult).then_inc(a_ready, 1)

            def conv(n):
                if n % 2 == 0:
                    wait_pair_out(dve, PJ["att"] + n // 2)
                if n >= 2:
                    dve.wait_ge(xbc_ready, n - 1)
                for k in range(TAPS):
                    for c in range(2):
                        ch = 2 * n + c
                        tap = conv_w[:, ch * TAPS + k:ch * TAPS + k + 1]
                        src = c_raw[:, n // 2 % 2, 2 * (n % 2) + c, k:k + T]
                        if k == 0:
                            last = V.tensor_scalar(c_acc[:, n % 2, c, :], src, tap, None, ALU.mult)
                        else:
                            last = V.scalar_tensor_tensor(out=c_acc[:, n % 2, c, :], in0=src, scalar=tap,
                                                          in1=c_acc[:, n % 2, c, :], op0=ALU.mult, op1=ALU.add)
                    if k < TAPS - 1:
                        link(last)
                last.then_inc(conv_ready, 1)

            dve.wait_ge(att_loaded, 16)
            for hd in range(ATT_H):
                u, b = hd % 2, AX["att"] + 3 * hd
                dve.wait_ge(aux_ready, AR["att"] + 3 * hd + 1)
                V.scalar_tensor_tensor(out=a_S[:, u, :], in0=aux(b), scalar=DH ** -0.5, in1=a_bias[:, hd, :],
                                       op0=ALU.mult, op1=ALU.add).then_inc(aux_out[b % 4], 1)
                wait_aux_out(dve, b)
                link(V.tensor_reduce(a_max[:, hd, :], a_S[:, u, :].rearrange("p (i n) -> p i n", i=NT), AXX, ALU.max))
                V.tensor_single_scalar(a_nmax[:, hd, :], a_max[:, hd, :], -1.0, ALU.mult).then_inc(att_max_ready, 1)
                if hd >= 2:
                    conv(hd - 2)
                dve.wait_ge(aux_ready, AR["att"] + 3 * hd + 3)
                V.tensor_copy(a_o[:, hd, :, :], aux(b + 2)[:, 0:NT * DH].rearrange("p (i d) -> p i d", i=NT)
                              ).then_inc(aux_out[(b + 2) % 4], 1)
            conv(10)
            conv(11)
            wait_aux_out(dve, AX["att"] + 3 * ATT_H - 1)
            V.engine_nop().then_inc(att_o_ready, ATT_H)
            flat = lambda t: t.rearrange("p h i -> p (h i)")
            pats = lambda t: flat(t).rearrange("p (a n) -> p a n", a=ATT_PAT)
            by_head = lambda t: flat(t).rearrange("p (a n) -> p n a", a=ATT_PAT)
            dve.wait_ge(att_lse_ready, 1)
            link(V.tensor_tensor(a_lse, a_lse, a_max, ALU.add))
            link(V.tensor_reduce(a_top, by_head(a_lse), AXX, ALU.max))
            V.tensor_tensor(pats(a_lse), pats(a_lse), a_top.unsqueeze(1).broadcast_to([P, ATT_PAT, 8]),
                            ALU.subtract).then_inc(att_mix_ready, 1)
            dve.wait_ge(att_lse_ready, 2)
            link(V.tensor_reduce(a_sum, by_head(a_w), AXX, ALU.add))
            link(V.reciprocal(a_sum, a_sum))
            link(V.reciprocal(a_den, a_den))
            link(V.tensor_tensor(a_w, a_w, a_den, ALU.mult))
            link(V.tensor_tensor(pats(a_w), pats(a_w), a_sum.unsqueeze(1).broadcast_to([P, ATT_PAT, 8]), ALU.mult))
            of = a_o.rearrange("p h i d -> p (h i) d")
            link(V.tensor_tensor(of, of, flat(a_w).unsqueeze(2).broadcast_to([P, 24, DH]), ALU.mult))
            link(V.tensor_tensor(of[:, 0:8], of[:, 0:8], of[:, 8:16], ALU.add))
            V.tensor_tensor(a_y.rearrange("p i (h d) -> p h i d", h=4), a_o[:, 0:4], a_o[:, 8:12],
                            ALU.add).then_inc(att_y_ready, 1)
            dve.wait_ge(aux_ready, AR["att_T"] + 1)
            V.tensor_copy(a_yT.rearrange("p c (i t) -> p i c t", i=NT),
                          aux(AX["att_T"]).rearrange("p (i c t) -> p i c t", i=NT, c=2)).then_inc(aux_out[AX["att_T"] % 4], 1)
            for b in range(0, 8, 2):
                dve.wait_ge(aux_ready, AR["xT"] + b + 1)
                V.tensor_copy(s_x[:, b // 4, b % 4 * 512:(b % 4 + 1) * 512],
                              aux(AX["xT"] + b)).then_inc(aux_out[(AX["xT"] + b) % 4], 1)

            for g in range(SSD_G):
                b, j = AX["ssd"] + 11 * g, PJ["ssd"] + 2 * g
                dve.wait_ge(aux_ready, AR["ssd"] + 11 * g + 1)
                if g:
                    dve.wait_ge(group_done, g)
                cb = aux(b)
                blocks = cb.rearrange("p (k t) -> p k t", k=4)
                same = bass.AP(tensor=cb.tensor, offset=cb.offset, ap=[cb.ap[0], [3 * P, 2], [1, P]])
                V.tensor_tensor(s_cb[:, 0:2], same, tri_le.unsqueeze(1).broadcast_to([P, 2, P]), ALU.mult)
                V.tensor_tensor(s_cb[:, 2:4], same, tri_ge.unsqueeze(1).broadcast_to([P, 2, P]), ALU.mult)
                V.tensor_copy(s_cbx, blocks[:, 1:3, :]).then_inc(aux_out[b % 4], 1)
                wait_aux_out(dve, b)
                V.engine_nop().then_inc(cb_ready, 1)
                for h_ in range(8):
                    hh = 8 * g + h_
                    wait_aux_out(dve, b + 1 + h_)
                    if hh >= 2:
                        dve.wait_ge(diag_done, hh - 1)
                    V.tensor_tensor(s_M[:, hh % 2].rearrange("p k t -> p (k t)"), s_L[:, hh % 2, :],
                                    s_cb.rearrange("p k t -> p (k t)"), ALU.mult).then_inc(m_ready, 1)
                heads = lambda t: t.rearrange("p (h d) -> p h d", h=8)
                dve.wait_ge(aux_ready, AR["ssd"] + 11 * (g + 1))
                for i in range(NT):
                    V.tensor_tensor(heads(s_t[:, i, :]), heads(aux(b + 9 + i)),
                                    s_E[:, i, 8 * g:8 * g + 8].unsqueeze(2).broadcast_to([P, 8, DH]),
                                    ALU.mult).then_inc(aux_out[(b + 9 + i) % 4], 1)
                wait_aux_out(dve, b + 9)
                wait_aux_out(dve, b + 10)
                dve.wait_ge(diag_done, 8 * (g + 1))
                V.tensor_tensor(s_t, s_t, pair(j).rearrange("p (i n) -> p i n", i=NT),
                                ALU.add).then_inc(pair_out[j % 2], 1)
                xg = s_x[:, :, g * 512:(g + 1) * 512]
                x4 = xg.rearrange("p i (h d) -> p i h d", h=8)
                dve.wait_ge(xdt_ready, g + 1)
                link(V.tensor_tensor(x4, x4, d_skip[:, 8 * g:8 * g + 8].unsqueeze(1).unsqueeze(3)
                                     .broadcast_to([P, NT, 8, DH]), ALU.mult))
                wait_pair_out(dve, j)
                link(V.tensor_tensor(xg, xg, s_t, ALU.add))
                wait_pair_out(dve, j + 1)
                V.tensor_tensor(xg, xg, s_z, ALU.mult).then_inc(ssd_y_ready, 1)
            dve.wait_ge(square_ready, 8)
            V.tensor_scalar(s_rstd, s_ss, 1.0 / 512, EPS, ALU.mult, ALU.add).then_inc(ssd_var_ready, 1)
            for c2 in range(4):
                b = AX["proj_attn"] + c2
                dve.wait_ge(aux_ready, AR["proj_attn"] + c2 + 1)
                V.tensor_tensor(mixT[:, 2 * c2:2 * c2 + 2, :], gateT[:, 8 + 2 * c2:10 + 2 * c2, :],
                                aux(b).rearrange("p (c t) -> p c t", c=2), ALU.mult).then_inc(aux_out[b % 4], 1)
            dve.wait_ge(ssd_std_ready, 1)
            link(V.reciprocal(s_rstd, s_rstd))
            for g in range(SSD_G):
                for i in range(NT):
                    x_ = s_x[:, i, g * 512:(g + 1) * 512]
                    V.scalar_tensor_tensor(out=x_, in0=x_, scalar=s_rstd[:, i, g:g + 1],
                                           in1=norm_w[:, g * 512:(g + 1) * 512],
                                           op0=ALU.mult, op1=ALU.mult).then_inc(ssd_n_ready, 1)
                b = 2 * g
                dve.wait_ge(aux_ready, AR["ssd_yT"] + b + 1)
                V.tensor_copy(s_yT[:, 4 * g:4 * g + 4, 0:P],
                              aux(AX["ssd_yT"] + b).rearrange("p (q t) -> p q t", q=4)
                              ).then_inc(aux_out[(AX["ssd_yT"] + b) % 4], 1)
            for s in range(4):
                b = AX["proj_ssd"] + s
                dve.wait_ge(slab_done, SL["proj_ssd"] + s + 1)
                if s:
                    dve.wait_ge(mix_ready, s)
                V.tensor_tensor(mix_t, gateT[:, 2 * s:2 * s + 2, :].rearrange("p c t -> p (c t)"), aux(b),
                                ALU.mult).then_inc(aux_out[b % 4], 1)
                wait_aux_out(dve, b)
                m = mixT[:, 2 * s:2 * s + 2, :].rearrange("p c t -> p (c t)")
                V.tensor_tensor(m, m, mix_t, ALU.add).then_inc(mix_ready, 1)
            add_residual_by_half("out2", ALPHA1)
            norm(4)
            for s in range(8):
                j = PJ["up"] + s
                dve.wait_ge(f_ready, s + 1)
                V.tensor_tensor(fT[:, 4 * s:4 * s + 4, :].rearrange("p c t -> p (c t)"), f_relu[:, s % 2, :], pair(j),
                                ALU.mult).then_inc(pair_out[j % 2], 1)
            add_residual_by_tile("down", ALPHA1)
            norm(5, transposed=False)


def _slab_8x512(w):
    n = w.shape[1] // 512
    return w.reshape(KC, P, n, 512).transpose(2, 1, 0, 3).reshape(n, P, SLAB)


def _slab_4x1024(w):
    n = w.shape[0] // 512
    return w.reshape(n, 4, P, D).transpose(0, 2, 1, 3).reshape(n, P, SLAB)


def _slab_16x256(w):
    n = w.shape[1] // 256
    return w.reshape(16, P, n, 256).transpose(2, 1, 0, 3).reshape(n, P, SLAB)


def _padded(w, cols):
    return np.concatenate([w, np.zeros((w.shape[0], cols - w.shape[1]), w.dtype)], 1)


def _rows(v):
    return np.broadcast_to(v.reshape(1, -1), (P, v.size))


def _moe_slabs(gate, up, down):
    g, u = (w.reshape(N_EXP, KC, P, 512).transpose(0, 2, 1, 3).reshape(N_EXP, P, SLAB) for w in (gate, up))
    d = down.reshape(N_EXP, 4, P, D).transpose(0, 2, 1, 3).reshape(N_EXP, P, SLAB)
    out = [g[0:1]]
    for e in range(N_EXP):
        out.append(u[e:e + 1])
        if e + 1 < N_EXP:
            out.append(g[e + 1:e + 2])
        out.append(d[e:e + 1])
    return out


def _chunks(w):
    return w.reshape(-1, P, w.shape[1]).transpose(1, 0, 2).reshape(P, -1)


def _rope(dim, theta=10000.0):
    f = np.float32
    inv = (f(theta) ** (-np.arange(0, dim, 2, dtype=f) / f(dim))).astype(f)
    ang = np.arange(T, dtype=f)[:, None] * inv[None, :]
    return np.cos(ang).astype(f), np.sin(ang).astype(f)


def _shape_constants():
    f = np.float32
    c = {}
    cos, sin = _rope(256)
    c["cosq"], c["sinq"] = cos.T, sin.T
    c["cosk"], c["sink"] = cos.T / f(16), sin.T / f(16)
    log_gamma = np.log1p(-(f(2.0) ** (f(-5.0) - np.arange(RET_H, dtype=f)))).astype(f)
    diff = (np.arange(T)[None, :] - np.arange(P)[:, None]).astype(f)
    decay = np.where(diff >= 0, np.exp(log_gamma[:, None, None] * np.maximum(diff, 0)), 0).astype(f)
    c["decay"] = decay.transpose(1, 0, 2).reshape(P, -1)
    c["ident"] = np.eye(P, dtype=f)
    c["tie"] = _rows((np.arange(4)[None, :] < np.arange(4)[:, None]).astype(f))
    cos, sin = _rope(DH)
    tokens = lambda t: t.reshape(NT, P, -1).transpose(1, 0, 2).reshape(P, -1)
    n = {"cosk": tokens(cos), "sink": tokens(sin), "cosq": tokens(cos / f(8)), "sinq": tokens(sin / f(8))}
    t, s = np.arange(P)[:, None], np.arange(T)[None, :]
    late = np.where(s <= t + P, 0, NEG).astype(f)
    early = np.where(s[:, :P] <= t, 0, NEG).astype(f)
    n["causal"] = np.concatenate([late, late, early, early], 1)
    end = np.arange(16)[None, :] * CMP_STRIDE + CMP_LEN - 1
    seen = np.concatenate([end <= t + P, end <= t], 1)
    n["cmp_add"], n["cmp_one"] = np.where(seen, 0, NEG).astype(f), seen.astype(f)
    c["nsa"] = n
    tri = {"le": t <= np.arange(P), "gt": t > np.arange(P), "ge": t >= np.arange(P), "lt": t < np.arange(P)}
    c["ssd"] = {k: v.astype(f) for k, v in tri.items()}
    slopes = (2.0 ** (-8.0 * np.arange(1, ATT_H + 1) / ATT_H)).astype(f)
    q = np.arange(T).reshape(NT, P).T
    rel = np.abs(q[:, :, None] - np.arange(T))
    bias = []
    for hd in range(ATT_H):
        window, dilation = ((128, 1), (512, 4), (2048, 16))[hd // ATT_HPP]
        seen = (rel % dilation == 0) & (rel // dilation <= window // (2 * dilation))
        bias.append(np.where(seen, -slopes[hd] * rel.astype(f), NEG).astype(f).reshape(P, -1))
    c["att"] = np.concatenate(bias, 1)
    return c


def _pack(cols, parts):
    return np.ascontiguousarray(np.concatenate([np.asarray(parts[n], np.float32) for n in cols], 1))


def _arrays(a):
    a = {n: np.asarray(v) for n, v in a.items()}
    c = _shape_constants()
    x = a["x"].reshape(T, D)
    ri = a["ret_w_in"][0]
    slabs = [_slab_8x512(ri), _slab_4x1024(a["ret_w_out"][0])]
    slabs += _moe_slabs(a["moe_w_gate"][0], a["moe_w_up"][0], a["moe_w_down"][0])
    slabs += [_slab_8x512(a["nsa_w_kv"]), _slab_8x512(a["nsa_w_in"][0][:, :D])]
    slabs += [a["cmp_k_w1"].reshape(1, 16, P, 256).transpose(0, 2, 1, 3).reshape(1, P, SLAB),
              a["cmp_v_w1"].reshape(1, 16, P, 256).transpose(0, 2, 1, 3).reshape(1, P, SLAB)]
    slabs += [_slab_8x512(a["nsa_w_out"][0])]
    slabs += _moe_slabs(a["moe_w_gate"][1], a["moe_w_up"][1], a["moe_w_down"][1])
    n = c["nsa"]
    n["pe_k"], n["pe_v"] = (a[k].reshape(16, P).T for k in ("cmp_pe_k", "cmp_pe_v"))
    n["w_gates"] = _chunks(a["nsa_w_in"][0][:, D:])
    w2 = a["cmp_k_w2"]
    n["w2k"], n["w2v"] = _chunks(np.concatenate([w2, w2], 1)), _chunks(a["cmp_v_w2"])
    w = a["w_in_2"]
    at = np.cumsum([0, D_INNER, CONV_CH * P, 2 * SSD_H, 2 * ATT_H * DH, ATT_H * DH, 2 * D])
    wz, wxbc, wdt, wqk, wv, wg = (w[:, i:j] for i, j in zip(at[:-1], at[1:]))
    v2 = np.zeros((1, P, SLAB), w.dtype)
    v2[0, :, :KC * 256] = _chunks(wv[:, 512:])
    slabs += [_slab_8x512(wqk), _slab_8x512(wv[:, :512]), v2, _slab_8x512(wxbc), _slab_8x512(wg), _slab_8x512(wz)]
    slabs += [_slab_16x256(a["w_proj_ssd_2"]), _slab_8x512(a["w_out_2"])]
    slabs += [_slab_8x512(a["w_up_2"]), _slab_4x1024(a["w_down_2"])]
    s = c["ssd"]
    s["w_dt"] = _chunks(wdt)
    s["dt_bias"] = _rows(np.concatenate([a["dt_bias_f_2"], a["dt_bias_b_2"]]))
    s["a_log"] = _rows(np.concatenate([a["a_log_f_2"], a["a_log_b_2"]]))
    s["d_skip"] = _rows(a["d_skip_2"])
    s["conv_w"] = a["conv_w_2"].reshape(TAPS, CONV_CH, P).transpose(2, 1, 0).reshape(P, -1)
    s["conv_b"] = a["conv_b_2"].reshape(CONV_CH, P).T
    s["b_gate"] = a["b_gate_2"].reshape(16, P).T
    s["norm_w"] = _rows(a["ssd_norm_w_2"])
    c["router_w"] = _chunks(a["router_w"])
    c["router_b"] = _rows(a["router_b"])
    ln = [np.stack([a["ln_mix_g"][0], a["ln_mix_b"][0]]), np.stack([a["ln_ffn_g"][0], a["ln_ffn_b"][0]]),
          np.stack([a["ln_mix_g"][1], a["ln_mix_b"][1]]), np.stack([a["ln_ffn_g"][1], a["ln_ffn_b"][1]]),
          np.stack([a["ln1_g_2"], a["ln1_b_2"]]), np.stack([a["ln2_g_2"], a["ln2_b_2"]])]
    out = {
        "x_tok": x.reshape(NT, P, D).transpose(1, 0, 2),
        "x_feat": x.T.reshape(KC, P, T).transpose(1, 0, 2),
        "slabs": np.concatenate(slabs, 0),
        "c_all": _pack(C_ALL, c), "c_ret": _pack(C_RET, c), "c_nsa": _pack(C_NSA, n), "c_ssd": _pack(C_SSD, s),
        "c_att": c["att"], "w_pattn": _chunks(a["w_proj_attn_2"]),
        "ln_gb": np.stack(ln).reshape(6, 2 * D),
    }
    return {n: np.ascontiguousarray(v) for n, v in out.items()}


def kernel(**inputs):
    import concourse.bacc as bacc
    from concourse.bass_utils import run_bass_kernel_spmd

    nc = bacc.Bacc("TRN2", target_bir_lowering=False, num_devices=1)
    arrays = _arrays(inputs)
    args = {n: nc.dram_tensor(n, v.shape, F32, kind="ExternalInput").ap() for n, v in arrays.items()}
    out = nc.dram_tensor("out", (NT, P, D), F32, kind="ExternalOutput").ap()
    build(nc, out=out, **args)
    r = run_bass_kernel_spmd(nc, [arrays], core_ids=[0])
    return r.results[0]["out"].reshape(1, T, D)
```

```python
from contextlib import ExitStack

import numpy as np
import concourse.bass as bass
from concourse import mybir

F32 = mybir.dt.float32
F32R = mybir.dt.float32r
ALU = mybir.AluOpType
ACT = mybir.ActivationFunctionType
AXX = mybir.AxisListType.X

P = 128
T = 256
NT = T // P
D = 1024
KC = D // P
SLAB = 4096
NSLOT = 3
WORK = 31520
SBUF_END = 229344
ALPHA0 = float((2.0 * 2) ** 0.25)
ALPHA1 = float(2.0 ** 0.25)
EPS = 1e-5
NEG = -1e30

RET_H = 4
RET_DV = 512
N_EXP = 16
EXP_PER_GROUP = 4
NSA_H, NSA_G, DH = 16, 4, 64
CMP_N, CMP_LEN, CMP_STRIDE = 15, 32, 16
SSD_H, SSD_G, SSD_N = 32, 4, 128
D_INNER = 2048
CONV_CH = 24
TAPS = 5
ATT_H, ATT_PAT, ATT_HPP = 12, 3, 4
D_FF = 4096

STAGES = [
    ("ret_in", 12, 12, 12, 12), ("ret_yT", 0, 0, 8, 8), ("ret_out", 4, 2, 0, 0), ("ln0", 0, 0, 4, 4),
    ("router0", 0, 0, 2, 2), ("moe0", 48, 0, 0, 0), ("ln1", 0, 0, 4, 4),
    ("nsa_in", 5, 5, 1, 1), ("nsa_T", 0, 0, 12, 12), ("cmp", 2, 0, 4, 2), ("nsa_att", 0, 16, 48, 48),
    ("nsa_oT", 0, 0, 4, 4), ("nsa_out", 2, 2, 0, 0), ("ln2", 0, 0, 4, 4),
    ("router1", 0, 0, 2, 2), ("moe1", 48, 0, 0, 0), ("ln3", 0, 0, 4, 4),
    ("att_in", 5, 5, 0, 0), ("dt", 0, 0, 1, 1), ("att", 6, 6, 36, 36), ("gates", 4, 4, 0, 0), ("att_T", 0, 0, 1, 1),
    ("cums", 0, 0, 1, 1), ("xT", 0, 0, 8, 8), ("ssd", 4, 8, 44, 44), ("proj_attn", 0, 0, 4, 4),
    ("ssd_yT", 0, 0, 8, 8), ("proj_ssd", 4, 0, 4, 0), ("out2", 2, 2, 0, 0), ("ln4", 0, 0, 4, 4),
    ("up", 8, 8, 0, 0), ("down", 8, 2, 0, 0),
]
SL, PJ, AX, AR = {}, {}, {}, {}
_at = [0, 0, 0, 0]
for _name, *_counts in STAGES:
    for _table, _n in zip((SL, PJ, AX, AR), _at):
        _table[_name] = _n
    _at = [x + n for x, n in zip(_at, _counts)]
N_SLABS = _at[0]
N_LN = 6
SLABS_OF = {name: n for name, n, *_ in STAGES}

def columns(**widths):
    at, out = 0, {}
    for name, w in widths.items():
        out[name] = (at, w)
        at += w
    return out, at

C_ALL, N_ALL = columns(ident=128, router_w=KC * N_EXP, router_b=N_EXP, tie=16,
                       before=128, ones=128, iota=128)
C_RET, N_RET = columns(cosq=256, sinq=256, cosk=256, sink=256, decay=RET_H * T)
C_NSA, N_NSA = columns(cosk=64, sink=64, cosq=64, sinq=64, causal=768, cmp_add=32, cmp_one=32,
                       pe_k=16, pe_v=16, w_gates=KC * 48, w2k=256, w2v=128)
C_SSD, N_SSD = columns(le=128, gt=128, ge=128, lt=128, w_dt=KC * 64, dt_bias=64, a_log=64, d_skip=SSD_H,
                       conv_w=CONV_CH * TAPS, conv_b=CONV_CH, b_gate=16, norm_w=D_INNER)
N_ATT = ATT_H * NT * T
N_PATTN = 2 * D


def build(nc, x_tok, x_feat, slabs, c_all, c_ret, c_nsa, c_ssd, c_att, w_pattn, ln_gb, out):
    ctx = ExitStack()
    with ctx:
        def sb(name, shape):
            return ctx.enter_context(nc.sbuf_tensor(name, shape, F32))

        def sem(name):
            return ctx.enter_context(nc.semaphore(name))

        ring = sb("ring", [P, NSLOT, SLAB])
        h = sb("h", [P, NT, D])
        hT = sb("hT", [P, KC, T])
        y = sb("y", [P, NT, D])
        gb = sb("gb", [P, 2, D])
        call = sb("call", [P, N_ALL])
        small = sb("small", [P, 512])
        work = nc.alloc_sbuf_tensor_at("work", [P, WORK], F32, offset=SBUF_END - 4 * WORK)

        def split_at(start, end):
            t = nc.alloc_sbuf_tensor_at(f"split{start}_{end}", [P, end - start], F32R,
                                        offset=SBUF_END - 4 * (WORK - start))
            return t[:, :]


        def const(t, cols, name):
            a, w = cols[name]
            return t[:, a:a + w]

        ident = const(call, C_ALL, "ident")
        router_w = const(call, C_ALL, "router_w").rearrange("p (k e) -> p k e", k=KC)
        router_b = const(call, C_ALL, "router_b")
        before, ones, iota = (const(call, C_ALL, n) for n in ("before", "ones", "iota"))
        tie = const(call, C_ALL, "tie").rearrange("p (i j) -> p i j", i=4)

        class Work:
            def __init__(self, at=0):
                self.at = at

            def __call__(self, n):
                self.at += n
                assert self.at <= WORK, self.at
                return work[:, self.at - n:self.at]

        ps = ctx.enter_context(nc.psum_tensor("ps", [P, 8, 512], F32))

        def bank(b, n=1):
            return ps[:, b:b + n, :].rearrange("p b n -> p (b n)")

        st6 = small[:, 0:24].rearrange("p (i a s) -> p i a s", i=NT, a=2)
        mv = small[:, 48:52].rearrange("p (i s) -> p i s", i=NT)
        rstd = small[:, 64:66]
        aff = small[:, 72:104].rearrange("p (i e) -> p i e", i=NT)
        selsc = small[:, 104:136]
        gw = small[:, 136:168].rearrange("p (i e) -> p i e", i=NT)
        rank = small[:, 168:200]
        grp = small[:, 200:208]
        grank = small[:, 208:216]
        wsum = small[:, 216:218]
        member = grank.rearrange("p (t g) -> p t g", t=NT)
        flag = ctx.enter_context(nc.sbuf_tensor("flag", [P, 1], mybir.dt.int32))
        rank4 = rank.rearrange("p (g i) -> p g i", i=4)
        best2 = small[:, 224:256]

        w_ = Work()
        cret = w_(N_RET)
        r_cos = [const(cret, C_RET, n) for n in ("cosq", "cosk")]
        r_sin = [const(cret, C_RET, n) for n in ("sinq", "sink")]
        decay = const(cret, C_RET, "decay").rearrange("p (h c) -> p h c", h=RET_H)
        r_qkT = w_(4096).rearrange("p (h f t) -> p h f t", h=2 * RET_H, f=2)
        r_v = w_(4096).rearrange("p (i n) -> p i n", i=NT)
        r_split = split_at(w_.at, w_.at + 12288)
        r_g = w_(4096).rearrange("p (i n) -> p i n", i=NT)
        r_o = w_(4096).rearrange("p (i n) -> p i n", i=NT)
        r_yT = w_(4096).rearrange("p (c t) -> p c t", c=16)
        r_P = w_(2 * 384).rearrange("p (b n) -> p b n", b=2)
        r_t = w_(4 * 512).rearrange("p (a h t) -> p a h t", a=4, h=2)
        r_st6 = w_(48).rearrange("p (h i s) -> p h i s", h=RET_H, i=NT)
        r_mv = w_(16).rearrange("p (h i s) -> p h i s", h=RET_H, i=NT)
        r_rstd = w_(8).rearrange("p (h i) -> p h i", h=RET_H)
        def two_parts(high, low, chunks):
            return [t.rearrange("p (c t) -> p c t", c=chunks) for t in (high, low)]

        def weight_halves(t):
            return t.rearrange("p (s b n) -> p s b n", s=2, b=2)

        r_hT = two_parts(r_split[:, 0:2048], r_split[:, 2048:4096], KC)
        r_w = weight_halves(r_split[:, 4096:12288])
        w_ = Work()
        n_hT_low = split_at(w_.at, w_.at + 2048)
        w_(2048)
        cnsa = w_(N_NSA)
        n_cos, n_sin, n_cosq, n_sinq = (const(cnsa, C_NSA, n).rearrange("p (i d) -> p i d", i=NT)
                                        for n in ("cosk", "sink", "cosq", "sinq"))
        causal = const(cnsa, C_NSA, "causal")
        cmp_add, cmp_one = (const(cnsa, C_NSA, n).rearrange("p (i n) -> p i n", i=NT)[:, :, 0:CMP_N]
                            for n in ("cmp_add", "cmp_one"))
        cmp_pe = [const(cnsa, C_NSA, n) for n in ("pe_k", "pe_v")]
        w_gates = const(cnsa, C_NSA, "w_gates")
        w2k = const(cnsa, C_NSA, "w2k").rearrange("p (f n) -> p f n", f=2)
        w2v = const(cnsa, C_NSA, "w2v").rearrange("p (f n) -> p f n", f=2)
        m_ = Work(w_.at)
        m_xT = m_(1024).rearrange("p (k s) -> p k s", k=KC)
        m_sg, m_he = m_(512), m_(512)
        m_heT = m_(512).rearrange("p (k s) -> p k s", k=4)
        m_S = m_(256).rearrange("p (i s) -> p i s", i=NT)
        m_ST = m_(1024)
        m_y = m_(4096)
        m_w = m_(16)
        m_pos = m_(8)
        m_tot = m_(4)
        m_c1, m_c2 = m_(128), m_(128)
        n_t = w_(4 * 512).rearrange("p (a n) -> p a n", a=4)
        KCMP, VCMP, KSLC, KWIN = range(4)
        n_dup_flat = w_(4 * 1024)
        n_dup = n_dup_flat.rearrange("p (y i g u d) -> p y i g u d", y=4, i=NT, g=NSA_G, u=2)
        n_oT = n_dup_flat[:, 0:2048].rearrange("p (c t) -> p c t", c=KC)
        n_v = w_(1024).rearrange("p (y i n) -> p y i n", y=2, i=NT)
        n_q = w_(2048).rearrange("p (i n) -> p i n", i=NT)
        n_w_split = weight_halves(split_at(w_.at, w_.at + 8192))
        n_qT = w_(2048).rearrange("p (c t) -> p c t", c=KC)
        n_kT = w_(2048).rearrange("p (y g t) -> p y g t", y=2, g=NSA_G)
        n_cT = w_(2048).rearrange("p (y g t) -> p y g t", y=2, g=NSA_G)
        n_blk = w_(2 * 960).rearrange("p (y c g n) -> p y c g n", y=2, c=16, g=NSA_G)
        n_hid = w_(240).rearrange("p (y f n) -> p y f n", y=2, f=2)
        n_kcmp = w_(60)
        n_vcmp = w_(256)
        n_gw = w_(96).rearrange("p (h k) -> p h k", h=NSA_H)
        n_S = w_(2 * 800).rearrange("p (b n) -> p b n", b=2)
        n_P = w_(2 * 1024).rearrange("p (b n) -> p b n", b=2)
        n_PT = w_(1024).rearrange("p (a t) -> p a t", a=8)
        n_o = w_(2048).rearrange("p (i n) -> p i n", i=NT)
        n_max = w_(12).rearrange("p (b k) -> p b k", b=2)
        n_nmax = w_(12).rearrange("p (b k) -> p b k", b=2)
        n_sum = w_(12).rearrange("p (b k) -> p b k", b=2)
        n_w = w_(12).rearrange("p (b k) -> p b k", b=2)
        n_ow = w_(384).rearrange("p (k d) -> p k d", k=6)
        n_o2 = w_(128).rearrange("p (i d) -> p i d", i=NT)
        n_hT = two_parts(split_at(WORK - 2048, WORK), n_hT_low, KC)
        assert w_.at <= WORK - 2048
        w_ = Work()
        cssd = w_(N_SSD)
        tri_le, tri_gt, tri_ge, tri_lt, w_dt, dt_bias, a_log, d_skip, conv_w, conv_b, b_gate, norm_w = (
            const(cssd, C_SSD, n) for n in C_SSD)
        pattn = y[:].rearrange("p i n -> p (i n)").rearrange("p (k n) -> p k n", k=2)
        a_w_split = split_at(w_.at, w_.at + 6144)
        xbcT = w_(6144).rearrange("p (c t) -> p c t", c=CONV_CH)
        s_yT = xbcT[:, 0:16, :]
        a_y = w_(512).rearrange("p (i n) -> p i n", i=NT)
        a_yT = w_(512).rearrange("p (c t) -> p c t", c=2)
        s_v = w_(128).rearrange("p (i n) -> p i n", i=NT)
        s_dt = w_(128).rearrange("p (i n) -> p i n", i=NT)
        s_a = w_(128).rearrange("p (i n) -> p i n", i=NT)
        s_u = w_(128).rearrange("p (i n) -> p i n", i=NT)
        s_l = w_(128).rearrange("p (i n) -> p i n", i=NT)
        s_m = w_(128).rearrange("p (i n) -> p i n", i=NT)
        s_A = w_(64)
        s_E = w_(128).rearrange("p (k h) -> p k h", k=4)
        shared_columns = w_.at
        catt = w_(N_ATT)
        a_bias = catt.rearrange("p (h n) -> p h n", h=ATT_H)
        a_qkT = w_(3072).rearrange("p (c t) -> p c t", c=12)
        a_v = w_(1536).rearrange("p (i n) -> p i n", i=NT)
        a_w_split2 = split_at(w_.at, w_.at + 2048)
        a_S = w_(1024).rearrange("p (b n) -> p b n", b=2)
        a_P = w_(1024).rearrange("p (b n) -> p b n", b=2)
        a_PT = w_(1024).rearrange("p (b n) -> p b n", b=2)
        a_o = w_(1536).rearrange("p (h i d) -> p h i d", h=ATT_H, i=NT)
        a_max, a_nmax, a_den, a_lse, a_w = (w_(24).rearrange("p (h i) -> p h i", h=ATT_H) for _ in range(5))
        a_top = w_(8)
        a_sum = w_(8)
        c_raw = w_(2 * 4 * 260).rearrange("p (b c t) -> p b c t", b=2, c=4)
        c_acc = w_(2 * 2 * 256).rearrange("p (b c t) -> p b c t", b=2, c=2)
        a_hT = two_parts(split_at(WORK - 4096, WORK - 2048), split_at(WORK - 2048, WORK), KC)
        w_ = Work(shared_columns)
        gateT = w_(4096).rearrange("p (c t) -> p c t", c=16)
        s_x = w_(4096).rearrange("p (i n) -> p i n", i=NT)
        s_xdt = w_(2048).rearrange("p (r i n) -> p r i n", r=2, i=NT)
        s_xd = w_(1024).rearrange("p (r n) -> p r n", r=2)
        s_cb = w_(512).rearrange("p (k t) -> p k t", k=4)
        s_cbx = w_(256).rearrange("p (k t) -> p k t", k=2)
        s_A4 = w_(1024).rearrange("p (b k t) -> p b k t", b=2, k=4)
        s_L = w_(1024).rearrange("p (b n) -> p b n", b=2)
        s_M = w_(1024).rearrange("p (b k t) -> p b k t", b=2, k=4)
        s_z = w_(1024).rearrange("p (i n) -> p i n", i=NT)
        s_t = w_(1024).rearrange("p (i n) -> p i n", i=NT)
        s_junk = w_(512)
        s_ss = w_(8).rearrange("p (i g) -> p i g", i=NT)
        s_rstd = w_(8).rearrange("p (i g) -> p i g", i=NT)
        mixT = s_xdt.rearrange("p r i n -> p (r i n)").rearrange("p (c t) -> p c t", c=KC)
        mix_t = s_z.rearrange("p i n -> p (i n)")[:, 0:512]
        w_ = Work()
        f_relu = w_(2048).rearrange("p (b n) -> p b n", b=2)
        f_T = two_parts(split_at(2048, 10240), split_at(10240, 18432), 32)
        f_hT = two_parts(split_at(18432, 20480), split_at(20480, 22528), KC)
        f_w = weight_halves(split_at(22528, 30720))

        slab_loaded = [sem(f"slab_loaded{i}") for i in range(NSLOT)]
        slab_done = sem("slab_done")
        pair_out = [sem("pair_out0"), sem("pair_out1")]
        aux_ready = sem("aux_ready")
        aux_out = [sem(f"aux_out{i}") for i in range(4)]
        x_loaded, h_loaded = sem("x_loaded"), sem("h_loaded")
        call_loaded = sem("call_loaded")
        stage_loaded = sem("stage_loaded")
        gb_loaded = sem("gb_loaded")
        stored = sem("stored")
        rope_ready = sem("rope_ready")
        ret_p_ready = sem("ret_p_ready")
        ret_var_ready = sem("ret_var_ready")
        ret_std_ready = sem("ret_std_ready")
        ret_y_ready = sem("ret_y_ready")
        nsa_rot = sem("nsa_rot")
        blk_ready = sem("blk_ready")
        score_ready = sem("score_ready")
        nmax_ready = sem("nmax_ready")
        att_loaded, pattn_loaded = sem("att_loaded"), sem("pattn_loaded")
        dt_v_ready, dt_u_ready, dt_w_ready, dt_l_ready, a_ready = (
            sem(n) for n in ("dt_v_ready", "dt_u_ready", "dt_w_ready", "dt_l_ready", "a_ready"))
        att_max_ready, att_exp_ready, att_o_ready = (sem(n) for n in ("att_max_ready", "att_exp_ready", "att_o_ready"))
        att_lse_ready, att_mix_ready, att_y_ready = (sem(n) for n in ("att_lse_ready", "att_mix_ready", "att_y_ready"))
        raw_zeroed, conv_ready, xbc_ready = sem("raw_zeroed"), sem("conv_ready"), sem("xbc_ready")
        a4_ready, xdt_ready, m_ready = sem("a4_ready"), sem("xdt_ready"), sem("m_ready")
        decay_ready, diag_done, group_done = sem("decay_ready"), sem("diag_done"), sem("group_done")
        cb_ready, ssd_y_ready, square_ready = sem("cb_ready"), sem("ssd_y_ready"), sem("square_ready")
        ssd_var_ready, ssd_std_ready, ssd_n_ready = sem("ssd_var_ready"), sem("ssd_std_ready"), sem("ssd_n_ready")
        mix_ready, f_ready = sem("mix_ready"), sem("f_ready")
        x_high, x_low = sem("x_high"), sem("x_low")
        w_high, w_low, half_done = sem("w_high"), sem("w_low"), sem("half_done")
        hT_high, f_high, f_low = sem("hT_high"), sem("f_high"), sem("f_low")
        exp_ready = sem("exp_ready")
        prob_ready = sem("prob_ready")
        o_ready = sem("o_ready")
        p_zeroed = sem("p_zeroed")
        var_ready = sem("var_ready")
        std_ready = sem("std_ready")
        h_ready = sem("h_ready")
        member_ready = sem("member_ready")
        flag_ready = sem("flag_ready")
        scattered, moe_out = sem("scattered"), sem("moe_out")
        over_scattered, over_out, over_pos = ([sem(f"{n}{layer}") for layer in range(2)]
                                              for n in ("over_scattered", "over_out", "over_pos"))

        class Pass:
            def __init__(self, layer, p):
                self.layer, self.p, self.n0 = layer, p, SL[f"moe{layer}"]
                tag = f"_{layer}{p}"
                self.onehot_ready, self.gathered, self.hidden_T = (sem(n + tag) for n in ("onehot", "gathered", "hidT"))
                self.gate_out, self.up_out, self.hidT_out, self.down_out, self.gather_out = (
                    sem(n + tag) for n in ("gate_out", "up_out", "hidT_out", "down_out", "gather_out"))
                if p:
                    self.loaded = [sem(f"over_loaded{i}{tag}") for i in range(NSLOT)]
                    self.done, self.base = sem("over_done" + tag), 0
                else:
                    self.loaded, self.done, self.base = slab_loaded, slab_done, self.n0

            def slot(self, m):
                return (self.n0 + m) % NSLOT

            def load_count(self, m):
                return 16 * ((m if self.p else self.n0 + m) // NSLOT + 1)

        passes = [[Pass(layer, p) for p in range(2)] for layer in range(2)]
        dve_stats = sem("dve_stats")
        dve_chain = sem("dve_chain")
        act_chain = sem("act_chain")
        pool_chain = sem("pool_chain")

        block = ctx.enter_context(nc.Block())

        def chain(eng, signal):
            count = [0]

            def link(ins):
                count[0] += 1
                ins.then_inc(signal, 1)
                eng.wait_ge(signal, count[0])
            return link

        def wait_pair_out(eng, j):
            eng.wait_ge(pair_out[j % 2], j // 2 + 1)

        def wait_aux_out(eng, b):
            eng.wait_ge(aux_out[b % 4], b // 4 + 1)

        def pair(j):
            return bank(2 * (j % 2), 2)

        def aux(b):
            return bank(4 + b % 4)

        SPLIT_STAGES = (("ret_in", 8), ("nsa_in", 5), ("att_in", 5), ("up", 8), ("down", 8))
        SPLIT_SLABS = [SL[name] + s for name, n in SPLIT_STAGES for s in range(n)]
        SPLIT_STAGE = [name for name, n in SPLIT_STAGES for _ in range(n)]
        HQ = {name: 2 * SPLIT_STAGE.index(name) for name, _ in SPLIT_STAGES}

        def by_columns(q):
            n = SPLIT_SLABS[q // 2]
            return n < 4 or SL["att_in"] <= n < SL["att_in"] + 3 or SL["up"] <= n < SL["down"]

        def half_size(q):
            return (SLAB if SPLIT_SLABS[q // 2] != SL["att_in"] + 4 else KC * 256) // 2

        def ring_half(q):
            w, n = ring[:, SPLIT_SLABS[q // 2] % NSLOT, :], half_size(q)
            if by_columns(q):
                return w.rearrange("p (k n) -> p k n", k=KC)[:, :, q % 2 * T:(q % 2 + 1) * T]
            return w[:, q % 2 * n:(q % 2 + 1) * n]

        def split_half(q, part):
            stage, half = SPLIT_STAGE[q // 2], q % 2
            if stage == "att_in":
                at = (2 * part + half) * 2048
                return (a_w_split[:, at:at + half_size(q)] if at < 6144 else a_w_split2[:, 0:half_size(q)])
            return {"ret_in": r_w, "nsa_in": n_w_split, "up": f_w, "down": f_w}[stage][:, part, half, :]

        def split_shaped(q, part):
            t = split_half(q, part)
            return t.rearrange("p (k n) -> p k n", k=KC) if by_columns(q) else t

        @block.sync
        def _(sp):
            def load(n, slot):
                sp.dma_start(ring[:, slot, :], slabs[n]).then_inc(slab_loaded[slot], 16)

            def stream(a, b):
                r0, r1 = -(-a // NSLOT), b // NSLOT
                for n in range(a, r0 * NSLOT):
                    if n >= NSLOT:
                        sp.wait_ge(slab_done, n - NSLOT + 1)
                    load(n, n % NSLOT)
                with sp.Fori(r0, r1) as r:
                    for slot in range(NSLOT):
                        sp.wait_ge(slab_done, r * NSLOT + (slot - NSLOT + 1))
                        load(r * NSLOT + slot, slot)
                for n in range(r1 * NSLOT, b):
                    sp.wait_ge(slab_done, n - NSLOT + 1)
                    load(n, n % NSLOT)

            def stream_again(over):
                n0 = over.n0
                sp.wait_ge(slab_done, n0 + 48)
                for m in range(NSLOT):
                    sp.dma_start(ring[:, over.slot(m), :], slabs[n0 + m]).then_inc(over.loaded[over.slot(m)], 16)
                with sp.Fori(1, 48 // NSLOT) as r:
                    for m in range(NSLOT):
                        sp.wait_ge(over.done, r * NSLOT + (m - NSLOT + 1))
                        sp.dma_start(ring[:, over.slot(m), :],
                                     slabs[r * NSLOT + (n0 + m)]).then_inc(over.loaded[over.slot(m)], 16)
                sp.wait_ge(over.done, 48)

            sp.dma_start(hT[:], x_feat).then_inc(x_loaded, 16)
            for n in range(NSLOT):
                load(n, n)
            at = NSLOT
            for layer in range(2):
                stream(at, SL[f"moe{layer}"] + 48)
                at = SL[f"moe{layer}"] + 48
                sp.wait_ge(flag_ready, layer + 1)
                with sp.If(sp.value_load(flag[0:1, 0:1], min_val=0, max_val=1)):
                    stream_again(passes[layer][1])
            stream(at, N_SLABS)
            for i in range(NT):
                sp.wait_ge(h_ready, 2 * N_LN - 1 + i)
                sp.dma_start(out[i], h[:, i, :]).then_inc(stored, 16)
            sp.wait_ge(stored, 16 * NT)

        @block.gpsimd
        def _(pool):
            pool.dma_start(cret, c_ret).then_inc(stage_loaded, 16)
            pool.dma_start(call[:], c_all).then_inc(call_loaded, 16)
            pool.dma_start(h[:], x_tok).then_inc(h_loaded, 16)

            def load_gb(n):
                if n:
                    pool.wait_ge(h_ready, 2 * n)
                pool.dma_start(gb[:].rearrange("p a n -> p (a n)"),
                               ln_gb[n:n + 1, :].broadcast_to([P, 2 * D])).then_inc(gb_loaded, 16)

            load_gb(0)
            load_gb(1)
            pool.dma_start(cnsa, c_nsa).then_inc(stage_loaded, 16)
            load_gb(2)
            nc.gpsimd.memset(n_P, 0.0).then_inc(p_zeroed, 1)
            load_gb(3)
            pool.wait_ge(h_ready, 8)
            pool.dma_start(cssd, c_ssd).then_inc(stage_loaded, 16)
            pool.dma_start(catt, c_att).then_inc(att_loaded, 16)
            pool.dma_start(y[:].rearrange("p i n -> p (i n)"), w_pattn).then_inc(pattn_loaded, 16)
            load_gb(4)
            pool.wait_ge(slab_done, SL["att"])
            nc.gpsimd.memset(c_raw, 0.0).then_inc(raw_zeroed, 1)

            pool.wait_ge(a_ready, 1)
            pool.wait_ge(xbc_ready, 12)

            def decays(hh):
                if hh >= 2:
                    pool.wait_ge(aux_ready, AR["ssd"] + 11 * ((hh - 2) // 8) + 2 + (hh - 2) % 8)
                for r, tri in enumerate((tri_gt, tri_lt)):
                    last = nc.gpsimd.tensor_tensor(s_A4[:, hh % 2, 2 * r:2 * r + 2, :],
                                                   tri.unsqueeze(1).broadcast_to([P, NT, P]),
                                                   s_a[:, :, 32 * r + hh:32 * r + hh + 1].broadcast_to([P, NT, P]),
                                                   ALU.mult)
                last.then_inc(a4_ready, 1)


            for hh in range(SSD_H):
                g, k = hh // 8, hh % 8
                if hh == 0:
                    wait_aux_out(pool, AX["xT"] + 7)
                    wait_aux_out(pool, AX["xT"] + 6)
                    wait_aux_out(pool, AX["xT"] + 5)
                    wait_aux_out(pool, AX["xT"] + 4)
                    pool.wait_ge(decay_ready, 1)
                decays(hh)
                if k == 0:
                    if g:
                        pool.wait_ge(group_done, g)
                    xg = s_x[:, :, g * 512:(g + 1) * 512].rearrange("p i (h d) -> p i h d", h=8)
                    for r in range(2):
                        d = s_dt[:, :, 32 * r + 8 * g:32 * r + 8 * g + 8].unsqueeze(3).broadcast_to([P, NT, 8, DH])
                        last = nc.gpsimd.tensor_tensor(s_xdt[:, r].rearrange("p i (h d) -> p i h d", h=8), xg, d, ALU.mult)
                    last.then_inc(pool_chain, 1)
                    pool.wait_ge(pool_chain, g + 1)
                    for r in range(2):
                        last = nc.gpsimd.tensor_tensor(
                            s_xd[:, r].rearrange("p (h d) -> p h d", h=8),
                            s_xdt[:, r, r].rearrange("p (h d) -> p h d", h=8),
                            s_E[:, 2 + r, 8 * g:8 * g + 8].unsqueeze(2).broadcast_to([P, 8, DH]), ALU.mult)
                    last.then_inc(xdt_ready, 1)
            load_gb(5)

        @block.tensor
        def _(pe):
            def slab(n):
                pe.wait_ge(slab_loaded[n % NSLOT], 16 * (n // NSLOT + 1))
                return ring[:, n % NSLOT, :]

            def take_pair(j):
                if j >= 2:
                    wait_pair_out(pe, j - 2)
                return pair(j)

            def take_aux(b):
                if b >= 4:
                    wait_aux_out(pe, b - 4)
                return aux(b)

            def mode_a(dst, w, src, cols=512):
                w3 = w[:, 0:KC * cols].rearrange("p (k n) -> p k n", k=KC)
                for i in range(NT):
                    for k in range(KC):
                        last = nc.tensor.matmul(dst[:, i, 0:cols], src[:, k, i * P:(i + 1) * P], w3[:, k, :],
                                                start=(k == 0), stop=(k == KC - 1))
                return last

            def mode_b(dst, w, src):
                w3 = w.rearrange("p (k n) -> p k n", k=KC)
                for c in range(4):
                    for k in range(KC):
                        last = nc.tensor.matmul(dst[:, c, :], w3[:, k, c * P:(c + 1) * P], src[:, k, :],
                                                start=(k == 0), stop=(k == KC - 1))
                return last

            def split_columns(dst, q, src):
                half = q % 2
                pe.wait_ge(w_low, q + 1)
                w3 = [split_half(q, part).rearrange("p (k n) -> p k n", k=KC) for part in range(2)]
                for c in range(2):
                    at = (2 * half + c) * T
                    for k in range(KC):
                        for t, (a, b) in enumerate(SPLIT):
                            last = nc.tensor.matmul(dst[:, at:at + T], w3[a][:, k, c * P:(c + 1) * P],
                                                    src[b][:, k, :], start=(k == 0 and t == 0),
                                                    stop=(k == KC - 1 and t == 2))
                last.then_inc((half_done, slab_done)[half], 1)

            def split_rows(dst, q, src):
                half = q % 2
                pe.wait_ge(w_low, q + 1)
                w3 = [split_half(q, part).rearrange("p (k n) -> p k n", k=4) for part in range(2)]
                cols = half_size(q) // 4
                for i in range(NT):
                    for k in range(4):
                        for t, (a, b) in enumerate(SPLIT):
                            last = nc.tensor.matmul(dst[:, i * 512:i * 512 + cols],
                                                    src[a][:, 4 * half + k, i * P:(i + 1) * P], w3[b][:, k, :],
                                                    start=(half == k == t == 0),
                                                    stop=(half == 1 and k == 3 and t == 2))
                last.then_inc((half_done, slab_done)[half], 1)

            def split_slabs(stage, n, src):
                for s in range(n):
                    dst = take_pair(PJ[stage] + s)
                    for q in (HQ[stage] + 2 * s, HQ[stage] + 2 * s + 1):
                        (split_columns if by_columns(q) else split_rows)(dst, q, src)

            def slab_a(n, j, src, cols=512):
                dst = take_pair(j).rearrange("p (i n) -> p i n", i=NT)
                mode_a(dst, slab(n), src, cols).then_inc(slab_done, 1)

            def slab_b(n, j, src):
                dst = take_pair(j).rearrange("p (c t) -> p c t", c=4)
                mode_b(dst, slab(n), src).then_inc(slab_done, 1)

            def transpose4(b, src):
                dst = take_aux(b)
                for q in range(4):
                    last = nc.tensor.transpose(dst[:, q * P:(q + 1) * P], src(q), ident)
                last.then_inc(aux_ready, 1)

            def tokens_to_features(stage, src, groups, ready, first):
                for i in range(NT):
                    pe.wait_ge(ready, first + i)
                    for c in range(groups):
                        transpose4(AX[stage] + groups * i + c,
                                   lambda q: src[:, i, (4 * c + q) * P:(4 * c + q + 1) * P])

            def wait_transposed(stage, batches):
                for b in range(max(0, batches - 4), batches):
                    wait_aux_out(pe, AX[stage] + b)

            SPLIT = ((0, 0), (0, 1), (1, 0))
            pe.wait_ge(x_low, 1)
            split_slabs("ret_in", 8, r_hT)
            pe.wait_ge(rope_ready, 4)
            for hd in range(RET_H):
                b = AX["ret_in"] + 3 * hd
                s = take_aux(b)
                for m in range(NT):
                    cols = slice(0, T) if m == 0 else slice(T, T + P)
                    for f in range(2):
                        last = nc.tensor.matmul(s[:, cols], r_qkT[:, RET_H + hd, f, m * P:(m + 1) * P],
                                                r_qkT[:, hd, f, m * P:T], start=(f == 0), stop=(f == 1))
                last.then_inc(aux_ready, 1)
                slab_a(8 + hd, 8 + hd, hT)
                pe.wait_ge(ret_p_ready, hd + 1)
                wait_pair_out(pe, 4 + hd)
                cols = slice(hd * RET_DV, (hd + 1) * RET_DV)
                o = take_aux(b + 1)
                nc.tensor.matmul(o, r_P[:, hd % 2, 0:P], r_v[:, 0, cols],
                                 start=True, stop=True).then_inc(aux_ready, 1)
                o = take_aux(b + 2)
                nc.tensor.matmul(o, r_P[:, hd % 2, P:T], r_v[:, 0, cols], start=True, stop=False)
                nc.tensor.matmul(o, r_P[:, hd % 2, T:T + P], r_v[:, 1, cols],
                                 start=False, stop=True).then_inc(aux_ready, 1)
            pe.wait_ge(call_loaded, 16)
            for hd in range(RET_H):
                for i in range(NT):
                    pe.wait_ge(ret_y_ready, 2 * hd + i + 1)
                    transpose4(AX["ret_yT"] + 2 * hd + i,
                               lambda q: r_o[:, i, (4 * hd + q) * P:(4 * hd + q + 1) * P])
            wait_transposed("ret_yT", 8)

            def accumulate(stage, n, src):
                dst = [take_pair(PJ[stage] + i) for i in range(NT)]
                for s in range(n):
                    w = slab(SL[stage] + s).rearrange("p (k n) -> p k n", k=4)
                    for i in range(NT):
                        for c in range(2):
                            for k in range(4):
                                last = nc.tensor.matmul(dst[i][:, c * 512:(c + 1) * 512],
                                                        src[:, 4 * s + k, i * P:(i + 1) * P],
                                                        w[:, k, c * 512:(c + 1) * 512],
                                                        start=(s == 0 and k == 0), stop=(s == n - 1 and k == 3))
                    last.then_inc(slab_done, 1)

            accumulate("ret_out", 4, r_yT)

            def norm_to_features(n):
                tokens_to_features(f"ln{n}", h, 2, h_ready, 2 * n + 1)
                wait_transposed(f"ln{n}", 4)

            norm_to_features(0)

            def expert_pass(ps_):
                def slab_of(m, G):
                    sl = ps_.slot(m)
                    pe.wait_ge(ps_.loaded[sl], G * 64 + ps_.load_count(m))
                    return ring[:, sl, :]

                def gather(g):
                    pe.wait_ge(ps_.onehot_ready, g + 1)
                    pe.wait_ge(ps_.gather_out, g + 1)

                    tok = bank(6, 2).rearrange("p (k s) -> p k s", k=KC)
                    for k in range(KC):
                        for i in range(NT):
                            nc.tensor.matmul(tok[:, k, :], h[:, i, k * P:(k + 1) * P], m_S[:, i, :],
                                             start=(i == 0), stop=(i == 1))
                    for i in range(NT):
                        nc.tensor.matmul(bank(3)[:, 0:4], m_S[:, i, :], gw[:, i, bass.ds(g * 4, 4)],
                                         start=(i == 0), stop=(i == 1))
                    for i in range(NT):
                        last = nc.tensor.transpose(bank(3)[:, (1 + i) * P:(2 + i) * P], m_S[:, i, :], ident)
                    last.then_inc(ps_.gathered, 1)

                def project(b, m, G, out_sem, e, part=range(KC)):
                    w3 = slab_of(m, G).rearrange("p (k n) -> p k n", k=KC)
                    if part[0] == 0:
                        pe.wait_ge(out_sem, e + 1)
                    for k in part:
                        last = nc.tensor.matmul(bank(b), m_xT[:, k, :], w3[:, k, :], start=(k == 0), stop=(k == KC - 1))
                    if part[-1] == KC - 1:
                        last.then_inc(ps_.done, 1)

                def transpose_hidden(e):
                    pe.wait_ge(ps_.up_out, e + 2)
                    pe.wait_ge(ps_.hidT_out, e + 1)
                    for q in range(4):
                        last = nc.tensor.transpose(bank(2)[:, q * P:(q + 1) * P], m_he[:, q * P:(q + 1) * P], ident)
                    last.then_inc(ps_.hidden_T, 1)

                def down(m, G, e):
                    w = slab_of(m, G).rearrange("p (k n) -> p k n", k=4)
                    pe.wait_ge(ps_.hidT_out, e + 2)
                    pe.wait_ge(ps_.down_out, e + 1)
                    for c in range(2):
                        for k in range(4):
                            last = nc.tensor.matmul(bank(4 + c), m_heT[:, k, :], w[:, k, c * 512:(c + 1) * 512],
                                                    start=(k == 0), stop=(k == 3))
                    last.then_inc(ps_.done, 1)

                def group(G, final):
                    for k in range(4):
                        e = G * 4 + k
                        project(1, 1 + 3 * k, G, ps_.up_out, e)
                        if k == 3 and not final:
                            gather(G + 1)
                            pe.wait_ge(ps_.gather_out, G + 3)
                        if k < 3 or not final:
                            project(0, 2 + 3 * k, G, ps_.gate_out, e + 1, range(0, 4))
                            transpose_hidden(e)
                            project(0, 2 + 3 * k, G, ps_.gate_out, e + 1, range(4, KC))
                            down(3 + 3 * k, G, e)
                        else:
                            transpose_hidden(e)
                            down(2 + 3 * k, G, e)

                gather(0)
                pe.wait_ge(ps_.gather_out, 2)
                project(0, 0, 0, ps_.gate_out, 0)
                with pe.Fori(0, 3) as G:
                    group(G, False)
                group(3, True)
                for out_sem in (ps_.gate_out, ps_.up_out, ps_.hidT_out, ps_.down_out):
                    pe.wait_ge(out_sem, 17)
                pe.wait_ge(ps_.gather_out, 5)
                for i in range(NT):
                    for c in range(2):
                        for g in range(4):
                            at = g * 256 + i * P
                            last = nc.tensor.matmul(bank(2 * i + c), m_ST[:, at:at + P],
                                                    m_y[:, g * 1024 + c * 512:g * 1024 + (c + 1) * 512],
                                                    start=(g == 0), stop=(g == 3))
                last.then_inc(over_scattered[ps_.layer] if ps_.p else scattered, 1)

            def experts(layer):
                logits = take_aux(AX[f"router{layer}"])
                for i in range(NT):
                    for k in range(KC):
                        last = nc.tensor.matmul(logits[:, i * N_EXP:(i + 1) * N_EXP], hT[:, k, i * P:(i + 1) * P],
                                                router_w[:, k, :], start=(k == 0), stop=(k == KC - 1))
                last.then_inc(aux_ready, 1)
                pos = take_aux(AX[f"router{layer}"] + 1)
                pe.wait_ge(member_ready, layer + 1)
                nc.tensor.matmul(pos[:, 0:4], before, member[:, 0, :], start=True, stop=True)
                for at, mat in ((4, before), (8, ones)):
                    nc.tensor.matmul(pos[:, at:at + 4], ones, member[:, 0, :], start=True, stop=False)
                    last = nc.tensor.matmul(pos[:, at:at + 4], mat, member[:, 1, :], start=False, stop=True)
                last.then_inc(aux_ready, 1)
                for q in range(2):
                    wait_aux_out(pe, AX[f"router{layer}"] + q)
                expert_pass(passes[layer][0])
                with pe.If(pe.value_load(flag[0:1, 0:1], min_val=0, max_val=1)):
                    pe.wait_ge(moe_out, layer + 1)
                    expert_pass(passes[layer][1])

            experts(0)
            norm_to_features(1)

            pe.wait_ge(stage_loaded, 32)
            mode_a(take_aux(AX["nsa_in"])[:, 0:96].rearrange("p (i n) -> p i n", i=NT),
                   w_gates, hT, 48).then_inc(aux_ready, 1)
            pe.wait_ge(x_low, 2)
            split_slabs("nsa_in", 5, n_hT)
            for ty in (KCMP, VCMP, KSLC, KWIN):
                pe.wait_ge(nsa_rot, (1, 1, 2, 3)[ty])
                for i in range(NT):
                    transpose4(AX["nsa_T"] + 2 * ty + i,
                               lambda g: n_dup[:, ty, i, g, :, :].rearrange("p u d -> p (u d)"))
            pe.wait_ge(nsa_rot, 5)
            for i in range(NT):
                for c in range(2):
                    transpose4(AX["nsa_T"] + 8 + 2 * i + c,
                               lambda q: n_q[:, i, (4 * c + q) * P:(4 * c + q + 1) * P])
            for kv in range(2):
                dst = take_aux(AX["cmp"] + kv)
                w = slab(SL["cmp"] + kv).rearrange("p (c n) -> p c n", c=16)
                pe.wait_ge(blk_ready, kv + 1)
                for f in range(2):
                    for c in range(16):
                        last = nc.tensor.matmul(dst[:, f * 60:(f + 1) * 60], w[:, c, f * P:(f + 1) * P],
                                                n_blk[:, kv, c, :, :].rearrange("p g n -> p (g n)"),
                                                start=(c == 0), stop=(c == 15))
                last.then_inc(slab_done, 1)
            dst = take_aux(AX["cmp"] + 2)
            wait_aux_out(pe, AX["cmp"])
            for f in range(2):
                last = nc.tensor.matmul(dst[:, 0:60], w2k[:, f, :], n_hid[:, 0, f, :], start=(f == 0), stop=(f == 1))
            last.then_inc(aux_ready, 1)
            dst = take_aux(AX["cmp"] + 3)
            wait_aux_out(pe, AX["cmp"] + 1)
            for g in range(NSA_G):
                for f in range(2):
                    last = nc.tensor.matmul(dst[0:CMP_N, g * DH:(g + 1) * DH],
                                            n_hid[:, 1, f, g * CMP_N:(g + 1) * CMP_N], w2v[:, f, :],
                                            start=(f == 0), stop=(f == 1))
            last.then_inc(aux_ready, 1)
            wait_aux_out(pe, AX["cmp"] + 2)
            wait_aux_out(pe, AX["cmp"] + 3)
            wait_transposed("nsa_T", 12)

            def nsa_scores(hd):
                s = take_pair(PJ["nsa_att"] + hd)
                g, half = hd // (NSA_H // NSA_G), slice(hd % 2 * DH, hd % 2 * DH + DH)
                q = [n_qT[half, hd // 2, i * P:(i + 1) * P] for i in range(NT)]
                for y_ in range(2):
                    nc.tensor.matmul(s[:, y_ * T:(y_ + 1) * T], q[1], n_kT[half, y_, g, :], start=True, stop=True)
                    nc.tensor.matmul(s[:, 512 + y_ * P:512 + (y_ + 1) * P], q[0], n_kT[half, y_, g, 0:P],
                                     start=True, stop=True)
                for i in (1, 0):
                    last = nc.tensor.matmul(s[:, 768 + (1 - i) * 16:768 + (1 - i) * 16 + CMP_N], q[i],
                                            n_kcmp[half, g * CMP_N:(g + 1) * CMP_N], start=True, stop=True)
                last.then_inc(score_ready, 1)

            nsa_scores(0)
            nsa_scores(1)
            for hd in range(NSA_H):
                b, g = AX["nsa_att"] + 3 * hd, hd // (NSA_H // NSA_G)
                pe.wait_ge(prob_ready, hd + 1)
                transpose4(b, lambda q: n_P[:, hd % 2, q * P:(q + 1) * P])
                transpose4(b + 1, lambda q: n_P[:, hd % 2, (4 + q) * P:(5 + q) * P])
                if hd + 2 < NSA_H:
                    nsa_scores(hd + 2)
                o = take_aux(b + 2)
                wait_aux_out(pe, b)
                wait_aux_out(pe, b + 1)
                cols = slice(g * DH, (g + 1) * DH)
                for y_ in range(2):
                    for i in range(NT):
                        nc.tensor.matmul(o[:, y_ * DH:(y_ + 1) * DH], n_PT[:, 2 * y_ + i, :], n_v[:, y_, i, cols],
                                         start=(i == 0), stop=(i == 1))
                for y_ in range(2):
                    nc.tensor.matmul(o[:, (2 + y_) * DH:(3 + y_) * DH], n_PT[:, 4 + y_, :], n_v[:, y_, 0, cols],
                                     start=True, stop=True)
                for i in range(NT):
                    last = nc.tensor.matmul(o[:, (4 + i) * DH:(5 + i) * DH], n_PT[0:CMP_N, 6 + i, :],
                                            n_vcmp[0:CMP_N, cols], start=True, stop=True)
                last.then_inc(aux_ready, 1)
            pe.wait_ge(o_ready, NSA_H)
            for i in range(NT):
                for c in range(2):
                    transpose4(AX["nsa_oT"] + 2 * i + c,
                               lambda q: n_o[:, 1 - i, (4 * c + q) * P:(4 * c + q + 1) * P])
            wait_transposed("nsa_oT", 4)
            for s in range(2):
                slab_a(SL["nsa_out"] + s, PJ["nsa_out"] + s, n_oT)
            norm_to_features(2)
            experts(1)
            norm_to_features(3)

            pe.wait_ge(stage_loaded, 48)
            mode_a(take_aux(AX["dt"])[:, 0:128].rearrange("p (i n) -> p i n", i=NT), w_dt, hT, 64).then_inc(aux_ready, 1)
            pe.wait_ge(x_low, 3)
            split_slabs("att_in", 5, a_hT)

            def att_scores(hd):
                s = take_aux(AX["att"] + 3 * hd)
                half = slice(hd % 2 * DH, hd % 2 * DH + DH)
                for i in range(NT):
                    last = nc.tensor.matmul(s[:, i * T:(i + 1) * T], a_qkT[half, hd // 2, i * P:(i + 1) * P],
                                            a_qkT[half, 6 + hd // 2, :], start=True, stop=True)
                last.then_inc(aux_ready, 1)

            def xbc_half(n):
                j = PJ["att"] + n // 2
                dst = (take_pair(j) if n % 2 == 0 else pair(j)).rearrange("p (c t) -> p c t", c=4)
                w3 = slab(SL["att"] + n // 2).rearrange("p (k n) -> p k n", k=KC)
                for c in (2 * (n % 2), 2 * (n % 2) + 1):
                    for k in range(KC):
                        last = nc.tensor.matmul(dst[:, c, :], w3[:, k, c * P:(c + 1) * P], hT[:, k, :],
                                                start=(k == 0), stop=(k == KC - 1))
                if n % 2:
                    last.then_inc(slab_done, 1)

            for s in (3, 4):
                wait_pair_out(pe, PJ["att_in"] + s)
            for hd in range(ATT_H):
                att_scores(hd)
                xbc_half(hd)
                b = AX["att"] + 3 * hd
                pe.wait_ge(att_exp_ready, hd + 1)
                transpose4(b + 1, lambda q: a_P[:, hd % 2, q * P:(q + 1) * P])
                o = take_aux(b + 2)
                wait_aux_out(pe, b + 1)
                for i in range(NT):
                    for k in range(NT):
                        last = nc.tensor.matmul(o[:, i * DH:(i + 1) * DH],
                                                a_PT[:, hd % 2, (2 * i + k) * P:(2 * i + k + 1) * P],
                                                a_v[:, k, hd * DH:(hd + 1) * DH], start=(k == 0), stop=(k == 1))
                last.then_inc(aux_ready, 1)

            for s in range(4):
                slab_b(SL["gates"] + s, PJ["gates"] + s, hT)
            pe.wait_ge(att_y_ready, 1)
            transpose4(AX["att_T"], lambda q: a_y[:, q // 2, q % 2 * P:(q % 2 + 1) * P])
            c = take_aux(AX["cums"])
            pe.wait_ge(a_ready, 1)
            for k, (tri, i, r) in enumerate(((tri_ge, 0, 1), (tri_le, 1, 0), (tri_gt, 0, 0), (tri_lt, 1, 1))):
                last = nc.tensor.matmul(c[:, k * 32:(k + 1) * 32], tri, s_a[:, i, r * 32:(r + 1) * 32],
                                        start=True, stop=True)
            last.then_inc(aux_ready, 1)
            pe.wait_ge(xbc_ready, 12)
            for i in range(NT):
                for g in range(SSD_G):
                    transpose4(AX["xT"] + 4 * i + g, lambda q: xbcT[:, 4 * g + q, i * P:(i + 1) * P])

            for g in range(SSD_G):
                b, j = AX["ssd"] + 11 * g, PJ["ssd"] + 2 * g
                cb = take_aux(b)
                for k in range(NT):
                    last = nc.tensor.matmul(cb[:, k * T:(k + 1) * T], xbcT[:, 16 + g, k * P:(k + 1) * P],
                                            xbcT[:, 20 + g, :], start=True, stop=True)
                last.then_inc(aux_ready, 1)
                diag = take_pair(j).rearrange("p (i n) -> p i n", i=NT)

                def decay_sums(h_):
                    dst = take_aux(b + 1 + h_)
                    hh = 8 * g + h_
                    pe.wait_ge(a4_ready, hh + 1)
                    for k in range(4):
                        last = nc.tensor.matmul(dst[:, k * P:(k + 1) * P], s_A4[:, hh % 2, k, :],
                                                (tri_le, tri_ge)[k // 2], start=True, stop=True)
                    last.then_inc(aux_ready, 1)

                def z_part(h_):
                    dst = (take_pair(j + 1) if h_ == 0 else pair(j + 1)).rearrange("p (i n) -> p i n", i=NT)
                    w3 = slab(SL["ssd"] + g).rearrange("p (k n) -> p k n", k=KC)
                    i = h_ // 4
                    for k in (2 * (h_ % 4), 2 * (h_ % 4) + 1):
                        last = nc.tensor.matmul(dst[:, i, :], hT[:, k, i * P:(i + 1) * P], w3[:, k, :],
                                                start=(k == 0), stop=(k == KC - 1))
                    if h_ == 7:
                        last.then_inc(slab_done, 1)

                decay_sums(0)
                for h_ in range(8):
                    hh = 8 * g + h_
                    if h_ < 7:
                        decay_sums(h_ + 1)
                    z_part(h_)
                    if h_ == 0:
                        pe.wait_ge(xdt_ready, g + 1)
                    pe.wait_ge(m_ready, hh + 1)
                    for i in range(NT):
                        for r in range(2):
                            last = nc.tensor.matmul(diag[:, i, h_ * DH:(h_ + 1) * DH], s_M[:, hh % 2, 2 * r + i, :],
                                                    s_xdt[:, r, i, h_ * DH:(h_ + 1) * DH],
                                                    start=(r == 0), stop=(r == 1))
                    last.then_inc(diag_done, 1)
                pe.wait_ge(cb_ready, g + 1)
                for i in range(NT):
                    last = nc.tensor.matmul(take_aux(b + 9 + i), s_cbx[:, 1 - i, :], s_xd[:, 1 - i, :],
                                            start=True, stop=True)
                    last.then_inc(aux_ready, 1)
                pe.wait_ge(aux_ready, AR["ssd"] + 11 * (g + 1))
                pe.nop().then_inc(group_done, 1)

            pe.wait_ge(pattn_loaded, 16)
            wait_aux_out(pe, AX["att_T"])
            for c2 in range(4):
                dst = take_aux(AX["proj_attn"] + c2)
                for c in range(2):
                    for k in range(2):
                        last = nc.tensor.matmul(dst[:, c * T:(c + 1) * T],
                                                pattn[:, k, (2 * c2 + c) * P:(2 * c2 + c + 1) * P], a_yT[:, k, :],
                                                start=(k == 0), stop=(k == 1))
                last.then_inc(aux_ready, 1)
            for g in range(SSD_G):
                for i in range(NT):
                    pe.wait_ge(ssd_n_ready, 2 * g + i + 1)
                    transpose4(AX["ssd_yT"] + 2 * g + i,
                               lambda q: s_x[:, i, (4 * g + q) * P:(4 * g + q + 1) * P])
            wait_transposed("ssd_yT", 8)
            for s in range(4):
                dst = take_aux(AX["proj_ssd"] + s)
                w = slab(SL["proj_ssd"] + s).rearrange("p (k n) -> p k n", k=16)
                for c in range(2):
                    for k in range(16):
                        last = nc.tensor.matmul(dst[:, c * T:(c + 1) * T], w[:, k, c * P:(c + 1) * P], s_yT[:, k, :],
                                                start=(k == 0), stop=(k == 15))
                last.then_inc(slab_done, 1)
            pe.wait_ge(mix_ready, 4)
            for s in range(2):
                slab_a(SL["out2"] + s, PJ["out2"] + s, mixT)
            norm_to_features(4)
            split_slabs("up", 8, f_hT)
            dst = [take_pair(PJ["down"] + i) for i in range(NT)]
            pe.wait_ge(f_low, 8)
            for s in range(8):
                for half in range(2):
                    q = HQ["down"] + 2 * s + half
                    pe.wait_ge(w_low, q + 1)
                    w3 = [split_half(q, part).rearrange("p (k n) -> p k n", k=2) for part in range(2)]
                    for i in range(NT):
                        for k in range(2):
                            for t, (a, b) in enumerate(SPLIT):
                                for c in range(2):
                                    last = nc.tensor.matmul(dst[i][:, c * 512:(c + 1) * 512],
                                                            f_T[a][:, 4 * s + 2 * half + k, i * P:(i + 1) * P],
                                                            w3[b][:, k, c * 512:(c + 1) * 512],
                                                            start=(s == half == k == t == 0),
                                                            stop=(s == 7 and half == k == 1 and t == 2))
                    last.then_inc((half_done, slab_done)[half], 1)

        @block.scalar
        def _(act):
            link = chain(act, act_chain)

            def copy_transposed(stage, batches, which, dst, groups=2):
                for b in which:
                    i, c = b // groups, b % groups
                    act.wait_ge(aux_ready, AR[stage] + b + 1)
                    nc.scalar.activation(dst[:, 4 * c:4 * c + 4, i * P:(i + 1) * P],
                                         aux(AX[stage] + b).rearrange("p (q t) -> p q t", q=4),
                                         ACT.Copy).then_inc(aux_out[(AX[stage] + b) % 4], 1)

            def high(q):
                n, half = SPLIT_SLABS[q // 2], q % 2
                fresh = q - half in (0, HQ["nsa_in"], HQ["att_in"], HQ["up"])
                if half == 0:
                    act.wait_ge(slab_loaded[n % NSLOT], 16 * (n // NSLOT + 1))
                    if not fresh:
                        act.wait_ge(half_done, q // 2)
                elif not fresh:
                    act.wait_ge(slab_done, n)
                nc.scalar.activation(split_shaped(q, 0), ring_half(q), ACT.Copy).then_inc(w_high, 1)

            act.wait_ge(x_loaded, 16)
            nc.scalar.activation(r_hT[0], hT[:], ACT.Copy).then_inc(x_high, 1)
            high(0)
            high(1)
            for j in range(8):
                if j < 7:
                    high(2 * j + 2)
                act.wait_ge(slab_done, j + 1)
                if j < 7:
                    high(2 * j + 3)
                if j >= 4:
                    nc.scalar.activation(r_v[:, :, (j - 4) * 512:(j - 3) * 512],
                                         pair(j).rearrange("p (i n) -> p i n", i=NT),
                                         ACT.Copy).then_inc(pair_out[j % 2], 1)
            for hd in range(RET_H):
                j = 8 + hd
                act.wait_ge(slab_done, j + 1)
                nc.scalar.activation(r_g[:, :, hd * 512:(hd + 1) * 512],
                                     pair(j).rearrange("p (i n) -> p i n", i=NT),
                                     ACT.Silu).then_inc(pair_out[j % 2], 1)
                for i in range(NT):
                    b = 3 * hd + 1 + i
                    act.wait_ge(aux_ready, b + 1)
                    nc.scalar.activation(r_o[:, i, hd * 512:(hd + 1) * 512], aux(b),
                                         ACT.Copy).then_inc(aux_out[b % 4], 1)
            act.wait_ge(ret_var_ready, 1)
            nc.scalar.activation(r_rstd, r_mv[:, :, :, 1], ACT.Sqrt).then_inc(ret_std_ready, 1)
            for hd in range(RET_H):
                b = 2 * hd + 1
                act.wait_ge(aux_ready, AR["ret_yT"] + b + 1)
                nc.scalar.activation(r_yT[:, 4 * hd:4 * hd + 4, P:T],
                                     aux(AX["ret_yT"] + b).rearrange("p (q t) -> p q t", q=4),
                                     ACT.Copy).then_inc(aux_out[(AX["ret_yT"] + b) % 4], 1)

            def norm(n):
                act.wait_ge(var_ready, n + 1)
                nc.scalar.activation(rstd, mv[:, :, 1], ACT.Sqrt).then_inc(std_ready, 1)
                copy_transposed(f"ln{n}", 4, (1, 3), hT)

            norm(0)

            def expert_pass(ps_):
                for out_sem in (ps_.gate_out, ps_.hidT_out, ps_.gather_out):
                    act.nop().then_inc(out_sem, 1)

                def tokens(g):
                    act.wait_ge(ps_.gathered, g + 1)
                    nc.scalar.activation(m_w[:, bass.ds(g * 4, 4)], bank(3)[:, 0:4], ACT.Copy)
                    nc.scalar.activation(m_ST[:, bass.ds(g * 256, 256)], bank(3)[:, P:3 * P], ACT.Copy)
                    nc.scalar.activation(m_xT.rearrange("p k s -> p (k s)"), bank(6, 2),
                                         ACT.Copy).then_inc(ps_.gather_out, 1)

                def silu(done, e):
                    act.wait_ge(ps_.done, done)
                    act.wait_ge(ps_.up_out, e + 1)
                    nc.scalar.activation(m_sg, bank(0), ACT.Silu).then_inc(ps_.gate_out, 1)

                def group(G, final):
                    for k in range(4):
                        e = G * 4 + k
                        if k == 3 and not final:
                            tokens(G + 1)
                        act.wait_ge(ps_.hidden_T, e + 1)
                        nc.scalar.activation(m_heT.rearrange("p k s -> p (k s)"), bank(2),
                                             ACT.Copy).then_inc(ps_.hidT_out, 1)
                        if k < 3 or not final:
                            silu(G * 12 + (ps_.base + 3 * k + 3), e + 1)

                tokens(0)
                silu(ps_.base + 1, 0)
                with act.Fori(0, 3) as G:
                    group(G, False)
                group(3, True)

            def experts(layer):
                act.wait_ge(aux_ready, AR[f"router{layer}"] + 1)
                logits = aux(AX[f"router{layer}"])
                nc.scalar.activation(aff, logits[:, 0:NT * N_EXP].rearrange("p (i e) -> p i e", i=NT),
                                     ACT.Sigmoid).then_inc(aux_out[AX[f"router{layer}"] % 4], 1)
                expert_pass(passes[layer][0])
                act.wait_ge(flag_ready, layer + 1)
                with act.If(act.value_load(flag[0:1, 0:1], min_val=0, max_val=1)):
                    expert_pass(passes[layer][1])

            def split_tokens(stage, ln, dst):
                act.wait_ge(var_ready, ln + 1)
                nc.scalar.activation(rstd, mv[:, :, 1], ACT.Sqrt).then_inc(std_ready, 1)
                high(HQ[stage])
                high(HQ[stage] + 1)
                copy_transposed(f"ln{ln}", 4, (1, 3), hT)
                for b in (0, 2):
                    wait_aux_out(act, AX[f"ln{ln}"] + b)
                    wait_aux_out(act, AX[f"ln{ln}"] + b + 1)
                nc.scalar.activation(dst[0], hT[:], ACT.Copy).then_inc(x_high, 1)

            experts(0)
            split_tokens("nsa_in", 1, n_hT)
            for q in range(HQ["nsa_in"] + 2, HQ["att_in"]):
                high(q)

            act.wait_ge(aux_ready, AR["nsa_in"] + 1)
            gates = aux(AX["nsa_in"])[:, 0:96].rearrange("p (i h n) -> p i h n", i=NT, h=NSA_H)
            for k, (i, n) in enumerate(((1, 1), (1, 2), (0, 1), (0, 2), (1, 0), (0, 0))):
                last = nc.scalar.activation(n_gw[:, :, k], gates[:, i, :, n], ACT.Sigmoid)
            last.then_inc(aux_out[AX["nsa_in"] % 4], 1)
            for ty in (KSLC, KWIN):
                for i in range(NT):
                    b = 2 * ty + i
                    act.wait_ge(aux_ready, AR["nsa_T"] + b + 1)
                    nc.scalar.activation(n_kT[:, ty - 2, :, i * P:(i + 1) * P],
                                         aux(AX["nsa_T"] + b).rearrange("p (g t) -> p g t", g=NSA_G),
                                         ACT.Copy).then_inc(aux_out[(AX["nsa_T"] + b) % 4], 1)
            for b in range(4):
                i, c = b // 2, b % 2
                act.wait_ge(aux_ready, AR["nsa_T"] + 8 + b + 1)
                nc.scalar.activation(n_qT[:, 4 * c:4 * c + 4, i * P:(i + 1) * P],
                                     aux(AX["nsa_T"] + 8 + b).rearrange("p (q t) -> p q t", q=4),
                                     ACT.Copy).then_inc(aux_out[(AX["nsa_T"] + 8 + b) % 4], 1)
            for kv in range(2):
                act.wait_ge(slab_done, SL["cmp"] + kv + 1)
                nc.scalar.activation(n_hid[:, kv, :, :].rearrange("p f n -> p (f n)"), aux(AX["cmp"] + kv)[:, 0:120],
                                     ACT.Gelu_apprx_tanh).then_inc(aux_out[(AX["cmp"] + kv) % 4], 1)
            act.wait_ge(aux_ready, AR["cmp"] + 1)
            nc.scalar.activation(n_kcmp, aux(AX["cmp"] + 2)[:, 0:60], ACT.Copy).then_inc(aux_out[(AX["cmp"] + 2) % 4], 1)
            act.wait_ge(aux_ready, AR["cmp"] + 2)
            nc.scalar.activation(n_vcmp[0:CMP_N, :], aux(AX["cmp"] + 3)[0:CMP_N, 0:256],
                                 ACT.Copy).then_inc(aux_out[(AX["cmp"] + 3) % 4], 1)
            act.wait_ge(p_zeroed, 1)

            def nsa_exps(hd):
                u = hd % 2
                act.wait_ge(nmax_ready, hd + 1)
                for k, (a, c, n) in enumerate(((0, 0, 256), (256, 256, 256), (512, 512, 128), (640, 640, 128),
                                               (768, 768, CMP_N), (784, 896, CMP_N))):
                    last = nc.scalar.activation(n_P[:, u, c:c + n], n_S[:, u, a:a + n], ACT.Exp,
                                                bias=n_nmax[:, u, k:k + 1], accum_out=n_sum[:, u, k:k + 1])
                last.then_inc(exp_ready, 1)

            nsa_exps(0)
            for hd in range(NSA_H):
                if hd + 1 < NSA_H:
                    nsa_exps(hd + 1)
                for v in range(2):
                    b = 3 * hd + v
                    act.wait_ge(aux_ready, AR["nsa_att"] + b + 1)
                    nc.scalar.activation(n_PT[:, 4 * v:4 * v + 4, :].rearrange("p a t -> p (a t)"),
                                         aux(AX["nsa_att"] + b), ACT.Copy).then_inc(aux_out[(AX["nsa_att"] + b) % 4], 1)
            copy_transposed("nsa_oT", 4, (1, 3), n_oT)
            norm(2)
            experts(1)
            split_tokens("att_in", 3, a_hT)

            for s in range(5):
                j = PJ["att_in"] + s
                if s < 4:
                    high(HQ["att_in"] + 2 * s + 2)
                act.wait_ge(slab_done, SL["att_in"] + s + 1)
                if s < 4:
                    high(HQ["att_in"] + 2 * s + 3)
                if s < 3:
                    nc.scalar.activation(a_qkT[:, 4 * s:4 * s + 4, :], pair(j).rearrange("p (c t) -> p c t", c=4),
                                         ACT.Copy).then_inc(pair_out[j % 2], 1)
                else:
                    n = (512, 256)[s - 3]
                    nc.scalar.activation(a_v[:, :, (s - 3) * 512:(s - 3) * 512 + n],
                                         pair(j).rearrange("p (i n) -> p i n", i=NT)[:, :, 0:n],
                                         ACT.Copy).then_inc(pair_out[j % 2], 1)
            act.wait_ge(stage_loaded, 48)
            act.wait_ge(dt_v_ready, 1)
            nc.scalar.activation(s_A, a_log, ACT.Exp)
            nc.scalar.activation(s_u, s_m, ACT.Exp, scale=-1.0).then_inc(dt_u_ready, 1)
            act.wait_ge(dt_w_ready, 1)
            nc.scalar.activation(s_l, s_m, ACT.Ln).then_inc(dt_l_ready, 1)

            act.wait_ge(raw_zeroed, 1)

            def conv_out(n):
                act.wait_ge(conv_ready, n + 1)
                for c in range(2):
                    last = nc.scalar.activation(xbcT[:, 2 * n + c, :], c_acc[:, n % 2, c, :], ACT.Silu,
                                                bias=conv_b[:, 2 * n + c:2 * n + c + 1])
                last.then_inc(xbc_ready, 1)

            for hd in range(ATT_H):
                u = hd % 2
                act.wait_ge(att_max_ready, hd + 1)
                for i in range(NT):
                    last = nc.scalar.activation(a_P[:, u, i * T:(i + 1) * T], a_S[:, u, i * T:(i + 1) * T], ACT.Exp,
                                                bias=a_nmax[:, hd, i:i + 1], accum_out=a_den[:, hd, i:i + 1])
                last.then_inc(att_exp_ready, 1)
                b = 3 * hd + 1
                act.wait_ge(aux_ready, AR["att"] + b + 1)
                nc.scalar.activation(a_PT[:, u, :], aux(AX["att"] + b), ACT.Copy).then_inc(aux_out[(AX["att"] + b) % 4], 1)
                if hd % 2:
                    s = hd // 2
                    j = PJ["att"] + s
                    act.wait_ge(slab_done, SL["att"] + s + 1)
                    if s >= 2:
                        act.wait_ge(conv_ready, 2 * (s - 2) + 2)
                    nc.scalar.activation(c_raw[:, s % 2, :, 2:2 + T], pair(j).rearrange("p (c t) -> p c t", c=4),
                                         ACT.Copy).then_inc(pair_out[j % 2], 1)
                if hd >= 3:
                    conv_out(hd - 3)
            for n in range(9, 12):
                conv_out(n)
            act.wait_ge(att_o_ready, ATT_H)
            nc.scalar.activation(a_lse, a_den, ACT.Ln).then_inc(att_lse_ready, 1)
            act.wait_ge(att_mix_ready, 1)
            nc.scalar.activation(a_w, a_lse, ACT.Exp).then_inc(att_lse_ready, 1)
            for s in range(4):
                j = PJ["gates"] + s
                act.wait_ge(slab_done, SL["gates"] + s + 1)
                for c in range(4):
                    last = nc.scalar.activation(gateT[:, 4 * s + c, :], pair(j)[:, c * T:(c + 1) * T], ACT.Sigmoid,
                                                bias=b_gate[:, 4 * s + c:4 * s + c + 1])
                last.then_inc(pair_out[j % 2], 1)
            act.wait_ge(aux_ready, AR["cums"] + 1)
            nc.scalar.activation(s_E, aux(AX["cums"])[:, 0:128].rearrange("p (k h) -> p k h", k=4),
                                 ACT.Exp).then_inc(aux_out[AX["cums"] % 4], 1)
            wait_aux_out(act, AX["cums"])
            act.nop().then_inc(decay_ready, 1)
            for b in range(1, 8, 2):
                act.wait_ge(aux_ready, AR["xT"] + b + 1)
                nc.scalar.activation(s_x[:, b // 4, b % 4 * 512:(b % 4 + 1) * 512], aux(AX["xT"] + b),
                                     ACT.Copy).then_inc(aux_out[(AX["xT"] + b) % 4], 1)
            for g in range(SSD_G):
                for h_ in range(8):
                    hh, b = 8 * g + h_, 11 * g + 1 + h_
                    act.wait_ge(aux_ready, AR["ssd"] + b + 1)
                    if hh >= 2:
                        act.wait_ge(m_ready, hh - 1)
                    nc.scalar.activation(s_L[:, hh % 2, :], aux(AX["ssd"] + b), ACT.Exp).then_inc(
                        aux_out[(AX["ssd"] + b) % 4], 1)
                j = PJ["ssd"] + 2 * g + 1
                act.wait_ge(slab_done, SL["ssd"] + g + 1)
                if g:
                    act.wait_ge(ssd_y_ready, g)
                nc.scalar.activation(s_z, pair(j).rearrange("p (i n) -> p i n", i=NT), ACT.Silu).then_inc(
                    pair_out[j % 2], 1)
                act.wait_ge(ssd_y_ready, g + 1)
                for i in range(NT):
                    last = nc.scalar.activation(s_junk, s_x[:, i, g * 512:(g + 1) * 512], ACT.Square,
                                                accum_out=s_ss[:, i, g:g + 1])
                    last.then_inc(square_ready, 1)
                    act.wait_ge(square_ready, 2 * g + i + 1)
            act.wait_ge(ssd_var_ready, 1)
            nc.scalar.activation(s_rstd, s_rstd, ACT.Sqrt).then_inc(ssd_std_ready, 1)
            for g in range(SSD_G):
                b = 2 * g + 1
                act.wait_ge(aux_ready, AR["ssd_yT"] + b + 1)
                nc.scalar.activation(s_yT[:, 4 * g:4 * g + 4, P:T],
                                     aux(AX["ssd_yT"] + b).rearrange("p (q t) -> p q t", q=4),
                                     ACT.Copy).then_inc(aux_out[(AX["ssd_yT"] + b) % 4], 1)
            act.wait_ge(slab_done, SL["up"])
            high(HQ["up"])
            high(HQ["up"] + 1)
            act.wait_ge(var_ready, 5)
            nc.scalar.activation(rstd, mv[:, :, 1], ACT.Sqrt).then_inc(std_ready, 1)
            for b in range(4):
                i, c = b // 2, b % 2
                act.wait_ge(aux_ready, AR["ln4"] + b + 1)
                nc.scalar.activation(f_hT[0][:, 4 * c:4 * c + 4, i * P:(i + 1) * P],
                                     aux(AX["ln4"] + b).rearrange("p (q t) -> p q t", q=4),
                                     ACT.Copy).then_inc(hT_high, 1)
            for s in range(8):
                j = PJ["up"] + s
                high(HQ["up"] + 2 * s + 2)
                if s:
                    act.wait_ge(f_ready, 2 * s)
                    nc.scalar.activation(f_T[0][:, 4 * s - 4:4 * s, :].rearrange("p c t -> p (c t)"),
                                         f_relu[:, (s - 1) % 2, :], ACT.Copy).then_inc(f_high, 1)
                act.wait_ge(slab_done, SL["up"] + s + 1)
                high(HQ["up"] + 2 * s + 3)
                if s >= 2:
                    act.wait_ge(f_low, s - 1)
                nc.scalar.activation(f_relu[:, s % 2, :], pair(j), ACT.Relu).then_inc(f_ready, 1)
            act.wait_ge(f_ready, 16)
            nc.scalar.activation(f_T[0][:, 28:32, :].rearrange("p c t -> p (c t)"), f_relu[:, 1, :],
                                 ACT.Copy).then_inc(f_high, 1)
            for q in range(18, 32):
                high(HQ["up"] + q)
            act.wait_ge(var_ready, 6)
            nc.scalar.activation(rstd, mv[:, :, 1], ACT.Sqrt).then_inc(std_ready, 1)

        @block.vector
        def _(dve):
            link = chain(dve, dve_chain)
            V = nc.vector

            def copy_transposed(stage, batches, which, dst, groups=2):
                for b in which:
                    i, c = b // groups, b % groups
                    dve.wait_ge(aux_ready, AR[stage] + b + 1)
                    V.tensor_copy(dst[:, 4 * c:4 * c + 4, i * P:(i + 1) * P],
                                  aux(AX[stage] + b).rearrange("p (q t) -> p q t", q=4)
                                  ).then_inc(aux_out[(AX[stage] + b) % 4], 1)

            def low(q):
                dve.wait_ge(w_high, q + 1)
                V.tensor_tensor(split_shaped(q, 1), ring_half(q), split_shaped(q, 0).bitcast(F32),
                                ALU.subtract).then_inc(w_low, 1)

            def low_tokens(stage, n, dst):
                if n > 1:
                    low(HQ[stage])
                dve.wait_ge(x_high, n)
                V.tensor_tensor(dst[1], hT[:], dst[0].bitcast(F32), ALU.subtract).then_inc(x_low, 1)
                if n == 1:
                    low(HQ[stage])
                low(HQ[stage] + 1)

            low_tokens("ret_in", 1, r_hT)
            dve.wait_ge(stage_loaded, 16)
            for j in range(4):
                low(2 * j + 2)
                low(2 * j + 3)
                dve.wait_ge(slab_done, j + 1)
                if j:
                    dve.wait_ge(rope_ready, j)
                src = pair(j).rearrange("p (h f t) -> p h f t", h=2, f=2)
                cos = r_cos[j // 2].unsqueeze(1).broadcast_to([P, 2, T])
                sin = r_sin[j // 2].unsqueeze(1).broadcast_to([P, 2, T])
                V.tensor_tensor(r_t[:, 0], src[:, :, 0, :], cos, ALU.mult)
                V.tensor_tensor(r_t[:, 1], src[:, :, 1, :], sin, ALU.mult)
                V.tensor_tensor(r_t[:, 2], src[:, :, 1, :], cos, ALU.mult)
                V.tensor_tensor(r_t[:, 3], src[:, :, 0, :], sin, ALU.mult).then_inc(pair_out[j % 2], 1)
                wait_pair_out(dve, j)
                V.tensor_tensor(r_qkT[:, 2 * j:2 * j + 2, 0, :], r_t[:, 0], r_t[:, 1], ALU.subtract)
                V.tensor_tensor(r_qkT[:, 2 * j:2 * j + 2, 1, :], r_t[:, 2], r_t[:, 3],
                                ALU.add).then_inc(rope_ready, 1)
            for q in range(10, 16):
                low(q)
            for hd in range(RET_H):
                b = 3 * hd
                dve.wait_ge(aux_ready, b + 1)
                V.tensor_tensor(r_P[:, hd % 2, 0:T], aux(b)[:, 0:T], decay[:, hd, :], ALU.mult)
                V.tensor_tensor(r_P[:, hd % 2, T:T + P], aux(b)[:, T:T + P], decay[:, hd, 0:P],
                                ALU.mult).then_inc(aux_out[b % 4], 1)
                wait_aux_out(dve, b)
                V.engine_nop().then_inc(ret_p_ready, 1)
                for i in range(NT):
                    wait_aux_out(dve, b + 1 + i)
                    V.bn_stats(r_st6[:, hd, i, :], r_o[:, i, hd * 512:(hd + 1) * 512]).then_inc(dve_stats, 1)
            dve.wait_ge(dve_stats, 8)
            for hd in range(RET_H):
                for i in range(NT):
                    last = V.bn_aggr(r_mv[:, hd, i, :], r_st6[:, hd, i, :])
            link(last)
            V.tensor_scalar_add(r_mv[:, :, :, 1], r_mv[:, :, :, 1], EPS).then_inc(ret_var_ready, 1)
            dve.wait_ge(ret_std_ready, 1)
            link(V.reciprocal(r_rstd, r_rstd))
            wait_pair_out(dve, 11)
            for hd in range(RET_H):
                for i in range(NT):
                    o = r_o[:, i, hd * 512:(hd + 1) * 512]
                    link(V.tensor_scalar(o, o, r_mv[:, hd, i, 0:1], r_rstd[:, hd, i:i + 1], ALU.subtract, ALU.mult))
                    V.tensor_tensor(o, o, r_g[:, i, hd * 512:(hd + 1) * 512], ALU.mult).then_inc(ret_y_ready, 1)

                b = 2 * hd
                dve.wait_ge(aux_ready, AR["ret_yT"] + b + 1)
                V.tensor_copy(r_yT[:, 4 * hd:4 * hd + 4, 0:P],
                              aux(AX["ret_yT"] + b).rearrange("p (q t) -> p q t", q=4)
                              ).then_inc(aux_out[(AX["ret_yT"] + b) % 4], 1)

            def norm(n, transposed=True):
                for i in range(NT):
                    for c in range(2):
                        last = V.bn_stats(st6[:, i, c, :], y[:, i, c * 512:(c + 1) * 512])
                link(last)
                for i in range(NT):
                    last = V.bn_aggr(mv[:, i, :], st6[:, i, :, :])
                link(last)
                V.tensor_scalar_add(mv[:, :, 1], mv[:, :, 1], EPS).then_inc(var_ready, 1)
                dve.wait_ge(std_ready, n + 1)
                link(V.reciprocal(rstd, rstd))
                dve.wait_ge(gb_loaded, 16 * (n + 1))
                for i in range(NT):
                    link(V.scalar_tensor_tensor(out=y[:, i, :], in0=y[:, i, :], scalar=mv[:, i, 0:1],
                                                in1=gb[:, 0, :], op0=ALU.subtract, op1=ALU.mult))
                    V.scalar_tensor_tensor(out=h[:, i, :], in0=y[:, i, :], scalar=rstd[:, i:i + 1],
                                           in1=gb[:, 1, :], op0=ALU.mult, op1=ALU.add).then_inc(h_ready, 1)
                if transposed:
                    copy_transposed(f"ln{n}", 4, (0, 2), hT)

            def add_residual_by_tile(stage, alpha):
                dve.wait_ge(slab_done, SL[stage] + SLABS_OF[stage])
                for i in range(NT):
                    j = PJ[stage] + i
                    V.scalar_tensor_tensor(out=y[:, i, :], in0=h[:, i, :], scalar=alpha, in1=pair(j),
                                           op0=ALU.mult, op1=ALU.add).then_inc(pair_out[j % 2], 1)
                    wait_pair_out(dve, j)

            dve.wait_ge(h_loaded, 16)
            add_residual_by_tile("ret_out", ALPHA0)
            norm(0)

            def experts(layer):
                n0, j0, b0 = SL[f"moe{layer}"], PJ[f"moe{layer}"], AX[f"moe{layer}"]
                wait_aux_out(dve, AX[f"router{layer}"])
                G = N_EXP // EXP_PER_GROUP
                link(V.tensor_tensor(selsc.rearrange("p (i e) -> p i e", i=NT), aff,
                                     router_b.unsqueeze(1).broadcast_to([P, NT, N_EXP]), ALU.add))
                def ranks(dst, values, n):
                    c1, c2 = (t[:, 0:16 * n].rearrange("p (n i j) -> p n i j", n=n, i=4) for t in (m_c1, m_c2))
                    vj = values.unsqueeze(2).broadcast_to([P, n, 4, 4])
                    vi = values.unsqueeze(3).broadcast_to([P, n, 4, 4])
                    V.tensor_tensor(c1, vj, vi, ALU.is_gt)
                    link(V.tensor_tensor(c2, vj, vi, ALU.is_equal))
                    link(V.tensor_tensor(c2, c2, tie.unsqueeze(1).broadcast_to([P, n, 4, 4]), ALU.mult))
                    link(V.tensor_tensor(c1, c1, c2, ALU.add))
                    link(V.tensor_reduce(dst, c1, AXX, ALU.add))

                ranks(rank4, selsc.rearrange("p (g i) -> p g i", i=4), NT * G)
                link(V.tensor_single_scalar(rank, rank, 1.5, ALU.is_lt))
                link(V.tensor_tensor(best2, selsc, rank, ALU.mult))
                link(V.tensor_reduce(grp, best2.rearrange("p (g i) -> p g i", i=4), AXX, ALU.add))
                ranks(member, grp.rearrange("p (t g) -> p t g", t=NT), NT)
                V.tensor_single_scalar(grank, grank, 0.5, ALU.is_lt).then_inc(member_ready, 1)
                dve.wait_ge(member_ready, layer + 1)
                link(V.tensor_tensor(rank4, rank4, grank.unsqueeze(2).broadcast_to([P, NT * G, 4]), ALU.mult))
                gflat = gw.rearrange("p i e -> p (i e)")
                link(V.tensor_tensor(gflat, aff.rearrange("p i e -> p (i e)"), rank, ALU.mult))
                link(V.tensor_reduce(wsum, gw, AXX, ALU.add))
                link(V.reciprocal(wsum, wsum))
                link(V.tensor_tensor(gw, gw, wsum.unsqueeze(2).broadcast_to([P, NT, N_EXP]), ALU.mult))

                b = AX[f"router{layer}"] + 1
                dve.wait_ge(aux_ready, AR[f"router{layer}"] + 2)
                V.tensor_copy(m_tot, aux(b)[:, 8:12])
                V.tensor_tensor(m_pos, aux(b)[:, 0:8], grank, ALU.mult).then_inc(aux_out[b % 4], 1)
                wait_aux_out(dve, b)
                link(V.tensor_scalar(m_c1[:, 0:8], grank, -1.0, 1000.0, ALU.add, ALU.mult))
                link(V.tensor_tensor(m_pos, m_pos, m_c1[:, 0:8], ALU.add))
                link(V.tensor_reduce(m_tot[:, 0:1], m_tot, AXX, ALU.max))
                link(V.tensor_single_scalar(m_tot[:, 0:1], m_tot[:, 0:1], P + 0.5, ALU.is_gt))
                V.tensor_copy(flag[:], m_tot[:, 0:1]).then_inc(flag_ready, 1)
                dve.wait_ge(flag_ready, layer + 1)
                expert_pass(passes[layer][0])
                with dve.If(dve.value_load(flag[0:1, 0:1], min_val=0, max_val=1)):
                    V.tensor_scalar_add(m_pos, m_pos, -float(P)).then_inc(over_pos[layer], 1)
                    dve.wait_ge(over_pos[layer], 1)
                    expert_pass(passes[layer][1])

            def expert_pass(ps_):
                for out_sem in (ps_.up_out, ps_.down_out):
                    V.engine_nop().then_inc(out_sem, 1)

                def onehot(g):
                    for i in range(NT):
                        last = V.tensor_scalar(m_S[:, i, :], iota, m_pos[:, bass.ds(g + 4 * i, 1)], None, ALU.is_equal)
                    last.then_inc(ps_.onehot_ready, 1)



                def hidden(done, e):
                    dve.wait_ge(ps_.done, done)
                    dve.wait_ge(ps_.gate_out, e + 2)
                    V.tensor_tensor(m_he, m_sg, bank(1), ALU.mult).then_inc(ps_.up_out, 1)

                def add(done, G, k):
                    part = m_y[:, bass.ds(G * 1024, 1024)]
                    dve.wait_ge(ps_.done, done)
                    weight = m_w[:, bass.ds(G * 4 + k, 1)]
                    if k == 0:
                        V.tensor_scalar(part, bank(4, 2), weight, None, ALU.mult).then_inc(ps_.down_out, 1)
                    else:
                        dve.wait_ge(ps_.down_out, G * 4 + (k + 1))
                        V.scalar_tensor_tensor(out=part, in0=bank(4, 2), scalar=weight, in1=part,
                                               op0=ALU.mult, op1=ALU.add).then_inc(ps_.down_out, 1)

                def group(G, final):
                    if not final:
                        dve.wait_ge(ps_.gathered, G + 1)
                        onehot(G + 1)
                    for k in range(4):
                        e = G * 4 + k
                        base = ps_.base + 3 * k
                        if k == 3 and final:
                            add(ps_.base + 48, G, k)
                            break
                        add(G * 12 + (base + 4), G, k)

                        dve.wait_ge(ps_.hidden_T, e + 1)
                        hidden(G * 12 + (base + 5), e + 1)

                onehot(0)

                hidden(ps_.base + 2, 0)
                with dve.Fori(0, 3) as G:
                    group(G, False)
                group(3, True)
                if ps_.p:
                    dve.wait_ge(over_scattered[ps_.layer], 1)
                else:
                    dve.wait_ge(scattered, ps_.layer + 1)
                for i in range(NT):
                    if ps_.p:
                        last = V.tensor_tensor(y[:, i, :], y[:, i, :], bank(2 * i, 2), ALU.add)
                    else:
                        last = V.scalar_tensor_tensor(out=y[:, i, :], in0=h[:, i, :], scalar=ALPHA0,
                                                      in1=bank(2 * i, 2), op0=ALU.mult, op1=ALU.add)
                out_sem = over_out[ps_.layer] if ps_.p else moe_out
                last.then_inc(out_sem, 1)
                dve.wait_ge(out_sem, 1 if ps_.p else ps_.layer + 1)

            experts(0)
            norm(1)

            low_tokens("nsa_in", 2, n_hT)
            dve.wait_ge(stage_loaded, 32)

            def rotate(src, heads, cos, sin, outs, signal):
                w4 = lambda t: t.unsqueeze(2).broadcast_to([P, NT, heads, 32])
                t = [n_t[:, a, 0:NT * heads * 32].rearrange("p (i h d) -> p i h d", i=NT, h=heads) for a in range(4)]
                V.tensor_tensor(t[0], src[:, :, :, 0, :], w4(cos), ALU.mult)
                V.tensor_tensor(t[1], src[:, :, :, 1, :], w4(sin), ALU.mult)
                V.tensor_tensor(t[2], src[:, :, :, 1, :], w4(cos), ALU.mult)
                last = V.tensor_tensor(t[3], src[:, :, :, 0, :], w4(sin), ALU.mult)
                signal(last)
                for o in outs:
                    V.tensor_tensor(o[:, :, :, 0, :], t[0], t[1], ALU.subtract)
                    last = V.tensor_tensor(o[:, :, :, 1, :], t[2], t[3], ALU.add)
                return last

            for s in range(5):
                j = PJ["nsa_in"] + s
                if s < 4:
                    low(HQ["nsa_in"] + 2 * s + 2)
                    low(HQ["nsa_in"] + 2 * s + 3)
                dve.wait_ge(slab_done, SL["nsa_in"] + s + 1)
                if s:
                    dve.wait_ge(nsa_rot, s)
                src = pair(j).rearrange("p (i n) -> p i n", i=NT)
                if s < 3:
                    k = src[:, :, 0:256].rearrange("p i (g f d) -> p i g f d", g=NSA_G, f=2)
                    v = src[:, :, 256:512]
                    kd = n_dup[:, (KCMP, KSLC, KWIN)[s]].rearrange("p i g u (f d) -> p i g u f d", f=2)
                    if s == 0:
                        v = v.rearrange("p i (g d) -> p i g d", g=NSA_G)
                        for u in range(2):
                            V.tensor_copy(n_dup[:, VCMP, :, :, u, :], v)
                    else:
                        V.tensor_copy(n_v[:, s - 1, :, :], v)
                    last = rotate(k, NSA_G, n_cos, n_sin, [kd[:, :, :, u] for u in range(2)],
                                  lambda x: (x.then_inc(pair_out[j % 2], 1), wait_pair_out(dve, j)))
                else:
                    q = src.rearrange("p i (h f d) -> p i h f d", h=8, f=2)
                    o = n_q[:, :, (s - 3) * 512:(s - 2) * 512].rearrange("p i (h f d) -> p i h f d", h=8, f=2)
                    last = rotate(q, 8, n_cosq, n_sinq, [o],
                                  lambda x: (x.then_inc(pair_out[j % 2], 1), wait_pair_out(dve, j)))
                last.then_inc(nsa_rot, 1)
            for kv in range(2):
                for i in range(NT):
                    b = 2 * kv + i
                    dve.wait_ge(aux_ready, AR["nsa_T"] + b + 1)
                    src = aux(AX["nsa_T"] + b).rearrange("p (g t) -> p g t", g=NSA_G)
                    first = 1 - i
                    V.tensor_copy(n_cT[0:64, kv, :, i * P:(i + 1) * P], src[0:64])
                    V.tensor_copy(n_cT[64:P, kv, :, i * P + first - 1:(i + 1) * P - 1],
                                  src[64:P, :, first:P]).then_inc(aux_out[(AX["nsa_T"] + b) % 4], 1)
            for kv in range(2):
                for i in range(NT):
                    wait_aux_out(dve, AX["nsa_T"] + 2 * kv + i)
                for g in range(NSA_G):
                    row = n_cT[:, kv, g, :]
                    win = bass.AP(tensor=row.tensor, offset=row.offset, ap=[row.ap[0], [2, 16], [CMP_STRIDE, CMP_N]])
                    last = V.tensor_tensor(n_blk[:, kv, :, g, :], win,
                                           cmp_pe[kv].unsqueeze(2).broadcast_to([P, 16, CMP_N]), ALU.add)
                last.then_inc(blk_ready, 1)

            def nsa_masked(hd):
                u, j = hd % 2, PJ["nsa_att"] + hd
                dve.wait_ge(score_ready, hd + 1)
                V.tensor_tensor(n_S[:, u, 0:768], pair(j)[:, 0:768], causal, ALU.add)
                sc = n_S[:, u, 768:800].rearrange("p (i n) -> p i n", i=NT)[:, :, 0:CMP_N]
                V.tensor_tensor(sc, pair(j)[:, 768:800].rearrange("p (i n) -> p i n", i=NT)[:, :, 0:CMP_N],
                                cmp_add, ALU.add).then_inc(pair_out[j % 2], 1)
                wait_pair_out(dve, j)
                V.tensor_reduce(n_max[:, u, 0:2], n_S[:, u, 0:512].rearrange("p (k n) -> p k n", k=2), AXX, ALU.max)
                V.tensor_reduce(n_max[:, u, 2:4], n_S[:, u, 512:768].rearrange("p (k n) -> p k n", k=2), AXX, ALU.max)
                link(V.tensor_reduce(n_max[:, u, 4:6], sc, AXX, ALU.max))
                V.tensor_single_scalar(n_nmax[:, u, :], n_max[:, u, :], -1.0, ALU.mult).then_inc(nmax_ready, 1)

            def nsa_weights(hd):
                u = hd % 2
                dve.wait_ge(exp_ready, hd + 1)
                pc = n_P[:, u, 768:1024].rearrange("p (i n) -> p i n", i=NT)[:, :, 0:CMP_N]
                V.tensor_tensor(pc, pc, cmp_one, ALU.mult).then_inc(prob_ready, 1)
                link(V.reciprocal(n_w[:, u, :], n_sum[:, u, :]))
                link(V.tensor_tensor(n_w[:, u, :], n_w[:, u, :], n_gw[:, hd, :], ALU.mult))

            nsa_masked(0)
            nsa_masked(1)
            nsa_weights(0)
            for hd in range(NSA_H):
                u, b = hd % 2, AX["nsa_att"] + 3 * hd
                if hd + 2 < NSA_H:
                    nsa_masked(hd + 2)
                if hd + 1 < NSA_H:
                    nsa_weights(hd + 1)
                dve.wait_ge(aux_ready, AR["nsa_att"] + 3 * hd + 3)
                if hd:
                    dve.wait_ge(o_ready, hd)
                V.tensor_tensor(n_ow, aux(b + 2)[:, 0:384].rearrange("p (k d) -> p k d", k=6),
                                n_w[:, u, :].unsqueeze(2).broadcast_to([P, 6, DH]),
                                ALU.mult).then_inc(aux_out[(b + 2) % 4], 1)
                wait_aux_out(dve, b + 2)
                four = n_ow[:, 0:4, :].rearrange("p (i y) d -> p i y d", i=NT)
                link(V.tensor_tensor(n_o2, four[:, :, 0, :], four[:, :, 1, :], ALU.add))
                V.tensor_tensor(n_o[:, :, hd * DH:(hd + 1) * DH], n_o2, n_ow[:, 4:6, :],
                                ALU.add).then_inc(o_ready, 1)
            copy_transposed("nsa_oT", 4, (0, 2), n_oT)

            def add_residual_by_half(stage, alpha):
                for s in range(2):
                    j = PJ[stage] + s
                    dve.wait_ge(slab_done, SL[stage] + s + 1)
                    V.scalar_tensor_tensor(out=y[:, :, s * 512:(s + 1) * 512], in0=h[:, :, s * 512:(s + 1) * 512],
                                           scalar=alpha, in1=pair(j).rearrange("p (i n) -> p i n", i=NT),
                                           op0=ALU.mult, op1=ALU.add).then_inc(pair_out[j % 2], 1)
                    wait_pair_out(dve, j)

            add_residual_by_half("nsa_out", ALPHA0)
            norm(2)
            experts(1)
            norm(3)

            low_tokens("att_in", 3, a_hT)
            for q in range(HQ["att_in"] + 2, HQ["up"]):
                low(q)
            dve.wait_ge(stage_loaded, 48)
            dve.wait_ge(aux_ready, AR["dt"] + 1)
            V.tensor_tensor(s_v, aux(AX["dt"])[:, 0:128].rearrange("p (i n) -> p i n", i=NT),
                            dt_bias.unsqueeze(1).broadcast_to([P, NT, 64]), ALU.add).then_inc(aux_out[AX["dt"] % 4], 1)
            wait_aux_out(dve, AX["dt"])
            V.scalar_tensor_tensor(out=s_m, in0=s_v, scalar=-1.0, in1=s_v, op0=ALU.mult,
                                   op1=ALU.max).then_inc(dt_v_ready, 1)
            dve.wait_ge(dt_u_ready, 1)
            V.tensor_scalar_add(s_m, s_u, 1.0).then_inc(dt_w_ready, 1)
            dve.wait_ge(dt_l_ready, 1)
            link(V.tensor_scalar_add(s_a, s_m, -1.0))
            link(V.tensor_single_scalar(s_dt, s_a, 0.0, ALU.is_equal))
            link(V.tensor_tensor(s_l, s_l, s_dt, ALU.add))
            link(V.tensor_tensor(s_a, s_a, s_dt, ALU.add))
            link(V.reciprocal(s_a, s_a))
            link(V.tensor_tensor(s_l, s_l, s_a, ALU.mult))
            link(V.tensor_tensor(s_l, s_l, s_u, ALU.mult))
            link(V.scalar_tensor_tensor(out=s_dt, in0=s_v, scalar=0.0, in1=s_l, op0=ALU.max, op1=ALU.add))
            V.scalar_tensor_tensor(out=s_a, in0=s_dt, scalar=-1.0, in1=s_A.unsqueeze(1).broadcast_to([P, NT, 64]),
                                   op0=ALU.mult, op1=ALU.mult).then_inc(a_ready, 1)

            def conv(n):
                if n % 2 == 0:
                    wait_pair_out(dve, PJ["att"] + n // 2)
                if n >= 2:
                    dve.wait_ge(xbc_ready, n - 1)
                for k in range(TAPS):
                    for c in range(2):
                        ch = 2 * n + c
                        tap = conv_w[:, ch * TAPS + k:ch * TAPS + k + 1]
                        src = c_raw[:, n // 2 % 2, 2 * (n % 2) + c, k:k + T]
                        if k == 0:
                            last = V.tensor_scalar(c_acc[:, n % 2, c, :], src, tap, None, ALU.mult)
                        else:
                            last = V.scalar_tensor_tensor(out=c_acc[:, n % 2, c, :], in0=src, scalar=tap,
                                                          in1=c_acc[:, n % 2, c, :], op0=ALU.mult, op1=ALU.add)
                    if k < TAPS - 1:
                        link(last)
                last.then_inc(conv_ready, 1)

            dve.wait_ge(att_loaded, 16)
            for hd in range(ATT_H):
                u, b = hd % 2, AX["att"] + 3 * hd
                dve.wait_ge(aux_ready, AR["att"] + 3 * hd + 1)
                V.scalar_tensor_tensor(out=a_S[:, u, :], in0=aux(b), scalar=DH ** -0.5, in1=a_bias[:, hd, :],
                                       op0=ALU.mult, op1=ALU.add).then_inc(aux_out[b % 4], 1)
                wait_aux_out(dve, b)
                link(V.tensor_reduce(a_max[:, hd, :], a_S[:, u, :].rearrange("p (i n) -> p i n", i=NT), AXX, ALU.max))
                V.tensor_single_scalar(a_nmax[:, hd, :], a_max[:, hd, :], -1.0, ALU.mult).then_inc(att_max_ready, 1)
                if hd >= 2:
                    conv(hd - 2)
                dve.wait_ge(aux_ready, AR["att"] + 3 * hd + 3)
                V.tensor_copy(a_o[:, hd, :, :], aux(b + 2)[:, 0:NT * DH].rearrange("p (i d) -> p i d", i=NT)
                              ).then_inc(aux_out[(b + 2) % 4], 1)
            conv(10)
            conv(11)
            wait_aux_out(dve, AX["att"] + 3 * ATT_H - 1)
            V.engine_nop().then_inc(att_o_ready, ATT_H)
            flat = lambda t: t.rearrange("p h i -> p (h i)")
            pats = lambda t: flat(t).rearrange("p (a n) -> p a n", a=ATT_PAT)
            by_head = lambda t: flat(t).rearrange("p (a n) -> p n a", a=ATT_PAT)
            dve.wait_ge(att_lse_ready, 1)
            link(V.tensor_tensor(a_lse, a_lse, a_max, ALU.add))
            link(V.tensor_reduce(a_top, by_head(a_lse), AXX, ALU.max))
            V.tensor_tensor(pats(a_lse), pats(a_lse), a_top.unsqueeze(1).broadcast_to([P, ATT_PAT, 8]),
                            ALU.subtract).then_inc(att_mix_ready, 1)
            dve.wait_ge(att_lse_ready, 2)
            link(V.tensor_reduce(a_sum, by_head(a_w), AXX, ALU.add))
            link(V.reciprocal(a_sum, a_sum))
            link(V.reciprocal(a_den, a_den))
            link(V.tensor_tensor(a_w, a_w, a_den, ALU.mult))
            link(V.tensor_tensor(pats(a_w), pats(a_w), a_sum.unsqueeze(1).broadcast_to([P, ATT_PAT, 8]), ALU.mult))
            of = a_o.rearrange("p h i d -> p (h i) d")
            link(V.tensor_tensor(of, of, flat(a_w).unsqueeze(2).broadcast_to([P, 24, DH]), ALU.mult))
            link(V.tensor_tensor(of[:, 0:8], of[:, 0:8], of[:, 8:16], ALU.add))
            V.tensor_tensor(a_y.rearrange("p i (h d) -> p h i d", h=4), a_o[:, 0:4], a_o[:, 8:12],
                            ALU.add).then_inc(att_y_ready, 1)
            dve.wait_ge(aux_ready, AR["att_T"] + 1)
            V.tensor_copy(a_yT.rearrange("p c (i t) -> p i c t", i=NT),
                          aux(AX["att_T"]).rearrange("p (i c t) -> p i c t", i=NT, c=2)).then_inc(aux_out[AX["att_T"] % 4], 1)
            for b in range(0, 8, 2):
                dve.wait_ge(aux_ready, AR["xT"] + b + 1)
                V.tensor_copy(s_x[:, b // 4, b % 4 * 512:(b % 4 + 1) * 512],
                              aux(AX["xT"] + b)).then_inc(aux_out[(AX["xT"] + b) % 4], 1)

            for g in range(SSD_G):
                b, j = AX["ssd"] + 11 * g, PJ["ssd"] + 2 * g
                dve.wait_ge(aux_ready, AR["ssd"] + 11 * g + 1)
                if g:
                    dve.wait_ge(group_done, g)
                cb = aux(b)
                blocks = cb.rearrange("p (k t) -> p k t", k=4)
                same = bass.AP(tensor=cb.tensor, offset=cb.offset, ap=[cb.ap[0], [3 * P, 2], [1, P]])
                V.tensor_tensor(s_cb[:, 0:2], same, tri_le.unsqueeze(1).broadcast_to([P, 2, P]), ALU.mult)
                V.tensor_tensor(s_cb[:, 2:4], same, tri_ge.unsqueeze(1).broadcast_to([P, 2, P]), ALU.mult)
                V.tensor_copy(s_cbx, blocks[:, 1:3, :]).then_inc(aux_out[b % 4], 1)
                wait_aux_out(dve, b)
                V.engine_nop().then_inc(cb_ready, 1)
                for h_ in range(8):
                    hh = 8 * g + h_
                    wait_aux_out(dve, b + 1 + h_)
                    if hh >= 2:
                        dve.wait_ge(diag_done, hh - 1)
                    V.tensor_tensor(s_M[:, hh % 2].rearrange("p k t -> p (k t)"), s_L[:, hh % 2, :],
                                    s_cb.rearrange("p k t -> p (k t)"), ALU.mult).then_inc(m_ready, 1)
                heads = lambda t: t.rearrange("p (h d) -> p h d", h=8)
                dve.wait_ge(aux_ready, AR["ssd"] + 11 * (g + 1))
                for i in range(NT):
                    V.tensor_tensor(heads(s_t[:, i, :]), heads(aux(b + 9 + i)),
                                    s_E[:, i, 8 * g:8 * g + 8].unsqueeze(2).broadcast_to([P, 8, DH]),
                                    ALU.mult).then_inc(aux_out[(b + 9 + i) % 4], 1)
                wait_aux_out(dve, b + 9)
                wait_aux_out(dve, b + 10)
                dve.wait_ge(diag_done, 8 * (g + 1))
                V.tensor_tensor(s_t, s_t, pair(j).rearrange("p (i n) -> p i n", i=NT),
                                ALU.add).then_inc(pair_out[j % 2], 1)
                xg = s_x[:, :, g * 512:(g + 1) * 512]
                x4 = xg.rearrange("p i (h d) -> p i h d", h=8)
                dve.wait_ge(xdt_ready, g + 1)
                link(V.tensor_tensor(x4, x4, d_skip[:, 8 * g:8 * g + 8].unsqueeze(1).unsqueeze(3)
                                     .broadcast_to([P, NT, 8, DH]), ALU.mult))
                wait_pair_out(dve, j)
                link(V.tensor_tensor(xg, xg, s_t, ALU.add))
                wait_pair_out(dve, j + 1)
                V.tensor_tensor(xg, xg, s_z, ALU.mult).then_inc(ssd_y_ready, 1)
            dve.wait_ge(square_ready, 8)
            V.tensor_scalar(s_rstd, s_ss, 1.0 / 512, EPS, ALU.mult, ALU.add).then_inc(ssd_var_ready, 1)
            for c2 in range(4):
                b = AX["proj_attn"] + c2
                dve.wait_ge(aux_ready, AR["proj_attn"] + c2 + 1)
                V.tensor_tensor(mixT[:, 2 * c2:2 * c2 + 2, :], gateT[:, 8 + 2 * c2:10 + 2 * c2, :],
                                aux(b).rearrange("p (c t) -> p c t", c=2), ALU.mult).then_inc(aux_out[b % 4], 1)
            dve.wait_ge(ssd_std_ready, 1)
            link(V.reciprocal(s_rstd, s_rstd))
            for g in range(SSD_G):
                for i in range(NT):
                    x_ = s_x[:, i, g * 512:(g + 1) * 512]
                    V.scalar_tensor_tensor(out=x_, in0=x_, scalar=s_rstd[:, i, g:g + 1],
                                           in1=norm_w[:, g * 512:(g + 1) * 512],
                                           op0=ALU.mult, op1=ALU.mult).then_inc(ssd_n_ready, 1)
                b = 2 * g
                dve.wait_ge(aux_ready, AR["ssd_yT"] + b + 1)
                V.tensor_copy(s_yT[:, 4 * g:4 * g + 4, 0:P],
                              aux(AX["ssd_yT"] + b).rearrange("p (q t) -> p q t", q=4)
                              ).then_inc(aux_out[(AX["ssd_yT"] + b) % 4], 1)
            for s in range(4):
                b = AX["proj_ssd"] + s
                dve.wait_ge(slab_done, SL["proj_ssd"] + s + 1)
                if s:
                    dve.wait_ge(mix_ready, s)
                V.tensor_tensor(mix_t, gateT[:, 2 * s:2 * s + 2, :].rearrange("p c t -> p (c t)"), aux(b),
                                ALU.mult).then_inc(aux_out[b % 4], 1)
                wait_aux_out(dve, b)
                m = mixT[:, 2 * s:2 * s + 2, :].rearrange("p c t -> p (c t)")
                V.tensor_tensor(m, m, mix_t, ALU.add).then_inc(mix_ready, 1)
            add_residual_by_half("out2", ALPHA1)
            norm(4, transposed=False)

            low(HQ["up"])
            for b in range(4):
                i, c = b // 2, b % 2
                dve.wait_ge(hT_high, b + 1)
                rounded, rest = (t[:, 4 * c:4 * c + 4, i * P:(i + 1) * P] for t in f_hT)
                V.tensor_tensor(rest, aux(AX["ln4"] + b).rearrange("p (q t) -> p q t", q=4),
                                rounded.bitcast(F32), ALU.subtract).then_inc(aux_out[(AX["ln4"] + b) % 4], 1)
            low(HQ["up"] + 1)
            def low_hidden(s):
                dve.wait_ge(f_high, s + 1)
                rounded, rest = (t[:, 4 * s:4 * s + 4, :].rearrange("p c t -> p (c t)") for t in f_T)
                V.tensor_tensor(rest, f_relu[:, s % 2, :], rounded.bitcast(F32), ALU.subtract).then_inc(f_low, 1)

            for s in range(8):
                j = PJ["up"] + s
                low(HQ["up"] + 2 * s + 2)
                if s:
                    low_hidden(s - 1)
                low(HQ["up"] + 2 * s + 3)
                dve.wait_ge(f_ready, 2 * s + 1)
                V.tensor_tensor(f_relu[:, s % 2, :], f_relu[:, s % 2, :], pair(j),
                                ALU.mult).then_inc(pair_out[j % 2], 1)
                wait_pair_out(dve, j)
                V.engine_nop().then_inc(f_ready, 1)
            low_hidden(7)
            for q in range(18, 32):
                low(HQ["up"] + q)
            add_residual_by_tile("down", ALPHA1)
            norm(5, transposed=False)


def _slab_8x512(w):
    n = w.shape[1] // 512
    return w.reshape(KC, P, n, 512).transpose(2, 1, 0, 3).reshape(n, P, SLAB)


def _slab_4x1024(w):
    n = w.shape[0] // 512
    return w.reshape(n, 4, P, D).transpose(0, 2, 1, 3).reshape(n, P, SLAB)


def _slab_16x256(w):
    n = w.shape[1] // 256
    return w.reshape(16, P, n, 256).transpose(2, 1, 0, 3).reshape(n, P, SLAB)


def _padded(w, cols):
    return np.concatenate([w, np.zeros((w.shape[0], cols - w.shape[1]), w.dtype)], 1)


def _rows(v):
    return np.broadcast_to(v.reshape(1, -1), (P, v.size))


def _moe_slabs(gate, up, down):
    g, u = (w.reshape(N_EXP, KC, P, 512).transpose(0, 2, 1, 3).reshape(N_EXP, P, SLAB) for w in (gate, up))
    d = down.reshape(N_EXP, 4, P, D).transpose(0, 2, 1, 3).reshape(N_EXP, P, SLAB)
    out = [g[0:1]]
    for e in range(N_EXP):
        out.append(u[e:e + 1])
        if e + 1 < N_EXP:
            out.append(g[e + 1:e + 2])
        out.append(d[e:e + 1])
    return out


def _chunks(w):
    return w.reshape(-1, P, w.shape[1]).transpose(1, 0, 2).reshape(P, -1)


def _rope(dim, theta=10000.0):
    f = np.float32
    inv = (f(theta) ** (-np.arange(0, dim, 2, dtype=f) / f(dim))).astype(f)
    ang = np.arange(T, dtype=f)[:, None] * inv[None, :]
    return np.cos(ang).astype(f), np.sin(ang).astype(f)


def _shape_constants():
    f = np.float32
    c = {}
    cos, sin = _rope(256)
    c["cosq"], c["sinq"] = cos.T, sin.T
    c["cosk"], c["sink"] = cos.T / f(16), sin.T / f(16)
    log_gamma = np.log1p(-(f(2.0) ** (f(-5.0) - np.arange(RET_H, dtype=f)))).astype(f)
    diff = (np.arange(T)[None, :] - np.arange(P)[:, None]).astype(f)
    decay = np.where(diff >= 0, np.exp(log_gamma[:, None, None] * np.maximum(diff, 0)), 0).astype(f)
    c["decay"] = decay.transpose(1, 0, 2).reshape(P, -1)
    c["ident"] = np.eye(P, dtype=f)
    c["before"] = (np.arange(P)[:, None] < np.arange(P)[None, :]).astype(f)
    c["ones"] = np.ones((P, P), f)
    c["iota"] = _rows(np.arange(P, dtype=f))
    c["tie"] = _rows((np.arange(4)[None, :] < np.arange(4)[:, None]).astype(f))
    cos, sin = _rope(DH)
    tokens = lambda t: t.reshape(NT, P, -1).transpose(1, 0, 2).reshape(P, -1)
    n = {"cosk": tokens(cos), "sink": tokens(sin), "cosq": tokens(cos / f(8)), "sinq": tokens(sin / f(8))}
    t, s = np.arange(P)[:, None], np.arange(T)[None, :]
    late = np.where(s <= t + P, 0, NEG).astype(f)
    early = np.where(s[:, :P] <= t, 0, NEG).astype(f)
    n["causal"] = np.concatenate([late, late, early, early], 1)
    end = np.arange(16)[None, :] * CMP_STRIDE + CMP_LEN - 1
    seen = np.concatenate([end <= t + P, end <= t], 1)
    n["cmp_add"], n["cmp_one"] = np.where(seen, 0, NEG).astype(f), seen.astype(f)
    c["nsa"] = n
    tri = {"le": t <= np.arange(P), "gt": t > np.arange(P), "ge": t >= np.arange(P), "lt": t < np.arange(P)}
    c["ssd"] = {k: v.astype(f) for k, v in tri.items()}
    slopes = (2.0 ** (-8.0 * np.arange(1, ATT_H + 1) / ATT_H)).astype(f)
    q = np.arange(T).reshape(NT, P).T
    rel = np.abs(q[:, :, None] - np.arange(T))
    bias = []
    for hd in range(ATT_H):
        window, dilation = ((128, 1), (512, 4), (2048, 16))[hd // ATT_HPP]
        seen = (rel % dilation == 0) & (rel // dilation <= window // (2 * dilation))
        bias.append(np.where(seen, -slopes[hd] * rel.astype(f), NEG).astype(f).reshape(P, -1))
    c["att"] = np.concatenate(bias, 1)
    return c


def _pack(cols, parts):
    return np.ascontiguousarray(np.concatenate([np.asarray(parts[n], np.float32) for n in cols], 1))


def _arrays(a):
    a = {n: np.asarray(v) for n, v in a.items()}
    c = _shape_constants()
    x = a["x"].reshape(T, D)
    ri = a["ret_w_in"][0]
    slabs = [_slab_8x512(ri), _slab_4x1024(a["ret_w_out"][0])]
    slabs += _moe_slabs(a["moe_w_gate"][0], a["moe_w_up"][0], a["moe_w_down"][0])
    slabs += [_slab_8x512(a["nsa_w_kv"]), _slab_8x512(a["nsa_w_in"][0][:, :D])]
    slabs += [a["cmp_k_w1"].reshape(1, 16, P, 256).transpose(0, 2, 1, 3).reshape(1, P, SLAB),
              a["cmp_v_w1"].reshape(1, 16, P, 256).transpose(0, 2, 1, 3).reshape(1, P, SLAB)]
    slabs += [_slab_8x512(a["nsa_w_out"][0])]
    slabs += _moe_slabs(a["moe_w_gate"][1], a["moe_w_up"][1], a["moe_w_down"][1])
    n = c["nsa"]
    n["pe_k"], n["pe_v"] = (a[k].reshape(16, P).T for k in ("cmp_pe_k", "cmp_pe_v"))
    n["w_gates"] = _chunks(a["nsa_w_in"][0][:, D:])
    w2 = a["cmp_k_w2"]
    n["w2k"], n["w2v"] = _chunks(np.concatenate([w2, w2], 1)), _chunks(a["cmp_v_w2"])
    w = a["w_in_2"]
    at = np.cumsum([0, D_INNER, CONV_CH * P, 2 * SSD_H, 2 * ATT_H * DH, ATT_H * DH, 2 * D])
    wz, wxbc, wdt, wqk, wv, wg = (w[:, i:j] for i, j in zip(at[:-1], at[1:]))
    v2 = np.zeros((1, P, SLAB), w.dtype)
    v2[0, :, :KC * 256] = _chunks(wv[:, 512:])
    slabs += [_slab_8x512(wqk), _slab_8x512(wv[:, :512]), v2, _slab_8x512(wxbc), _slab_8x512(wg), _slab_8x512(wz)]
    slabs += [_slab_16x256(a["w_proj_ssd_2"]), _slab_8x512(a["w_out_2"])]
    slabs += [_slab_8x512(a["w_up_2"]), _slab_4x1024(a["w_down_2"])]
    s = c["ssd"]
    s["w_dt"] = _chunks(wdt)
    s["dt_bias"] = _rows(np.concatenate([a["dt_bias_f_2"], a["dt_bias_b_2"]]))
    s["a_log"] = _rows(np.concatenate([a["a_log_f_2"], a["a_log_b_2"]]))
    s["d_skip"] = _rows(a["d_skip_2"])
    s["conv_w"] = a["conv_w_2"].reshape(TAPS, CONV_CH, P).transpose(2, 1, 0).reshape(P, -1)
    s["conv_b"] = a["conv_b_2"].reshape(CONV_CH, P).T
    s["b_gate"] = a["b_gate_2"].reshape(16, P).T
    s["norm_w"] = _rows(a["ssd_norm_w_2"])
    c["router_w"] = _chunks(a["router_w"])
    c["router_b"] = _rows(a["router_b"])
    ln = [np.stack([a["ln_mix_g"][0], a["ln_mix_b"][0]]), np.stack([a["ln_ffn_g"][0], a["ln_ffn_b"][0]]),
          np.stack([a["ln_mix_g"][1], a["ln_mix_b"][1]]), np.stack([a["ln_ffn_g"][1], a["ln_ffn_b"][1]]),
          np.stack([a["ln1_g_2"], a["ln1_b_2"]]), np.stack([a["ln2_g_2"], a["ln2_b_2"]])]
    out = {
        "x_tok": x.reshape(NT, P, D).transpose(1, 0, 2),
        "x_feat": x.T.reshape(KC, P, T).transpose(1, 0, 2),
        "slabs": np.concatenate(slabs, 0),
        "c_all": _pack(C_ALL, c), "c_ret": _pack(C_RET, c), "c_nsa": _pack(C_NSA, n), "c_ssd": _pack(C_SSD, s),
        "c_att": c["att"], "w_pattn": _chunks(a["w_proj_attn_2"]),
        "ln_gb": np.stack(ln).reshape(6, 2 * D),
    }
    return {n: np.ascontiguousarray(v) for n, v in out.items()}


def kernel(**inputs):
    import concourse.bacc as bacc
    from concourse.bass_utils import run_bass_kernel_spmd

    nc = bacc.Bacc("TRN2", target_bir_lowering=False, num_devices=1)
    arrays = _arrays(inputs)
    args = {n: nc.dram_tensor(n, v.shape, F32, kind="ExternalInput").ap() for n, v in arrays.items()}
    out = nc.dram_tensor("out", (NT, P, D), F32, kind="ExternalOutput").ap()
    build(nc, out=out, **args)
    r = run_bass_kernel_spmd(nc, [arrays], core_ids=[0])
    return r.results[0]["out"].reshape(1, T, D)
```
